# Optimizing a Trainium2 kernel written in Bass

```python
import math
import jax, jax.numpy as jnp
from jax import lax
import numpy as np
import jax
import jax.numpy as jnp

D_MODEL = 1024
BATCH = 1
SEQ = 256
DEPTH = 2

GRID_W = 64
CTX_LEN = 256
RMS_EPS = 1e-6
ROPE_BASE = 10000.0

FNET_GROUPS = 4
FNET_GROUP_DIM = 64
FNET_WIDTH = FNET_GROUPS * FNET_GROUP_DIM
NA_HEADS = 12
NA_HEAD_DIM = 64
NA_WIDTH = NA_HEADS * NA_HEAD_DIM
NA_KH = 8
NA_KW = 16
NA_KEYW = 2 * NA_KW
NA_NCB = GRID_W // NA_KW
AB_IN = FNET_WIDTH + 3 * NA_WIDTH
AB_OUT = FNET_WIDTH + NA_WIDTH

RET_HEADS = 4
RET_DK = D_MODEL // RET_HEADS
RET_DV = 2 * RET_DK
RET_QK = RET_HEADS * RET_DK
RET_V = RET_HEADS * RET_DV
RET_IN = 2 * RET_QK + 2 * RET_V
RET_CHUNK = 128

N_EXPERTS = 16
N_GROUPS = 4
EXPERTS_PER_GROUP = N_EXPERTS // N_GROUPS
TOP_K = 2
D_EXPERT = D_MODEL // 2


def rmsnorm(x, g):
    xf = x.astype(jnp.float32)
    y = xf * lax.rsqrt(jnp.mean(xf * xf, axis=-1, keepdims=True) + RMS_EPS)
    return y.astype(x.dtype) * g

def modulate(x, shift, scale):
    return x * (1 + scale) + shift

def _rope_half(x, pos):
    n = x.shape[-1] // 2
    inv_freq = ROPE_BASE ** (-jnp.arange(n, dtype=jnp.float32) / n)
    ang = pos.astype(jnp.float32)[:, None] * inv_freq[None, :]
    cos = jnp.cos(ang)[None, :, None, :]
    sin = jnp.sin(ang)[None, :, None, :]
    xf = x.astype(jnp.float32)
    x1, x2 = xf[..., :n], xf[..., n:]
    return jnp.concatenate([x1 * cos - x2 * sin, x2 * cos + x1 * sin], axis=-1)

def axial_rope(x, row, col):
    half = x.shape[-1] // 2
    return jnp.concatenate([_rope_half(x[..., :half], row), _rope_half(x[..., half:], col)], axis=-1).astype(x.dtype)

def fourier_mix(a):
    B, N, _ = a.shape
    ag = a.reshape(B, N, FNET_GROUPS, FNET_GROUP_DIM).astype(jnp.float32)
    return jnp.fft.fft2(ag, axes=(1, 3), norm='ortho').real.astype(a.dtype).reshape(B, N, FNET_WIDTH)

def dense_attention(q, k, v):
    s = jnp.einsum('bqhd,bkhd->bhqk', q, k).astype(jnp.float32) * (q.shape[-1] ** -0.5)
    p = jax.nn.softmax(s, axis=-1).astype(v.dtype)
    return jnp.einsum('bhqk,bkhd->bqhd', p, v)

def _na_static():
    j = np.arange(NA_NCB)
    key_start = np.clip(j * NA_KW - NA_KW // 2, 0, GRID_W - NA_KEYW)
    key_cols = key_start[:, None] + np.arange(NA_KEYW)[None, :]
    q_cols = j[:, None] * NA_KW + np.arange(NA_KW)[None, :]
    win_start = np.clip(q_cols - NA_KW // 2, 0, GRID_W - NA_KW)[:, :, None]
    kc = key_cols[:, None, :]
    col_mask = (kc >= win_start) & (kc < win_start + NA_KW)
    dc_idx = np.clip(kc - q_cols[:, :, None] + NA_KW - 1, 0, 2 * NA_KW - 2)
    return key_cols, col_mask, dc_idx

def neighborhood_attention(q, k, v, k_ctx, v_ctx, rpb):
    B, L, H, Dh = q.shape
    rows = L // GRID_W
    kh = min(NA_KH, rows)
    scale = Dh ** -0.5
    key_cols, col_mask, dc_idx = _na_static()
    qg = q.reshape(B, rows, NA_NCB, NA_KW, H, Dh)
    kg = k.reshape(B, rows, GRID_W, H, Dh)
    vg = v.reshape(B, rows, GRID_W, H, Dh)
    rpb_cols = rpb[:, :, dc_idx]
    mask = jnp.asarray(col_mask)[None, None, :, :, None, :]

    def row_block(r):
        rs = jnp.clip(r - kh // 2, 0, rows - kh)
        k_blk = lax.dynamic_slice_in_dim(kg, rs, kh, axis=1)[:, :, key_cols]
        v_blk = lax.dynamic_slice_in_dim(vg, rs, kh, axis=1)[:, :, key_cols]
        q_r = lax.dynamic_index_in_dim(qg, r, axis=1, keepdims=False)
        s_loc = jnp.einsum('bjqhd,brjkhd->bhjqrk', q_r, k_blk).astype(jnp.float32) * scale
        dr = rs + jnp.arange(kh) - r + (NA_KH - 1)
        bias = jnp.transpose(rpb_cols[:, dr], (0, 2, 3, 1, 4)).astype(jnp.float32)
        s_loc = jnp.where(mask, s_loc + bias[None], -jnp.inf).reshape(B, H, NA_NCB, NA_KW, kh * NA_KEYW)
        s_ctx = jnp.einsum('bjqhd,bkhd->bhjqk', q_r, k_ctx).astype(jnp.float32) * scale
        p = jax.nn.softmax(jnp.concatenate([s_loc, s_ctx], axis=-1), axis=-1).astype(v.dtype)
        p_loc = p[..., :kh * NA_KEYW].reshape(B, H, NA_NCB, NA_KW, kh, NA_KEYW)
        p_ctx = p[..., kh * NA_KEYW:]
        return (jnp.einsum('bhjqrk,brjkhd->bjqhd', p_loc, v_blk)
                + jnp.einsum('bhjqk,bkhd->bjqhd', p_ctx, v_ctx))

    o = lax.map(row_block, jnp.arange(rows))
    return jnp.moveaxis(o, 0, 1).reshape(B, L, H * Dh)

def fnet_na_mixer(xm, cm, w_in, w_out, rpb, need_ctx):
    B, L, _ = xm.shape
    pl = xm @ w_in
    pc = cm @ w_in

    def heads(p):
        qkv = p[..., FNET_WIDTH:].reshape(p.shape[0], p.shape[1], 3, NA_HEADS, NA_HEAD_DIM)
        return qkv[:, :, 0], qkv[:, :, 1], qkv[:, :, 2]

    ql, kl, vl = heads(pl)
    qc, kc, vc = heads(pc)
    a_lat = fourier_mix(pl[..., :FNET_WIDTH])
    o_lat = neighborhood_attention(ql, kl, vl, kc, vc, rpb)
    y_lat = jnp.concatenate([a_lat, o_lat], axis=-1) @ w_out
    y_ctx = None
    if need_ctx:
        a_ctx = fourier_mix(pc[..., :FNET_WIDTH])
        o_ctx = dense_attention(qc, kc, vc).reshape(B, -1, NA_WIDTH)
        y_ctx = jnp.concatenate([a_ctx, o_ctx], axis=-1) @ w_out
    return y_lat, y_ctx

def retention_scan(q, k, v, log_gamma):
    B, H, N, dk = q.shape
    dv = v.shape[-1]
    nc = N // RET_CHUNK

    def chunks(t):
        return jnp.moveaxis(t.reshape(B, H, nc, RET_CHUNK, t.shape[-1]), 2, 0)

    pos = jnp.arange(RET_CHUNK, dtype=jnp.float32)
    diff = pos[:, None] - pos[None, :]
    lower = diff >= 0
    intra_decay = jnp.where(lower, jnp.exp(jnp.where(lower, diff, 0.0)[None] * log_gamma[:, None, None]), 0.0)
    q_decay = jnp.exp((pos + 1.0)[None, :] * log_gamma[:, None])[..., None]
    k_decay = jnp.exp((RET_CHUNK - 1.0 - pos)[None, :] * log_gamma[:, None])[..., None]
    chunk_decay = jnp.exp(RET_CHUNK * log_gamma)[:, None, None]

    def step(state, qkv):
        qc, kc, vc = qkv
        scores = jnp.einsum('bhnd,bhmd->bhnm', qc, kc) * intra_decay
        out = (jnp.einsum('bhnm,bhmv->bhnv', scores, vc)
               + jnp.einsum('bhnd,bhdv->bhnv', qc * q_decay, state))
        state = state * chunk_decay + jnp.einsum('bhmd,bhmv->bhdv', kc * k_decay, vc)
        return state, out

    state0 = jnp.zeros((B, H, dk, dv), jnp.float32)
    _, out = lax.scan(step, state0, (chunks(q), chunks(k), chunks(v)))
    return jnp.moveaxis(out, 0, 2).reshape(B, H, N, dv)

def retention_mixer(xm, cm, w_in, w_out, decay_param, row, col, need_ctx):
    B, L, _ = xm.shape
    n_ctx = cm.shape[1]

    def split(p):
        n = p.shape[1]
        q = p[..., :RET_QK].reshape(B, n, RET_HEADS, RET_DK)
        k = p[..., RET_QK:2 * RET_QK].reshape(B, n, RET_HEADS, RET_DK) * (RET_DK ** -0.5)
        v = p[..., 2 * RET_QK:2 * RET_QK + RET_V].reshape(B, n, RET_HEADS, RET_DV)
        g = p[..., 2 * RET_QK + RET_V:]
        return q, k, v, g

    ql, kl, vl, gl = split(xm @ w_in)
    qc, kc, vc, gc = split(cm @ w_in)
    ql = axial_rope(ql, row, col)
    kl = axial_rope(kl, row, col)

    def bhnd(t_ctx, t_lat):
        return jnp.concatenate([t_ctx, t_lat], axis=1).transpose(0, 2, 1, 3).astype(jnp.float32)

    q, k, v = bhnd(qc, ql), bhnd(kc, kl), bhnd(vc, vl)
    log_gamma = jnp.log1p(-jnp.exp(decay_param.astype(jnp.float32)))

    def flip(t):
        return jnp.concatenate([t[:, :, :n_ctx][:, :, ::-1], t[:, :, n_ctx:][:, :, ::-1]], axis=2)

    o = retention_scan(q, k, v, log_gamma[0]) + flip(retention_scan(flip(q), flip(k), flip(v), log_gamma[1]))

    def gated_out(o_part, g):
        on = o_part * lax.rsqrt(jnp.mean(o_part * o_part, axis=-1, keepdims=True) + RMS_EPS)
        on = on.transpose(0, 2, 1, 3).reshape(B, -1, RET_V).astype(g.dtype)
        return (jax.nn.silu(g) * on) @ w_out

    y_lat = gated_out(o[:, :, n_ctx:], gl)
    y_ctx = gated_out(o[:, :, :n_ctx], gc) if need_ctx else None
    return y_lat, y_ctx

def moe_ffn(tok, router_w, router_b, w1, w3, w2):
    T = tok.shape[0]
    scores = jax.nn.sigmoid((tok @ router_w).astype(jnp.float32))
    biased = (scores + router_b.astype(jnp.float32)).reshape(T, N_GROUPS, EXPERTS_PER_GROUP)
    group_score = lax.top_k(biased, TOP_K)[0].sum(axis=-1)
    g_sel = jnp.argmax(group_score, axis=-1)
    in_group = jnp.take_along_axis(biased, g_sel[:, None, None], axis=1)[:, 0]
    _, local = lax.top_k(in_group, TOP_K)
    expert_idx = g_sel[:, None] * EXPERTS_PER_GROUP + local
    w = jnp.take_along_axis(scores, expert_idx, axis=-1)
    w = w / jnp.sum(w, axis=-1, keepdims=True)
    gate = jnp.sum(jax.nn.one_hot(expert_idx, N_EXPERTS, dtype=jnp.float32) * w[..., None], axis=1).astype(tok.dtype)
    out = jnp.zeros_like(tok)
    for e in range(N_EXPERTS):
        hid = jax.nn.silu(tok @ w1[e]) * (tok @ w3[e])
        out = out + gate[:, e:e + 1] * (hid @ w2[e])
    return out

def first_inputs(seed: int = 0) -> dict:
    key = jax.random.key(seed)
    ks = jax.random.split(key, 20)
    n_even = (DEPTH + 1) // 2
    n_odd = DEPTH // 2

    def nrm(k, shape, scale):
        return jax.random.normal(k, shape, jnp.float32) * scale

    base_decay = -(5.0 + jnp.arange(RET_HEADS, dtype=jnp.float32)) * math.log(2.0)
    return {
        'x': nrm(ks[0], (BATCH, SEQ, D_MODEL), 1.0),
        'c': nrm(ks[1], (BATCH, D_MODEL), 1.0),
        'ctx': nrm(ks[2], (BATCH, CTX_LEN, D_MODEL), 1.0),
        'c_ctx': nrm(ks[3], (D_MODEL,), 1.0),
        'ada_w': nrm(ks[4], (DEPTH, D_MODEL, 6 * D_MODEL), 0.5 * D_MODEL ** -0.5),
        'ada_b': nrm(ks[5], (DEPTH, 6 * D_MODEL), 0.02),
        'norm_g': 1.0 + nrm(ks[6], (DEPTH, 2, D_MODEL), 0.02),
        'final_norm_g': 1.0 + nrm(ks[7], (D_MODEL,), 0.02),
        'mixab_w_in': nrm(ks[8], (n_even, D_MODEL, AB_IN), D_MODEL ** -0.5),
        'mixab_w_out': nrm(ks[9], (n_even, AB_OUT, D_MODEL), AB_OUT ** -0.5),
        'na_rpb': nrm(ks[10], (n_even, NA_HEADS, 2 * NA_KH - 1, 2 * NA_KW - 1), 0.1),
        'ret_w_in': nrm(ks[11], (n_odd, D_MODEL, RET_IN), D_MODEL ** -0.5),
        'ret_w_out': nrm(ks[12], (n_odd, RET_V, D_MODEL), RET_V ** -0.5),
        'ret_decay': base_decay[None, None, :] + nrm(ks[13], (n_odd, 2, RET_HEADS), 0.05),
        'router_w': nrm(ks[14], (D_MODEL, N_EXPERTS), D_MODEL ** -0.5),
        'router_b': nrm(ks[15], (N_EXPERTS,), 0.01),
        'moe_w1': nrm(ks[16], (DEPTH, N_EXPERTS, D_MODEL, D_EXPERT), D_MODEL ** -0.5),
        'moe_w3': nrm(ks[17], (DEPTH, N_EXPERTS, D_MODEL, D_EXPERT), D_MODEL ** -0.5),
        'moe_w2': nrm(ks[18], (DEPTH, N_EXPERTS, D_EXPERT, D_MODEL), D_EXPERT ** -0.5),
    }

def first_block(x, c, ctx, c_ctx, ada_w, ada_b, norm_g, final_norm_g, mixab_w_in, mixab_w_out, na_rpb,
              ret_w_in, ret_w_out, ret_decay, router_w, router_b, moe_w1, moe_w3, moe_w2):
    B, L, D = x.shape
    t = jnp.arange(L)
    row, col = t // GRID_W, t % GRID_W
    h, hc = x, ctx
    for layer in range(DEPTH):
        need_ctx = layer < DEPTH - 1
        mod = jax.nn.silu(c) @ ada_w[layer] + ada_b[layer]
        mod_c = jax.nn.silu(c_ctx) @ ada_w[layer] + ada_b[layer]
        sh1, sc1, g1, sh2, sc2, g2 = [m[:, None, :] for m in jnp.split(mod, 6, axis=-1)]
        sh1c, sc1c, g1c, sh2c, sc2c, g2c = jnp.split(mod_c, 6, axis=-1)
        xm = modulate(rmsnorm(h, norm_g[layer, 0]), sh1, sc1)
        cm = modulate(rmsnorm(hc, norm_g[layer, 0]), sh1c, sc1c)
        idx = layer // 2
        if layer % 2 == 0:
            y, yc = fnet_na_mixer(xm, cm, mixab_w_in[idx], mixab_w_out[idx], na_rpb[idx], need_ctx)
        else:
            y, yc = retention_mixer(xm, cm, ret_w_in[idx], ret_w_out[idx], ret_decay[idx], row, col, need_ctx)
        h = h + g1 * y
        xm2 = modulate(rmsnorm(h, norm_g[layer, 1]), sh2, sc2)
        if need_ctx:
            hc = hc + g1c * yc
            cm2 = modulate(rmsnorm(hc, norm_g[layer, 1]), sh2c, sc2c)
            n_c = cm2.shape[0] * cm2.shape[1]
            tok = jnp.concatenate([cm2.reshape(-1, D), xm2.reshape(-1, D)], axis=0)
            f = moe_ffn(tok, router_w, router_b, moe_w1[layer], moe_w3[layer], moe_w2[layer])
            hc = hc + g2c * f[:n_c].reshape(hc.shape)
            h = h + g2 * f[n_c:].reshape(h.shape)
        else:
            f = moe_ffn(xm2.reshape(-1, D), router_w, router_b, moe_w1[layer], moe_w3[layer], moe_w2[layer])
            h = h + g2 * f.reshape(h.shape)
    return rmsnorm(h, final_norm_g)


DEPTH_2 = 1

EPS = 1e-6
ATTN_GROUPS = ((128, 1), (512, 4), (2048, 16))
N_GROUPS_2 = 3
HEADS_PER_GROUP = 8
HEAD_DIM = 64
ATTN_WIDTH = HEADS_PER_GROUP * HEAD_DIM
N_ATTN_HEADS = N_GROUPS_2 * HEADS_PER_GROUP
ATTN_QKV_COLS = N_GROUPS_2 * 3 * ATTN_WIDTH
NUM_BUCKETS = 32
REL_MAX_DISTANCE = 1024
NEG_INF = -1e30
HG_HEADS = 8
HG_DK = D_MODEL // HG_HEADS
HG_DV = D_MODEL // HG_HEADS
HG_WIDTH = HG_HEADS * HG_DV
HG_CHUNK = 32
SPLIT_SIZES = (ATTN_QKV_COLS, ATTN_WIDTH, HG_WIDTH, HG_WIDTH, HG_WIDTH, HG_WIDTH, HG_WIDTH, D_MODEL, D_MODEL)
IN_COLS = ATTN_QKV_COLS + ATTN_WIDTH + 5 * HG_WIDTH + 2 * D_MODEL


def rms_norm(t, w):
    t32 = t.astype(jnp.float32)
    return t32 * lax.rsqrt(jnp.mean(t32 * t32, axis=-1, keepdims=True) + EPS) * w.astype(jnp.float32)

def t5_bucket(rel):
    half = NUM_BUCKETS // 2
    max_exact = half // 2
    n = np.abs(rel)
    large = max_exact + (np.log(np.maximum(n, 1) / max_exact)
                         / np.log(REL_MAX_DISTANCE / max_exact) * (half - max_exact)).astype(np.int32)
    large = np.minimum(large, half - 1)
    return np.where(rel > 0, half, 0) + np.where(n < max_exact, n, large)

def dilated_window_attention(q, k, v, bias_table, window, dilation):
    B, S, H, Dh = q.shape
    side = (window // 2) // dilation
    blk = side
    L = S // dilation
    nb = -(-L // blk)
    Lp = nb * blk

    def to_blocks(t):
        t = t.reshape(B, L, dilation, H, Dh)
        t = jnp.pad(t, ((0, 0), (0, Lp - L), (0, 0), (0, 0), (0, 0)))
        return t.reshape(B, nb, blk, dilation, H, Dh)

    def with_halo(t):
        tp = jnp.pad(t, ((0, 0), (1, 1), (0, 0), (0, 0), (0, 0), (0, 0)))
        return jnp.concatenate([tp[:, :-2], tp[:, 1:-1], tp[:, 2:]], axis=2)

    def from_blocks(t):
        t = t.reshape((B, Lp) + t.shape[3:])[:, :L]
        return t.reshape((B, S) + t.shape[3:])

    qb = to_blocks(q) * (HEAD_DIM ** -0.5)
    kh = with_halo(to_blocks(k))
    vh = with_halo(to_blocks(v))

    i_idx = np.arange(blk)[:, None]
    j_idx = np.arange(3 * blk)[None, :]
    rel = j_idx - blk - i_idx
    bias = jnp.transpose(bias_table[t5_bucket(rel * dilation)], (2, 0, 1))
    t_key = np.arange(nb)[:, None, None] * blk - blk + j_idx[None]
    valid = (np.abs(rel)[None] <= side) & (t_key >= 0) & (t_key < L)

    s = jnp.einsum('bnqrhd,bnkrhd->bnrhqk', qb, kh) + bias
    s = jnp.where(valid[None, :, None, None], s, NEG_INF)
    m = jnp.max(s, axis=-1, keepdims=True)
    p = jnp.exp(s - m)
    den = jnp.transpose(jnp.sum(p, axis=-1), (0, 1, 4, 2, 3))
    o = jnp.einsum('bnrhqk,bnkrhd->bnqrhd', p, vh) / den[..., None]
    m = jnp.transpose(m[..., 0], (0, 1, 4, 2, 3))
    return from_blocks(o), from_blocks(m), from_blocks(den)

def gla_chunk_scan(q, k, v, log_f):
    B, T, H, DK = q.shape
    DV = v.shape[-1]
    N = T // HG_CHUNK

    def chunks(t):
        return t.reshape(B, N, HG_CHUNK, H, t.shape[-1]).transpose(1, 0, 3, 2, 4)

    qc, kc, vc, gc = chunks(q), chunks(k), chunks(v), chunks(log_f)
    b = jnp.cumsum(gc, axis=3)
    b_last = b[:, :, :, -1, :]
    q_t = qc * jnp.exp(b)
    k_t = kc * jnp.exp(-b)
    k_s = kc * jnp.exp(b_last[:, :, :, None, :] - b)
    lower = jnp.tril(jnp.ones((HG_CHUNK, HG_CHUNK), dtype=bool))
    a = jnp.where(lower, jnp.einsum('nbhik,nbhjk->nbhij', q_t, k_t), 0.0)
    o_intra = jnp.einsum('nbhij,nbhjv->nbhiv', a, vc)

    def step(state, xs):
        q_n, k_n, v_n, dec_n = xs
        o_n = jnp.einsum('bhik,bhkv->bhiv', q_n, state)
        state = dec_n[..., None] * state + jnp.einsum('bhik,bhiv->bhkv', k_n, v_n)
        return state, o_n

    s0 = jnp.zeros((B, H, DK, DV), jnp.float32)
    _, o_inter = lax.scan(step, s0, (q_t, k_s, vc, jnp.exp(b_last)))
    o = o_intra + o_inter
    return o.transpose(1, 0, 3, 2, 4).reshape(B, T, H, DV)

def hgrn2_scan(q, i, z_f, lb):
    f = lb + (1.0 - lb) * jax.nn.sigmoid(z_f)
    return gla_chunk_scan(q, 1.0 - f, i, jnp.log(f))

def second_inputs(seed: int = 0) -> dict:
    key = jax.random.key(seed)
    ks = jax.random.split(key, 12)
    f32 = jnp.float32
    nrm = jax.random.normal
    return {
        "x": nrm(ks[0], (BATCH, SEQ, D_MODEL), f32),
        "norm_w": 1.0 + 0.02 * nrm(ks[1], (DEPTH_2, D_MODEL), f32),
        "w_in": nrm(ks[2], (DEPTH_2, D_MODEL, IN_COLS), f32) * D_MODEL ** -0.5,
        "q_norm_w": 1.0 + 0.02 * nrm(ks[3], (DEPTH_2, N_GROUPS_2, HEAD_DIM), f32),
        "k_norm_w": 1.0 + 0.02 * nrm(ks[4], (DEPTH_2, N_GROUPS_2, HEAD_DIM), f32),
        "rel_bias": 0.5 * nrm(ks[5], (NUM_BUCKETS, N_ATTN_HEADS), f32),
        "lb_fwd": 0.1 * nrm(ks[6], (DEPTH_2 + 1, HG_HEADS * HG_DK), f32),
        "lb_bwd": 0.1 * nrm(ks[7], (DEPTH_2 + 1, HG_HEADS * HG_DK), f32),
        "hg_norm_w": 1.0 + 0.02 * nrm(ks[8], (DEPTH_2, HG_DV), f32),
        "w_proj_a": nrm(ks[9], (DEPTH_2, ATTN_WIDTH, D_MODEL), f32) * ATTN_WIDTH ** -0.5,
        "w_proj_b": nrm(ks[10], (DEPTH_2, HG_WIDTH, D_MODEL), f32) * HG_WIDTH ** -0.5,
        "w_out": nrm(ks[11], (DEPTH_2, D_MODEL, D_MODEL), f32) * D_MODEL ** -0.5,
    }

def second_block(x, norm_w, w_in, q_norm_w, k_norm_w, rel_bias, lb_fwd, lb_bwd, hg_norm_w,
              w_proj_a, w_proj_b, w_out):
    f32 = jnp.float32
    B, S, _ = x.shape
    split_points = np.cumsum(SPLIT_SIZES)[:-1].tolist()
    lb_f_all = jnp.cumsum(jax.nn.softmax(lb_fwd.astype(f32), axis=0), axis=0)
    lb_b_all = jnp.cumsum(jax.nn.softmax(lb_bwd.astype(f32), axis=0), axis=0)
    bias_tab = rel_bias.astype(f32)
    h_res = x.astype(f32)
    for layer in range(DEPTH_2):
        h = rms_norm(h_res, norm_w[layer])
        z = jnp.einsum('bsd,dc->bsc', h, w_in[layer].astype(f32))
        qkv_a, g_a, q_b, zf_fwd, zf_bwd, i_b, g_b, zgate_a, zgate_b = jnp.split(z, split_points, axis=-1)

        qkv_a = qkv_a.reshape(B, S, N_GROUPS_2, 3, HEADS_PER_GROUP, HEAD_DIM)
        outs, maxes, dens = [], [], []
        for g, (window, dilation) in enumerate(ATTN_GROUPS):
            q = rms_norm(qkv_a[:, :, g, 0], q_norm_w[layer, g])
            k = rms_norm(qkv_a[:, :, g, 1], k_norm_w[layer, g])
            v = qkv_a[:, :, g, 2]
            o_g, m_g, d_g = dilated_window_attention(
                q, k, v, bias_tab[:, g * HEADS_PER_GROUP:(g + 1) * HEADS_PER_GROUP], window, dilation)
            outs.append(o_g)
            maxes.append(m_g)
            dens.append(d_g)
        m_all = jnp.stack(maxes)
        wts = jnp.stack(dens) * jnp.exp(m_all - jnp.max(m_all, axis=0, keepdims=True))
        o_a = jnp.sum(wts[..., None] * jnp.stack(outs), axis=0) / jnp.sum(wts, axis=0)[..., None]
        y_a = jnp.einsum('bsc,cd->bsd', o_a.reshape(B, S, ATTN_WIDTH) * jax.nn.silu(g_a),
                         w_proj_a[layer].astype(f32))

        q_b = q_b.reshape(B, S, HG_HEADS, HG_DK)
        i_b = i_b.reshape(B, S, HG_HEADS, HG_DV)
        zf_fwd = zf_fwd.reshape(B, S, HG_HEADS, HG_DK)
        zf_bwd = zf_bwd.reshape(B, S, HG_HEADS, HG_DK)
        lb_f = lb_f_all[layer].reshape(HG_HEADS, HG_DK)
        lb_b = lb_b_all[layer].reshape(HG_HEADS, HG_DK)
        o_fwd = hgrn2_scan(q_b, i_b, zf_fwd, lb_f)
        o_bwd = jnp.flip(hgrn2_scan(jnp.flip(q_b, 1), jnp.flip(i_b, 1), jnp.flip(zf_bwd, 1), lb_b), 1)
        o_b = rms_norm(o_fwd + o_bwd, hg_norm_w[layer]) * jax.nn.silu(g_b.reshape(B, S, HG_HEADS, HG_DV))
        y_b = jnp.einsum('bsc,cd->bsd', o_b.reshape(B, S, HG_WIDTH), w_proj_b[layer].astype(f32))

        merged = jax.nn.sigmoid(zgate_a) * y_a + jax.nn.sigmoid(zgate_b) * y_b
        h_res = h_res + jnp.einsum('bsd,de->bse', merged, w_out[layer].astype(f32))
    return h_res.astype(x.dtype)


def setup_inputs(seed=0):
    out = dict(first_inputs(seed))
    for name, value in second_inputs(seed + 1).items():
        if name != "x":
            out[name + "_2"] = value
    return out


def reference(
    x, c, ctx, c_ctx, ada_w, ada_b, norm_g, final_norm_g, mixab_w_in, mixab_w_out, na_rpb,
    ret_w_in, ret_w_out, ret_decay, router_w, router_b, moe_w1, moe_w3, moe_w2, norm_w_2,
    w_in_2, q_norm_w_2, k_norm_w_2, rel_bias_2, lb_fwd_2, lb_bwd_2, hg_norm_w_2, w_proj_a_2,
    w_proj_b_2, w_out_2,
):
    x = first_block(
        x, c, ctx, c_ctx, ada_w, ada_b, norm_g, final_norm_g, mixab_w_in, mixab_w_out, na_rpb,
        ret_w_in, ret_w_out, ret_decay, router_w, router_b, moe_w1, moe_w3, moe_w2,
    )
    return second_block(
        x, norm_w_2, w_in_2, q_norm_w_2, k_norm_w_2, rel_bias_2, lb_fwd_2, lb_bwd_2,
        hg_norm_w_2, w_proj_a_2, w_proj_b_2, w_out_2,
    )


_drawn_inputs = setup_inputs


def setup_inputs(seed=0):
    import zlib

    import numpy as np

    out = dict(_drawn_inputs(seed))
    spreads = {}
    factors = {'na_rpb': 8.0,
     'norm_w_2': 3.946,
     'q_norm_w_2': 8.0,
     'k_norm_w_2': 8.0,
     'rel_bias_2': 3.478,
     'lb_fwd_2': 3.077,
     'lb_bwd_2': 3.207,
     'hg_norm_w_2': 8.0}
    for name, (base, spread) in spreads.items():
        noise = np.random.default_rng([zlib.crc32(name.encode()), seed]).standard_normal(out[name].shape)
        drawn = base * np.exp(spread * noise) if base else spread * noise
        out[name] = jnp.asarray(drawn.astype(out[name].dtype))
    for name, factor in factors.items():
        out[name] = (out[name] * factor).astype(out[name].dtype)
    return out
```

```python
from contextlib import ExitStack

import numpy as np
import concourse.bass as bass
from concourse import mybir

F32 = mybir.dt.float32
ALU = mybir.AluOpType
ACT = mybir.ActivationFunctionType
AX = mybir.AxisListType

P = 128
D = 1024
KT = D // P
SEQ = 256
T = 2 * SEQ
CTX, LAT = slice(0, SEQ), slice(SEQ, T)
SLOTS = 3
BLK = 4096
BIG = 1e30
EPS = 1e-6

GRID_W = 64
ROWS = SEQ // GRID_W
NA_H = 12
NA_KH, NA_KW = 8, 16
RPB_W = 2 * NA_KW - 1
RPB_HEAD = (2 * NA_KH - 1) * RPB_W
HD = 64

RET_H = 4
EXPERTS = 16

AT_H = 8
AT_G = 3
GROUPS = ((128, 1), (512, 4), (2048, 16))
BUCKETS = 32
HG = 8
CH = 32
NCH = SEQ // CH

B_ADA = 0
B_MIX = B_ADA + 24
B_MIXO = B_MIX + 5
B_MOE0 = B_MIXO + 2
B_RET = B_MOE0 + 48
B_RETO = B_RET + 12
B_MOE1 = B_RETO + 4
B_Z1 = B_MOE1 + 48
B_IB = B_Z1 + 12
B_Z2 = B_IB + 2
B_V2 = B_Z2 + 7
B_PA = B_V2 + 3
B_PB = B_PA + 1
B_WO = B_PB + 2
N_BLK = B_WO + 2



def columns(*parts):
    at, out = 0, {}
    for name, n in parts:
        out[name] = slice(at, at + n)
        at += n
    return out, at


CST, CST_N = columns(("ident", P), ("ones", P), ("ones64", P), ("flip", P), ("flip64", P), ("tie", 16))
CA, CA_N = columns(("dft64", 2 * P), ("cos", 2 * SEQ), ("msin", 2 * SEQ), ("keep8", GRID_W), ("shut8", GRID_W))
CB, CB_N = columns(("rcos", SEQ), ("rsin", SEQ), ("ctx_f", 2 * SEQ), ("ctx_b", 2 * SEQ), ("lat_f", 2 * SEQ),
                   ("lat_b", 2 * SEQ), ("twice", 2 * SEQ))
CC, CC_N = columns(("runs", SEQ), ("mask_f", P), ("mask_b", P), ("onehot", 511), ("shut8", 511))
SM, SM_N = columns(("c2", 2 * KT), ("ada_b", 96), ("norm_g", 4 * KT), ("final_g", KT), ("norm_w2", KT),
                   ("router_w", KT * 16), ("router_b", 16), ("decay", 8), ("qn", 3), ("kn", 3), ("lb", 32),
                   ("hgw", 1), ("rel_bias", 24))


def t5_bucket(rel):
    half = BUCKETS // 2
    exact = half // 2
    n = np.abs(rel)
    large = exact + (np.log(np.maximum(n, 1) / exact) / np.log(1024 / exact) * (half - exact)).astype(np.int32)
    return np.where(rel > 0, half, 0) + np.where(n < exact, n, np.minimum(large, half - 1))


def constants():
    f = np.float32
    i128 = np.arange(P)
    cst = np.zeros((P, CST_N), f)
    cst[:, CST["ident"]] = np.eye(P)
    cst[:, CST["ones"]] = 1
    same64 = i128[:, None] // HD == i128[None] // HD
    cst[:, CST["ones64"]] = same64
    cst[:, CST["flip"]] = np.eye(P)[::-1]
    cst[:, CST["flip64"]] = same64 * (i128[:, None] % HD + i128[None] % HD == HD - 1)
    cst[:, CST["tie"]] = (np.arange(4)[None, :] < np.arange(4)[:, None]).reshape(1, 16)

    ca = np.zeros((P, CA_N), f)
    w64 = 2 * np.pi * np.outer(np.arange(64), np.arange(64)) / 64
    same = (i128[:, None] // 64 == i128[None] // 64)
    ca[:, CA["dft64"]] = np.concatenate([np.tile(np.cos(w64), (2, 2)) * same, np.tile(np.sin(w64), (2, 2)) * same], 1)
    w256 = 2 * np.pi * (np.outer(np.arange(256), np.arange(256)) % 256) / 256
    tiles = lambda m: m.reshape(2, P, SEQ).transpose(1, 0, 2).reshape(P, 2 * SEQ)
    ca[:, CA["cos"]] = tiles(np.cos(w256) / 128)
    ca[:, CA["msin"]] = tiles(-np.sin(w256) / 128)
    qc = (GRID_W - 1 - i128 % GRID_W)[:, None]
    kc = np.arange(GRID_W)[None]
    ws = np.clip(qc - NA_KW // 2, 0, GRID_W - NA_KW)
    inside = (kc >= ws) & (kc < ws + NA_KW)
    ca[:, CA["keep8"]] = inside * 8.0
    ca[:, CA["shut8"]] = np.where(inside, 0.0, -8.0 * BIG)

    cb = np.zeros((P, CB_N), f)
    t = np.arange(SEQ)
    inv = f(10000.0) ** (-np.arange(64, dtype=f) / f(64))
    ang = np.concatenate([inv[:, None] * (t // GRID_W).astype(f)[None], inv[:, None] * (t % GRID_W).astype(f)[None]], 0)
    cb[:, CB["rcos"]] = np.cos(ang.astype(f))
    cb[:, CB["rsin"]] = np.sin(ang.astype(f))
    m, n = np.arange(SEQ)[:, None], np.arange(SEQ)[None]
    cb[:, CB["ctx_f"]] = tiles(SEQ + n - m)
    cb[:, CB["ctx_b"]] = tiles(SEQ - n + m)
    cb[:, CB["lat_f"]] = tiles(np.maximum(n - m, 0))
    cb[:, CB["lat_b"]] = tiles(np.maximum(m - n, 0))
    cb[:, CB["twice"]] = tiles(1.0 + (m == n))

    cc = np.zeros((P, CC_N), f)
    cc[:, CC["runs"]] = (t % CH != 0)
    chunk = i128[:, None] // CH == i128[None] // CH
    cc[:, CC["mask_f"]] = (chunk & (i128[:, None] <= i128[None])) | (i128[:, None] // CH < i128[None] // CH)
    cc[:, CC["mask_b"]] = (chunk & (i128[:, None] >= i128[None])) | (i128[:, None] // CH > i128[None] // CH)
    delta = np.arange(-255, 256)
    for g, (window, dil) in enumerate(GROUPS):
        cc[g * AT_H:(g + 1) * AT_H, CC["shut8"]] = np.where(
            (delta % dil == 0) & (np.abs(delta) <= (window // 2) // dil * dil), 0.0, -8.0 * BIG)
    cc[:BUCKETS, CC["onehot"]] = t5_bucket(delta)[None] == np.arange(BUCKETS)[:, None]

    sel = np.zeros((EXPERTS, EXPERTS, P), f)
    sel[np.arange(EXPERTS), np.arange(EXPERTS)] = 1
    return dict(cst=cst, ca=ca, cb=cb, cc=cc, sel=sel.reshape(EXPERTS, EXPERTS * P))


def build(nc, w_all, h0, smalls, rpb, cst_d, ca_d, cb_d, cc_d, sel_d, toep_d, out_d, dbg=None):
    ctx = ExitStack()
    with ctx:
        def sb(name, cols):
            return ctx.enter_context(nc.sbuf_tensor(name, [P, cols], F32))

        def sem(name):
            return ctx.enter_context(nc.semaphore(name))

        ps = ctx.enter_context(nc.psum_tensor("ps", [P, 8, 512], F32))

        ring = sb("ring", SLOTS * BLK)
        hT = sb("hT", KT * T)[:, :].rearrange("p (k t) -> p k t", k=KT)
        XT = sb("XT", KT * T)[:, :].rearrange("p (k t) -> p k t", k=KT)
        cst = sb("cst", CST_N)
        sm = sb("sm", SM_N)
        c2s = sb("c2s", 2 * KT)
        modc = sb("modc", 2 * 96)[:, :].rearrange("p (l m s) -> p l m s", l=2, s=2)
        gains = sb("gains", 4 * 2 * KT)[:, :].rearrange("p (n m s) -> p n m s", n=4, s=2)
        inv_rms = sb("inv_rms", T)
        tiny = sb("tiny", 64)
        eps_col = tiny[:, 32:33]
        tick = ctx.enter_context(nc.sbuf_tensor("tick", [P, 32], mybir.dt.bfloat16))
        arena = sb("arena", 30400)

        def area(at, cols):
            assert at + cols <= 30400
            return arena[:, at:at + cols]

        ident = cst[:, CST["ident"]]
        ones = cst[:, CST["ones"]]
        ones64 = cst[:, CST["ones64"]]
        flip, flip64 = cst[:, CST["flip"]], cst[:, CST["flip64"]]

        fnT = area(0, 1024).rearrange("p (f t) -> p f t", f=2)
        qkT = area(1024, 6144).rearrange("p (m t) -> p m t", m=12)
        Vt = area(7168, 3072).rearrange("p (t c) -> p t c", t=4)
        bias_na = area(10240, 6144).rearrange("p (q h k) -> p q h k", q=2, h=NA_H)
        ca = area(16384, CA_N)
        acs = area(18560, 1024).rearrange("p (b t c) -> p b t c", b=2, t=2)
        probs0 = area(20000, 1024).rearrange("p (b k) -> p b k", b=2)
        probsT0 = area(21024, 1024).rearrange("p (b k q) -> p b k q", b=2, k=4)
        stat = area(22048, 8 * 48 + 8)

        acc = area(0, 4096).rearrange("p (k t) -> p k t", k=KT)
        Gt = area(4096, 8192).rearrange("p (e t) -> p e t", e=EXPERTS)
        silu_b = area(12288, 1024).rearrange("p (b t) -> p b t", b=2)
        gated = area(13312, 1024).rearrange("p (b t) -> p b t", b=2)
        hid = area(14336, 2048).rearrange("p (m t) -> p m t", m=4)
        sel = area(16384, 2048).rearrange("p (e m) -> p e m", e=EXPERTS)
        rt = area(18432, 1024)
        gateT = area(19456, 512)

        qR = area(0, 2048).rearrange("p (h ab t) -> p h ab t", h=4, ab=2)
        kR = area(2048, 4096).rearrange("p (h ab t) -> p h ab t", h=4, ab=2)
        vR = area(6144, 8192).rearrange("p (t c) -> p t c", t=4)
        gR = area(14336, 4096).rearrange("p (m t) -> p m t", m=16)
        cb = area(18432, CB_N)
        decayT = area(21504, 2048).rearrange("p (b k t) -> p b k t", b=2, k=4)
        scoreT = area(23552, 2048).rearrange("p (b k t) -> p b k t", b=2, k=4)
        oR = area(25600, 1024).rearrange("p (m t) -> p m t", m=4)
        sqR = area(26624, 1024).rearrange("p (m t) -> p m t", m=4)
        rope_t = area(27648, 2048).rearrange("p (b h t) -> p b h t", b=2, h=4)
        irR = area(29696, SEQ)
        dec_t = area(29952, 128)

        z1 = area(0, 12288).rearrange("p (s h t) -> p s h t", s=6, h=8)
        z1m = area(0, 12288).rearrange("p (m t) -> p m t", m=48)
        zf = z1[:, 0:2]
        q_b, g_b, zgA, zgB = z1[:, 2], z1[:, 3], z1[:, 4], z1[:, 5]
        ib = area(12288, 2048).rearrange("p (t c) -> p t c", t=2)
        lf = area(14336, 4096).rearrange("p (d h t) -> p d h t", d=2, h=8)
        bc = area(18432, 4096).rearrange("p (d h t) -> p d h t", d=2, h=8)
        cc = area(22528, CC_N)
        pt_b = area(24064, 1024).rearrange("p (b j i) -> p b j i", b=2, j=2)
        o_b = area(25088, 512).rearrange("p (b t) -> p b t", b=2)
        sq_b = area(25600, 512).rearrange("p (b t) -> p b t", b=2)
        ir_b = area(26112, 512).rearrange("p (b t) -> p b t", b=2)
        decs = area(26624, 128).rearrange("p (d h c) -> p d h c", d=2, h=8)
        lbt = area(26752, 128)
        toep = area(26880, 512)
        mrg = area(27392, 256)
        z2 = area(14336, 7168).rearrange("p (m t) -> p m t", m=28)
        v2 = area(21504, 3072).rearrange("p (g t c) -> p g t c", g=3, t=2)
        bias2 = area(24576, 3072).rearrange("p (b q g k) -> p b q g k", b=2, q=2, g=3)
        probs2 = area(27648, 1536).rearrange("p (b k) -> p b k", b=2)
        sq2 = area(29184, 1024).rearrange("p (b t) -> p b t", b=2)
        probsT2 = area(0, 768).rearrange("p (k q) -> p k q", k=6)
        ir2 = area(768, 1024).rearrange("p (b t) -> p b t", b=2)
        stat2 = area(1792, 64)

        ld_cst, ld_sm, ld_h, ld_rpb, ld_ca, ld_cb, ld_cc, ld_sel = map(sem, (
            "ld_cst", "ld_sm", "ld_h", "ld_rpb", "ld_ca", "ld_cb", "ld_cc", "ld_sel"))
        ld_bias2 = [sem(f"ld_bias2{j}") for j in range(2)]
        w_full = [sem(f"w_full{j}") for j in range(SLOTS)]
        w_free = sem("w_free")
        c2_ready, mod_ready, tick_ready = sem("c2_ready"), sem("mod_ready"), sem("tick_ready")
        nm_sq, nm_ms, nm_std, nm_tmp, nm_x = map(sem, ("nm_sq", "nm_ms", "nm_std", "nm_tmp", "nm_x"))
        res_done = sem("res_done")
        dve_step, act_step = sem("dve_step"), sem("act_step")
        mx_mm, mx_ev = sem("mx_mm"), sem("mx_ev")
        fn_mm, fn_ev = sem("fn_mm"), sem("fn_ev")
        bias_ready = sem("bias_ready")
        na_s, na_neg, na_e, na_p, na_t, na_c, na_o, na_ev = map(sem, (
            "na_s", "na_neg", "na_e", "na_p", "na_t", "na_c", "na_o", "na_ev"))
        mo_mm, mo_ev = sem("mo_mm"), sem("mo_ev")
        rt_mm, rt_sig, gate_ready, gT_mm, gT_ev, gb_mm, gb_ev = map(sem, (
            "rt_mm", "rt_sig", "gate_ready", "gT_mm", "gT_ev", "gb_mm", "gb_ev"))
        up1, up3, silu_rdy, gated_rdy, hid_rdy, dn_mm, dn_free = map(sem, (
            "up1", "up3", "silu_rdy", "gated_rdy", "hid_rdy", "dn_mm", "dn_free"))
        rp_mm, rp_ev, rope_done, lg_ready, dk_arg, dk_exp, dk_rdy, rs_mm, rs_rdy, ro_mm, ro_ev, rn_mm, rn_std, rn_rdy = \
            map(sem, ("rp_mm", "rp_ev", "rope_done", "lg_ready", "dk_arg", "dk_exp", "dk_rdy", "rs_mm", "rs_rdy",
                      "ro_mm", "ro_ev", "rn_mm", "rn_std", "rn_rdy"))
        y_mm, y_ev = sem("y_mm"), sem("y_ev")
        z1_mm, z1_ev, ib_mm, ib_ev = map(sem, ("z1_mm", "z1_ev", "ib_mm", "ib_ev"))
        f_rdy, lf_rdy, b_rdy, e_rdy = map(sem, ("f_rdy", "lf_rdy", "b_rdy", "e_rdy"))
        K_rdy, K_used, pt_rdy, ho_mm, ho_ev, hn_mm, hn_std, hg_done = map(sem, (
            "K_rdy", "K_used", "pt_rdy", "ho_mm", "ho_ev", "hn_mm", "hn_std", "hg_done"))
        lb_e, lb_s, tz_mm, tz_rdy, tz_st = map(sem, ("lb_e", "lb_s", "tz_mm", "tz_rdy", "tz_st"))
        z2_mm, z2_ev, v2_mm, v2_ev = map(sem, ("z2_mm", "z2_ev", "v2_mm", "v2_ev"))
        qn_sq, qn_mm, qn_std, qn_done = map(sem, ("qn_sq", "qn_mm", "qn_std", "qn_done"))
        at_s, at_neg, at_e, at_p, at_t, at_c, at_o, at_ev = map(sem, (
            "at_s", "at_neg", "at_e", "at_p", "at_t", "at_c", "at_o", "at_ev"))
        ya_mm, ya_ev, yb_mm, yb_ev, yo_mm, yo_ev, out_done = map(sem, (
            "ya_mm", "ya_ev", "yb_mm", "yb_ev", "yo_mm", "yo_ev", "out_done"))

        def slot(n, pattern=None, **kw):
            s = ring[:, (n % SLOTS) * BLK:(n % SLOTS + 1) * BLK]
            return s.rearrange(pattern, **kw) if pattern else s

        NORM_COLS = [(0, T), (0, T), (0, T), (SEQ, T), (SEQ, T), (SEQ, T)]
        NA_UNITS = [(seg, h, q) for seg in (1, 0) for h in range(NA_H) for q in range(2)]
        AT_UNITS = [(h, q) for h in range(AT_H) for q in range(2)]

        def na_q(seg, q):
            return slice(seg * SEQ + q * P, seg * SEQ + (q + 1) * P)

        def half(h):
            return slice(HD * (h % 2), HD * (h % 2) + HD)

        block = ctx.enter_context(nc.Block())

        @block.sync
        def _(sp):
            sp.dma_start(sm[:, :], smalls).then_inc(ld_sm, 16)
            for j in range(SLOTS):
                sp.dma_start(slot(j), w_all[j]).then_inc(w_full[j], 16)
                if j == 0:
                    sp.dma_start(cst[:, :], cst_d).then_inc(ld_cst, 16)
                    sp.dma_start(hT, h0).then_inc(ld_h, 16)
            with sp.Fori(0, (N_BLK - SLOTS) // SLOTS) as i:
                for j in range(SLOTS):
                    sp.wait_ge(w_free, i * SLOTS + j + 1)
                    sp.dma_start(slot(j), w_all[i * SLOTS + SLOTS + j]).then_inc(w_full[j], 16)
            for n in range(N_BLK - (N_BLK - SLOTS) % SLOTS, N_BLK):
                sp.wait_ge(w_free, n - SLOTS + 1)
                sp.dma_start(slot(n), w_all[n]).then_inc(w_full[n % SLOTS], 16)
            sp.wait_ge(yo_ev, KT)
            sp.dma_start(out_d, XT[:, :, LAT]).then_inc(out_done, 16)
            sp.wait_ge(out_done, 16)

        @block.gpsimd
        def _(pool):
            pool.dma_start(ca, ca_d).then_inc(ld_ca, 16)
            for layer in range(2):
                pool.wait_ge(res_done, 2 * layer + 1)
                pool.dma_start(sel[0:EXPERTS], sel_d).then_inc(ld_sel, 16)
                pool.wait_ge(res_done, 2 * layer + 2)
                if layer == 0:
                    pool.dma_start(cb, cb_d).then_inc(ld_cb, 16)
            pool.dma_start(cc, cc_d).then_inc(ld_cc, 16)
            pool.wait_ge(tz_rdy, 1)
            pool.dma_start(toep_d, toep[0:24, :]).then_inc(tz_st, 16)
            pool.wait_ge(tz_st, 16)
            pool.wait_ge(hg_done, HG)
            for h in range(AT_H):
                if h >= 2:
                    pool.wait_ge(at_s, 2 * (h - 1))
                for q in range(2):
                    pool.dma_start(bias2[:, h % 2, q], bass.AP(
                        tensor=toep_d.tensor, offset=h * 512 + P - P * q,
                        ap=[[1, P], [AT_H * 512, AT_G], [1, SEQ]])).then_inc(ld_bias2[h % 2], 16)

        @block.tensor
        def _(pe):
            def arrive(n):
                pe.wait_ge(w_full[n % SLOTS], 16 * (n // SLOTS + 1))

            def chain(out, pairs):
                for i, (a, b) in enumerate(pairs):
                    last = nc.tensor.matmul(out, a, b, start=(i == 0), stop=(i == len(pairs) - 1))
                return last

            def release():
                nc.tensor.matmul(ps[0:32, 7, 0:2], tick[:, 0:32], tick[:, 0:2], start=True, stop=True).then_inc(w_free, 1)

            def norm(i):
                a, b = NORM_COLS[i]
                for k in range(KT):
                    pe.wait_ge(nm_sq, KT * i + k + 1)
                    last = nc.tensor.matmul(ps[:, 7, 0:b - a], ones, XT[:, k, a:b], start=(k == 0), stop=(k == KT - 1))
                last.then_inc(nm_ms, 1)

            def router(layer):
                tts = range(4) if layer == 0 else range(2)
                t0 = 0 if layer == 0 else SEQ
                w = sm[:, SM["router_w"]].rearrange("p (k e) -> p k e", k=KT)
                for tt in tts:
                    last = chain(ps[:, 0, tt * 16:tt * 16 + 16],
                                 [(XT[:, k, t0 + tt * P:t0 + (tt + 1) * P], w[:, k]) for k in range(KT)])
                last.then_inc(rt_mm, 1)
                pe.wait_ge(gate_ready, layer + 1)
                for tt in tts:
                    last = nc.tensor.matmul(ps[0:16, 1, tt * P:(tt + 1) * P], rt[:, tt * 16:tt * 16 + 16], ident,
                                            start=True, stop=True)
                last.then_inc(gT_mm, 1)
                pe.wait_ge(gT_ev, layer + 1)
                pe.wait_ge(ld_sel, 16 * (layer + 1))
                n = len(tts) * P
                for e in range(EXPERTS):
                    if e >= 4:
                        pe.wait_ge(gb_ev, EXPERTS * layer + e - 3)
                    nc.tensor.matmul(ps[:, 2 + e % 4, 0:n], sel[0:EXPERTS, e], gateT[0:EXPERTS, 0:n],
                                     start=True, stop=True).then_inc(gb_mm, 1)
                pe.wait_ge(gb_ev, EXPERTS * (layer + 1))

            def experts(layer):
                base = B_MOE0 if layer == 0 else B_MOE1
                t0, n = (0, T) if layer == 0 else (SEQ, SEQ)
                pe.sem_inc(hid_rdy, 2)
                pe.sem_inc(dn_free, 2)
                u0, d0 = (4 * EXPERTS + 2) * layer, (8 * EXPERTS + 2) * layer
                w = [slot(base + j) for j in range(3)]
                w1, w3 = (x.rearrange("p (k m) -> p k m", k=KT) for x in w[:2])
                w2 = w[2].rearrange("p (k m) -> p k m", k=4)

                def arrive_e(e, n):
                    pe.wait_ge(w_full[n % SLOTS], e * 16 + 16 * (n // SLOTS + 1))

                with pe.Fori(0, EXPERTS) as e:
                    for m in range(4):
                        pe.wait_ge(hid_rdy, e * 4 + (u0 + m + 1))
                        for j, wj, done in ((0, w1, up1), (1, w3, up3)):
                            if m == 0:
                                arrive_e(e, base + j)
                            chain(ps[:, 2 * (m % 2) + j, 0:n],
                                  [(wj[:, k, m * P:(m + 1) * P], XT[:, k, t0:t0 + n]) for k in range(KT)]).then_inc(done, 1)
                            if m == 3:
                                release()
                    arrive_e(e, base + 2)
                    pe.wait_ge(hid_rdy, e * 4 + (u0 + 6))
                    for m in range(8):
                        pe.wait_ge(dn_free, e * 8 + (d0 + m + 1))
                        chain(ps[:, 4 + m % 2, 0:n],
                              [(w2[:, k, m * P:(m + 1) * P], hid[:, k, 0:n]) for k in range(4)]).then_inc(dn_mm, 1)
                    release()

            pe.wait_ge(ld_sm, 16)
            pe.wait_ge(c2_ready, 1)
            c2v = c2s[:, :].rearrange("p (k s) -> p k s", s=2)
            for layer in range(2):
                with pe.Fori(0, 4) as i:
                    for j in range(3):
                        n = B_ADA + 12 * layer + j
                        pe.wait_ge(w_full[n % SLOTS], i * 16 + 16 * (n // SLOTS + 1))
                        w = slot(n, "p (k m) -> p k m", k=KT)
                        for m in range(4):
                            last = chain(ps[:, layer, bass.ds(i * 24 + (8 * j + 2 * m), 2)],
                                         [(w[:, k, m * P:(m + 1) * P], c2v[:, k]) for k in range(KT)])
                        last.then_inc(w_free, 1)

            pe.wait_ge(ld_cst, 16)
            pe.wait_ge(tick_ready, 1)
            norm(0)
            pe.wait_ge(nm_x, KT)
            pe.wait_ge(mod_ready, 2)
            unit = 0
            for b in range(5):
                arrive(B_MIX + b)
                w = slot(B_MIX + b, "p (k m) -> p k m", k=KT)
                for m in range((4, 4, 4, 2, 0)[b]):
                    if unit >= 4:
                        pe.wait_ge(mx_ev, unit - 3)
                    chain(ps[:, unit % 4, :],
                          [(w[:, k, m * P:(m + 1) * P], XT[:, k, :]) for k in range(KT)]).then_inc(mx_mm, 1)
                    unit += 1
                if b >= 3:
                    cols = slice(256, 512) if b == 3 else slice(0, 512)
                    for tt in range(4):
                        pe.wait_ge(mx_ev, unit - 3)
                        chain(ps[:, unit % 4, 0:cols.stop - cols.start],
                              [(XT[:, k, tt * P:(tt + 1) * P], w[:, k, cols]) for k in range(KT)]).then_inc(mx_mm, 1)
                        unit += 1
                release()
            pe.wait_ge(mx_ev, unit)

            pe.wait_ge(ld_ca, 16)
            cosN = ca[:, CA["cos"]].rearrange("p (t n) -> p t n", t=2)
            msinN = ca[:, CA["msin"]].rearrange("p (t n) -> p t n", t=2)
            for n, (seg, f) in enumerate((s, f) for s in range(2) for f in range(2)):
                if n:
                    pe.wait_ge(fn_ev, 2 * n - 1)
                for tt in range(2):
                    last = nc.tensor.matmul(ps[:, 4, tt * 256:(tt + 1) * 256], fnT[:, f, na_q(seg, tt)],
                                            ca[:, CA["dft64"]], start=True, stop=True)
                last.then_inc(fn_mm, 1)
                pe.wait_ge(fn_ev, 2 * n + 1)
                chain(ps[:, 5, 0:SEQ], [(acs[:, 0, tt, c * P:(c + 1) * P], (cosN, msinN)[c][:, tt])
                                        for tt in range(2) for c in range(2)]).then_inc(fn_mm, 1)
            pe.wait_ge(fn_ev, 8)

            pe.wait_ge(bias_ready, 1)
            for i in range(len(NA_UNITS) + 2):
                if i < len(NA_UNITS):
                    seg, h, q = NA_UNITS[i]
                    nk = T if seg else SEQ
                    if i >= 3:
                        pe.wait_ge(na_e, i - 2)
                    last = nc.tensor.matmul(ps[:, i % 3, 0:nk], qkT[half(h), h // 2, na_q(seg, q)],
                                            qkT[half(h), 6 + h // 2, 0:nk], start=True, stop=not seg)
                    if seg:
                        last = nc.tensor.matmul(ps[:, i % 3, LAT], flip64, bias_na[:, q, h], start=False, stop=True)
                    last.then_inc(na_s, 1)
                if 0 <= i - 1 < len(NA_UNITS):
                    u = i - 1
                    pe.wait_ge(na_p, u + 1)
                    if u >= 2:
                        pe.wait_ge(na_c, u - 1)
                    for kt in range(4 if NA_UNITS[u][0] else 2):
                        last = nc.tensor.transpose(ps[:, 3 + u % 2, kt * P:(kt + 1) * P],
                                                   probs0[:, u % 2, kt * P:(kt + 1) * P], ident)
                    last.then_inc(na_t, 1)
                if i >= 2:
                    u = i - 2
                    seg, h, q = NA_UNITS[u]
                    pe.wait_ge(na_c, u + 1)
                    if u >= 2:
                        pe.wait_ge(na_ev, u - 1)
                    chain(ps[half(h), 5 + u % 2, 0:P],
                          [(Vt[:, kt, h * HD:(h + 1) * HD], probsT0[:, u % 2, kt])
                           for kt in range(4 if seg else 2)]).then_inc(na_o, 1)
            pe.wait_ge(na_ev, len(NA_UNITS))
            for b in range(2):
                arrive(B_MIXO + b)
                w = slot(B_MIXO + b, "p (k m) -> p k m", k=KT)
                for m in range(4):
                    u = 4 * b + m
                    if u >= 4:
                        pe.wait_ge(mo_ev, u - 3)
                    chain(ps[:, u % 4, :], [(w[:, k, m * P:(m + 1) * P], XT[:, k]) for k in range(KT)]).then_inc(mo_mm, 1)
                release()

            norm(1)
            pe.wait_ge(nm_x, 2 * KT)
            router(0)
            experts(0)

            norm(2)
            pe.wait_ge(nm_x, 3 * KT)
            unit = 0
            for b in range(12):
                arrive(B_RET + b)
                w = slot(B_RET + b, "p (k m) -> p k m", k=KT)
                for m in range(4):
                    if unit >= 4:
                        pe.wait_ge(rp_ev, unit - 3)
                    if 4 <= b < 8:
                        pairs = [(XT[:, k, m * P:(m + 1) * P], w[:, k]) for k in range(KT)]
                    else:
                        pairs = [(w[:, k, m * P:(m + 1) * P], XT[:, k, (0 if 2 <= b < 4 else SEQ):T]) for k in range(KT)]
                    chain(ps[:, unit % 4, 0:(T if 2 <= b < 8 else SEQ)], pairs).then_inc(rp_mm, 1)
                    unit += 1
                release()
            pe.wait_ge(rp_ev, unit)
            pe.wait_ge(rope_done, 2)

            def ret_scores(h):
                if h:
                    pe.wait_ge(rs_rdy, 2 * h)
                for kt in range(4):
                    last = chain(ps[:, kt // 2, (kt % 2) * SEQ:(kt % 2 + 1) * SEQ],
                                 [(kR[:, h, ab, kt * P:(kt + 1) * P], qR[:, h, ab]) for ab in range(2)])
                last.then_inc(rs_mm, 1)

            ret_scores(0)
            for h in range(RET_H):
                pe.wait_ge(rs_rdy, 2 * h + 2)
                if h:
                    pe.wait_ge(ro_ev, h)
                for dv in range(4):
                    last = chain(ps[:, 2 + dv // 2, (dv % 2) * SEQ:(dv % 2 + 1) * SEQ],
                                 [(vR[:, kt, h * 512 + dv * P:h * 512 + (dv + 1) * P], scoreT[:, h % 2, kt])
                                  for kt in range(4)])
                last.then_inc(ro_mm, 1)
                if h + 1 < RET_H:
                    ret_scores(h + 1)
                pe.wait_ge(ro_ev, h + 1)
                chain(ps[:, 4, 0:SEQ], [(ones, sqR[:, m]) for m in range(4)]).then_inc(rn_mm, 1)
            pe.wait_ge(rn_rdy, RET_H)
            for b in range(4):
                arrive(B_RETO + b)
                w = slot(B_RETO + b, "p (k m) -> p k m", k=16)
                for m in range(2):
                    u = 2 * b + m
                    if u >= 4:
                        pe.wait_ge(y_ev, u - 3)
                    chain(ps[:, u % 4, 0:SEQ], [(w[:, k, m * P:(m + 1) * P], gR[:, k]) for k in range(16)]).then_inc(y_mm, 1)
                release()

            norm(3)
            pe.wait_ge(nm_x, 4 * KT)
            router(1)
            experts(1)

            norm(4)
            norm(5)
            pe.wait_ge(nm_tmp, 6 * KT)
            pe.sem_inc(z1_ev, 6)
            with pe.Fori(0, 4) as i:
                for j in range(3):
                    n = B_Z1 + j
                    pe.wait_ge(w_full[n % SLOTS], i * 16 + 16 * (n // SLOTS + 1))
                    w = slot(n, "p (k m) -> p k m", k=KT)
                    for hf in range(2):
                        pe.wait_ge(z1_ev, i * 6 + (2 * j + hf + 1))
                        for m in range(2):
                            last = chain(ps[:, 2 * j + hf, m * SEQ:(m + 1) * SEQ],
                                         [(w[:, k, (2 * hf + m) * P:(2 * hf + m + 1) * P], XT[:, k, LAT]) for k in range(KT)])
                        last.then_inc(z1_mm, 1)
                    release()
            pe.wait_ge(z1_ev, 30)
            for b in range(2):
                arrive(B_IB + b)
                w = slot(B_IB + b, "p (k m) -> p k m", k=KT)
                for tt in range(2):
                    chain(ps[:, 2 * b + tt, :],
                          [(XT[:, k, SEQ + tt * P:SEQ + (tt + 1) * P], w[:, k]) for k in range(KT)]).then_inc(ib_mm, 1)
                release()
            pe.wait_ge(ld_cc, 16)
            nc.tensor.matmul(ps[0:24, 6, 0:511], sm[0:BUCKETS, SM["rel_bias"]], cc[0:BUCKETS, CC["onehot"]],
                             start=True, stop=True).then_inc(tz_mm, 1)
            pe.wait_ge(ib_ev, 4)

            def gla_scores(h):
                if h >= 2:
                    pe.wait_ge(pt_rdy, h - 1)
                for d in range(2):
                    pe.wait_ge(K_rdy, 2 * h + d + 1)
                    near, far = (0, 1) if d == 0 else (1, 0)
                    bank = 2 * (h % 2) + d
                    for c in range(NCH):
                        Kc = zf[:, d, c]
                        qc = lf[:, d, h, c * CH:(c + 1) * CH]
                        last = nc.tensor.matmul(ps[:, bank, c * CH:(c + 1) * CH], Kc[:, near * P:(near + 1) * P], qc,
                                                start=True, stop=True)
                        if c // 4 == far:
                            at = SEQ + (c % 4) * CH
                            last = nc.tensor.matmul(ps[:, bank, at:at + CH], Kc[:, far * P:(far + 1) * P], qc,
                                                    start=True, stop=True)
                    last.then_inc(K_used, 1)

            pe.wait_ge(tz_rdy, 1)
            gla_scores(0)
            for h in range(HG):
                if h + 1 < HG:
                    gla_scores(h + 1)
                pe.wait_ge(pt_rdy, h + 1)
                if h >= 2:
                    pe.wait_ge(ho_ev, h - 1)
                chain(ps[:, 4 + h % 2, 0:SEQ],
                      [(ib[:, j, h * P:(h + 1) * P], pt_b[:, h % 2, j]) for j in range(2)]).then_inc(ho_mm, 1)
                pe.wait_ge(ho_ev, h + 1)
                if h:
                    pe.wait_ge(hn_std, h)
                nc.tensor.matmul(ps[:, 6, 0:SEQ], ones, sq_b[:, h % 2], start=True, stop=True).then_inc(hn_mm, 1)
            pe.wait_ge(hg_done, HG)

            for b in range(10):
                arrive(B_Z2 + b)
                w = slot(B_Z2 + b, "p (k m) -> p k m", k=KT)
                for hf in range(2):
                    u = 2 * b + hf
                    if u >= 6:
                        pe.wait_ge(z2_ev, u - 5)
                    if b < 7:
                        for m in range(2):
                            last = chain(ps[:, u % 6, m * SEQ:(m + 1) * SEQ],
                                         [(w[:, k, (2 * hf + m) * P:(2 * hf + m + 1) * P], XT[:, k, LAT]) for k in range(KT)])
                    else:
                        last = chain(ps[:, u % 6, :],
                                     [(XT[:, k, SEQ + hf * P:SEQ + (hf + 1) * P], w[:, k]) for k in range(KT)])
                    last.then_inc(z2_mm, 1)
                release()
            for u in range(12):
                pe.wait_ge(qn_sq, u + 1)
                if u >= 2:
                    pe.wait_ge(qn_std, u - 1)
                nc.tensor.matmul(ps[:, 6 + u % 2, :], ones64, sq2[:, u % 2], start=True, stop=True).then_inc(qn_mm, 1)
            pe.wait_ge(qn_done, 12)
            pe.wait_ge(z2_ev, 20)

            for i in range(len(AT_UNITS) + 2):
                if i < len(AT_UNITS):
                    h, q = AT_UNITS[i]
                    if i >= 2:
                        pe.wait_ge(at_e, i - 1)
                    for g in range(AT_G):
                        last = nc.tensor.matmul(ps[:, 2 * (i % 2) + g // 2, (g % 2) * SEQ:(g % 2 + 1) * SEQ],
                                                z2[half(h), 4 + 8 * g + h // 2, q * P:(q + 1) * P],
                                                z2[half(h), 8 + 8 * g + h // 2, :], start=(g != 1), stop=False,
                                                skip_group_check=True)
                    pe.wait_ge(ld_bias2[h % 2], 32 * (h // 2 + 1))
                    for g in range(0, AT_G, 2):
                        last = nc.tensor.matmul(ps[:, 2 * (i % 2) + g // 2, 0:(2 * SEQ if g == 0 else SEQ)], flip,
                                                bias2[:, h % 2, q, g:min(g + 2, AT_G)], start=False, stop=True,
                                                skip_group_check=True)
                    last.then_inc(at_s, 1)
                if 0 <= i - 1 < len(AT_UNITS):
                    u = i - 1
                    pe.wait_ge(at_p, u + 1)
                    if u:
                        pe.wait_ge(at_c, u)
                    for kt in range(6):
                        last = nc.tensor.transpose(ps[:, 4 + kt // 4, (kt % 4) * P:(kt % 4 + 1) * P],
                                                   probs2[:, u % 2, kt * P:(kt + 1) * P], ident)
                    last.then_inc(at_t, 1)
                if i >= 2:
                    u = i - 2
                    h, q = AT_UNITS[u]
                    pe.wait_ge(at_c, u + 1)
                    if u >= 2:
                        pe.wait_ge(at_ev, u - 1)
                    chain(ps[half(h), 6 + u % 2, 0:P],
                          [(v2[:, kt // 2, kt % 2, h * HD:(h + 1) * HD], probsT2[:, kt]) for kt in range(6)]).then_inc(at_o, 1)
            pe.wait_ge(at_ev, len(AT_UNITS))

            arrive(B_PA)
            w = slot(B_PA, "p (k m) -> p k m", k=4)
            for m in range(8):
                if m >= 4:
                    pe.wait_ge(ya_ev, m - 3)
                chain(ps[:, m % 4, 0:SEQ], [(w[:, k, m * P:(m + 1) * P], z2[:, k]) for k in range(4)]).then_inc(ya_mm, 1)
            release()
            for m in range(8):
                if m % 4 == 0:
                    arrive(B_PB + m // 4)
                    w = slot(B_PB + m // 4, "p (k m) -> p k m", k=KT)
                if m >= 2:
                    pe.wait_ge(yb_ev, m - 1)
                chain(ps[:, 4 + m % 2, 0:SEQ],
                      [(w[:, k, (m % 4) * P:(m % 4 + 1) * P], g_b[:, k]) for k in range(KT)]).then_inc(yb_mm, 1)
                if m % 4 == 3:
                    release()
            pe.wait_ge(yb_ev, KT)
            for m in range(8):
                if m % 4 == 0:
                    arrive(B_WO + m // 4)
                    w = slot(B_WO + m // 4, "p (k m) -> p k m", k=KT)
                if m >= 4:
                    pe.wait_ge(yo_ev, m - 3)
                chain(ps[:, m % 4, 0:SEQ],
                      [(w[:, k, (m % 4) * P:(m % 4 + 1) * P], zgA[:, k]) for k in range(KT)]).then_inc(yo_mm, 1)

        @block.scalar
        def _(act):
            def norm_in(i):
                a, b = NORM_COLS[i]
                if i == 0:
                    act.wait_ge(ld_h, 16)
                elif i < 5:
                    act.wait_ge(res_done, i)
                else:
                    act.wait_ge(nm_tmp, 5 * KT)
                for k in range(KT):
                    nc.scalar.activation(XT[:, k, a:b], hT[:, k, a:b], ACT.Square).then_inc(nm_sq, 1)
                act.wait_ge(nm_ms, i + 1)
                nc.scalar.activation(inv_rms[:, 0:b - a], ps[:, 7, 0:b - a], ACT.Sqrt, bias=eps_col, scale=1.0 / D).then_inc(nm_std, 1)

            def norm_out(i):
                a, b = NORM_COLS[i]
                act.wait_ge(mod_ready, i // 2 + 1)
                for k in range(KT):
                    act.wait_ge(nm_tmp, KT * i + k + 1)
                    for seg in range(a // SEQ, 2):
                        part = XT[:, k, seg * SEQ:(seg + 1) * SEQ]
                        last = nc.scalar.activation(part, part, ACT.Identity, scale=gains[:, i, k, seg:seg + 1],
                                                    bias=modc[:, i // 2, 24 * (i % 2) + k, seg:seg + 1])
                    last.then_inc(nm_x, 1)

            def router(layer):
                nt = 4 if layer == 0 else 2
                act.wait_ge(rt_mm, layer + 1)
                nc.scalar.activation(rt[:, 64:64 + 16 * nt], ps[:, 0, 0:16 * nt], ACT.Sigmoid).then_inc(rt_sig, 1)
                act.wait_ge(gT_mm, layer + 1)
                nc.scalar.activation(gateT[0:EXPERTS, 0:nt * P], ps[0:EXPERTS, 1, 0:nt * P], ACT.Copy).then_inc(gT_ev, 1)
                for e in range(EXPERTS):
                    act.wait_ge(gb_mm, EXPERTS * layer + e + 1)
                    nc.scalar.activation(Gt[:, e, 0:nt * P], ps[:, 2 + e % 4, 0:nt * P], ACT.Copy).then_inc(gb_ev, 1)

            def experts(layer):
                n = T if layer == 0 else SEQ
                with act.Fori(0, EXPERTS) as e:
                    for m in range(4):
                        act.wait_ge(up1, e * 4 + (4 * EXPERTS * layer + m + 1))
                        nc.scalar.activation(silu_b[:, m % 2, 0:n], ps[:, 2 * (m % 2), 0:n], ACT.Silu).then_inc(silu_rdy, 1)

            for r in range(ROWS):
                for kr in range(ROWS):
                    act.dma_start(bias_na[(r % 2) * GRID_W:(r % 2 + 1) * GRID_W, r // 2, :, kr * GRID_W:(kr + 1) * GRID_W],
                                  bass.AP(tensor=rpb.tensor,
                                          offset=(kr - r + NA_KH - 1) * RPB_W + NA_KW - GRID_W,
                                          ap=[[1, GRID_W], [RPB_HEAD, NA_H], [1, GRID_W]])).then_inc(ld_rpb, 16)
            act.wait_ge(ld_sm, 16)
            nc.scalar.activation(c2s[:, :], sm[:, SM["c2"]], ACT.Silu).then_inc(c2_ready, 1)
            act.wait_ge(tick_ready, 1)
            norm_in(0)
            norm_out(0)
            for u in range(22):
                act.wait_ge(mx_mm, u + 1)
                if u < 2:
                    dst = fnT[:, u, :]
                elif u < 14:
                    dst = qkT[:, u - 2, :]
                elif u < 18:
                    dst = Vt[:, u - 14, 0:256]
                else:
                    dst = Vt[:, u - 18, 256:768]
                nc.scalar.activation(dst, ps[:, u % 4, 0:(256 if 14 <= u < 18 else 512)], ACT.Copy).then_inc(mx_ev, 1)
            for n, (seg, f) in enumerate((s, f) for s in range(2) for f in range(2)):
                act.wait_ge(fn_mm, 2 * n + 1)
                nc.scalar.activation(acs[:, 0], ps[:, 4, :].rearrange("p (t c) -> p t c", t=2), ACT.Copy).then_inc(fn_ev, 1)
                act.wait_ge(fn_mm, 2 * n + 2)
                nc.scalar.activation(XT[:, f, seg * SEQ:(seg + 1) * SEQ], ps[:, 5, 0:SEQ], ACT.Copy).then_inc(fn_ev, 1)
            for i in range(len(NA_UNITS) + 2):
                if i < len(NA_UNITS):
                    nk = T if NA_UNITS[i][0] else SEQ
                    act.wait_ge(na_neg, i + 1)
                    if i >= 2:
                        act.wait_ge(na_t, i - 1)
                    nc.scalar.activation(probs0[:, i % 2, 0:nk], ps[:, i % 3, 0:nk], ACT.Exp, scale=0.125,
                                         bias=stat[:, 4 * i + 1:4 * i + 2], accum_out=stat[:, 4 * i + 2:4 * i + 3]).then_inc(na_e, 1)
                if 0 <= i - 1 < len(NA_UNITS):
                    u = i - 1
                    nk = T if NA_UNITS[u][0] else SEQ
                    act.wait_ge(na_t, u + 1)
                    if u >= 2:
                        act.wait_ge(na_o, u - 1)
                    nc.scalar.activation(probsT0[:, u % 2, 0:nk // P],
                                         ps[:, 3 + u % 2, 0:nk].rearrange("p (k q) -> p k q", q=P), ACT.Copy).then_inc(na_c, 1)
                if i >= 2:
                    u = i - 2
                    seg, h, q = NA_UNITS[u]
                    act.wait_ge(na_o, u + 1)
                    nc.scalar.activation(XT[half(h), 2 + h // 2, na_q(seg, q)], ps[half(h), 5 + u % 2, 0:P],
                                         ACT.Copy).then_inc(na_ev, 1)
            norm_in(1)
            norm_out(1)
            router(0)
            experts(0)

            norm_in(2)
            norm_out(2)
            nc.scalar.activation(dec_t[:, 0:8], sm[:, SM["decay"]], ACT.Exp).then_inc(lg_ready, 1)
            act.wait_ge(lg_ready, 2)
            nc.scalar.activation(dec_t[:, 16:24], dec_t[:, 8:16], ACT.Ln).then_inc(lg_ready, 1)
            for u in range(48):
                act.wait_ge(rp_mm, u + 1)
                b, m = u // 4, u % 4
                if b < 2:
                    dst, n = qR.rearrange("p h ab t -> p (h ab) t")[:, u], SEQ
                elif b < 4:
                    dst, n = kR.rearrange("p h ab t -> p (h ab) t")[:, u - 8], T
                elif b < 8:
                    dst, n = vR[:, m, (b - 4) * 512:(b - 3) * 512], T
                else:
                    dst, n = gR[:, u - 32], SEQ
                nc.scalar.activation(dst, ps[:, u % 4, 0:n], ACT.Silu if b >= 8 else ACT.Copy).then_inc(rp_ev, 1)

            def decays(h):
                act.wait_ge(dk_arg, h + 1)
                act.wait_ge(ld_cb, 16)
                lat = decayT[:, h % 2, 2:4].rearrange("p k t -> p (k t)")
                nc.scalar.activation(lat, lat, ACT.Exp)
                nc.scalar.activation(decayT[:, h % 2, 0:2].rearrange("p k t -> p (k t)"), cb[:, CB["ctx_f"]], ACT.Exp,
                                     scale=dec_t[:, 48 + h:49 + h])
                nc.scalar.activation(rope_t[:, h % 2, 0:2].rearrange("p k t -> p (k t)"), cb[:, CB["ctx_b"]], ACT.Exp,
                                     scale=dec_t[:, 52 + h:53 + h]).then_inc(dk_exp, 1)

            decays(0)
            for h in range(RET_H):
                if h + 1 < RET_H:
                    decays(h + 1)
                act.wait_ge(ro_mm, h + 1)
                if h:
                    act.wait_ge(rn_rdy, h)
                o = ps[:, 2:4, :].rearrange("p b (m t) -> p (b m) t", m=2)
                nc.scalar.activation(oR, o, ACT.Copy)
                nc.scalar.activation(sqR, o, ACT.Square).then_inc(ro_ev, 1)
                act.wait_ge(rn_mm, h + 1)
                nc.scalar.activation(irR, ps[:, 4, 0:SEQ], ACT.Sqrt, bias=eps_col, scale=1.0 / 512).then_inc(rn_std, 1)
            norm_in(3)
            norm_out(3)
            router(1)
            experts(1)

            norm_in(4)
            norm_in(5)
            act.wait_ge(lb_s, 1)
            nc.scalar.activation(lbt[:, 48:80], lbt[:, 16:48], ACT.Exp).then_inc(lb_e, 1)
            funcs = (ACT.Sigmoid, ACT.Sigmoid, ACT.Copy, ACT.Silu, ACT.Sigmoid, ACT.Sigmoid)
            for u in range(24):
                act.wait_ge(z1_mm, u + 1)
                nc.scalar.activation(z1m[:, 2 * u:2 * u + 2], ps[:, u % 6, :].rearrange("p (m t) -> p m t", m=2),
                                     funcs[u // 4]).then_inc(z1_ev, 1)
            for u in range(4):
                act.wait_ge(ib_mm, u + 1)
                nc.scalar.activation(ib[:, u % 2, (u // 2) * 512:(u // 2 + 1) * 512], ps[:, u, :], ACT.Copy).then_inc(ib_ev, 1)
            for d in range(2):
                act.wait_ge(f_rdy, d + 1)
                nc.scalar.activation(lf[:, d], zf[:, d], ACT.Ln).then_inc(lf_rdy, 1)
            for d in range(2):
                act.wait_ge(b_rdy, d + 1)
                nc.scalar.activation(lf[:, d], bc[:, d], ACT.Exp)
                nc.scalar.activation(bc[:, d], bc[:, d], ACT.Exp, scale=-1.0).then_inc(e_rdy, 1)
            for h in range(HG):
                act.wait_ge(ho_mm, h + 1)
                if h >= 2:
                    act.wait_ge(hg_done, h - 1)
                nc.scalar.activation(o_b[:, h % 2], ps[:, 4 + h % 2, 0:SEQ], ACT.Copy)
                nc.scalar.activation(sq_b[:, h % 2], ps[:, 4 + h % 2, 0:SEQ], ACT.Square).then_inc(ho_ev, 1)
                act.wait_ge(hn_mm, h + 1)
                nc.scalar.activation(ir_b[:, h % 2], ps[:, 6, 0:SEQ], ACT.Sqrt, bias=eps_col, scale=1.0 / P).then_inc(hn_std, 1)
            act.wait_ge(hg_done, HG)
            for u in range(20):
                act.wait_ge(z2_mm, u + 1)
                src = ps[:, u % 6, :]
                if u < 14:
                    nc.scalar.activation(z2[:, 2 * u:2 * u + 2], src.rearrange("p (m t) -> p m t", m=2),
                                         ACT.Silu if u < 2 else ACT.Copy).then_inc(z2_ev, 1)
                else:
                    nc.scalar.activation(v2[:, (u - 14) // 2, u % 2], src, ACT.Copy).then_inc(z2_ev, 1)
            for u in range(13):
                if u < 12:
                    if u >= 2:
                        act.wait_ge(qn_mm, u - 1)
                    nc.scalar.activation(sq2[:, u % 2].rearrange("p (m t) -> p m t", m=2), z2[:, 4 + 2 * u:6 + 2 * u],
                                         ACT.Square).then_inc(qn_sq, 1)
                if u:
                    act.wait_ge(qn_mm, u)
                    if u >= 3:
                        act.wait_ge(qn_done, u - 2)
                    nc.scalar.activation(ir2[:, (u - 1) % 2], ps[:, 6 + (u - 1) % 2, :], ACT.Sqrt, bias=eps_col,
                                         scale=1.0 / HD).then_inc(qn_std, 1)
            for i in range(len(AT_UNITS) + 1):
                if i < len(AT_UNITS):
                    act.wait_ge(at_neg, i + 1)
                    if i >= 2:
                        act.wait_ge(at_t, i - 1)
                    src = ps[:, 2 * (i % 2):2 * (i % 2) + 2, :].rearrange("p b k -> p (b k)")[:, 0:768]
                    nc.scalar.activation(probs2[:, i % 2], src, ACT.Exp, scale=0.125, bias=stat2[:, 4 * (i % 16) + 1:4 * (i % 16) + 2],
                                         accum_out=stat2[:, 4 * (i % 16) + 2:4 * (i % 16) + 3]).then_inc(at_e, 1)
                if i:
                    u = i - 1
                    act.wait_ge(at_t, u + 1)
                    if u:
                        act.wait_ge(at_o, u)
                    src = ps[:, 4:6, :].rearrange("p b k -> p (b k)")[:, 0:768].rearrange("p (k q) -> p k q", q=P)
                    nc.scalar.activation(probsT2, src, ACT.Copy).then_inc(at_c, 1)

        @block.vector
        def _(dve):
            steps = [0]

            def link(ins):
                steps[0] += 1
                ins.then_inc(dve_step, 1)
                dve.wait_ge(dve_step, steps[0])

            def norm(i):
                a, b = NORM_COLS[i]
                r = inv_rms[:, 0:b - a]
                dve.wait_ge(nm_std, i + 1)
                link(nc.vector.reciprocal(r, r))
                for k in range(KT):
                    if i < 4:
                        nc.vector.tensor_tensor(XT[:, k, a:b], hT[:, k, a:b], r, ALU.mult).then_inc(nm_tmp, 1)
                    else:
                        g = sm[:, SM["final_g" if i == 4 else "norm_w2"]][:, k:k + 1]
                        nc.vector.scalar_tensor_tensor((hT if i == 4 else XT)[:, k, a:b], hT[:, k, a:b], g, r,
                                                       ALU.mult, ALU.mult).then_inc(nm_tmp, 1)

            def rank(src, out, q):
                bj = src.unsqueeze(2).broadcast_to([P, q, 4, 4])
                bi = src.unsqueeze(3).broadcast_to([P, q, 4, 4])
                gt = rt[:, 192:192 + 16 * q].rearrange("p (q i j) -> p q i j", q=q, i=4)
                eq = rt[:, 448:448 + 16 * q].rearrange("p (q i j) -> p q i j", q=q, i=4)
                tie = cst[:, CST["tie"]].unsqueeze(1).broadcast_to([P, q, 16])
                nc.vector.tensor_tensor(gt, bj, bi, ALU.is_gt)
                link(nc.vector.tensor_tensor(eq, bj, bi, ALU.is_equal))
                eqf = rt[:, 448:448 + 16 * q].rearrange("p (q x) -> p q x", q=q)
                link(nc.vector.tensor_tensor(eqf, eqf, tie, ALU.mult))
                link(nc.vector.tensor_tensor(eqf, eqf, rt[:, 192:192 + 16 * q].rearrange("p (q x) -> p q x", q=q), ALU.add))
                link(nc.vector.tensor_reduce(out, eq, AX.X, ALU.add))

            def router(layer):
                nt = 4 if layer == 0 else 2
                q = 4 * nt
                scores = rt[:, 64:64 + 16 * nt]
                biased = rt[:, 128:128 + 16 * nt]
                rk = rt[:, 704:704 + 4 * q]
                gs, grk, den = rt[:, 768:768 + q], rt[:, 800:800 + q], rt[:, 832:832 + nt]
                val = rt[:, 896:896 + 4 * q]
                v3 = lambda x: x.rearrange("p (q j) -> p q j", j=4)
                dve.wait_ge(rt_sig, layer + 1)
                link(nc.vector.tensor_tensor(biased.rearrange("p (t e) -> p t e", t=nt), scores.rearrange("p (t e) -> p t e", t=nt),
                                             sm[:, SM["router_b"]].unsqueeze(1).broadcast_to([P, nt, 16]), ALU.add))
                rank(v3(biased), v3(rk), q)
                link(nc.vector.tensor_scalar(rk, rk, 1.5, None, ALU.is_lt))
                link(nc.vector.tensor_tensor(val, rk, biased, ALU.mult))
                link(nc.vector.tensor_reduce(gs, v3(val), AX.X, ALU.add))
                rank(v3(gs), v3(grk), nt)
                link(nc.vector.tensor_scalar(grk, grk, 0.5, None, ALU.is_lt))
                link(nc.vector.tensor_tensor(v3(rk), v3(rk), grk.unsqueeze(2).broadcast_to([P, q, 4]), ALU.mult))
                link(nc.vector.tensor_tensor(val, rk, scores, ALU.mult))
                link(nc.vector.tensor_reduce(den, val.rearrange("p (t e) -> p t e", t=nt), AX.X, ALU.add))
                link(nc.vector.reciprocal(den, den))
                nc.vector.tensor_tensor(rt[:, 0:16 * nt].rearrange("p (t e) -> p t e", t=nt), val.rearrange("p (t e) -> p t e", t=nt),
                                        den.unsqueeze(2).broadcast_to([P, nt, 16]), ALU.mult).then_inc(gate_ready, 1)

            def experts(layer):
                t0, n = (0, T) if layer == 0 else (SEQ, SEQ)
                u0, d0 = 4 * EXPERTS * layer, 8 * EXPERTS * layer
                dc = (8 * EXPERTS + 2) * layer + 2
                for k in range(KT):
                    last = nc.vector.memset(acc[:, k, 0:n], 0.0)
                link(last)
                dve.wait_ge(gb_ev, EXPERTS * (layer + 1))
                with dve.Fori(0, EXPERTS) as e:
                    for m in range(4):
                        dve.wait_ge(up3, e * 4 + (u0 + m + 1))
                        nc.vector.tensor_tensor(gated[:, m % 2, 0:n], ps[:, 2 * (m % 2) + 1, 0:n],
                                                Gt[:, bass.ds(e, 1), 0:n].rearrange("p e t -> p (e t)"), ALU.mult).then_inc(gated_rdy, 1)
                        dve.wait_ge(gated_rdy, e * 4 + (u0 + m + 1))
                        dve.wait_ge(silu_rdy, e * 4 + (u0 + m + 1))
                        nc.vector.tensor_tensor(hid[:, m, 0:n], gated[:, m % 2, 0:n], silu_b[:, m % 2, 0:n],
                                                ALU.mult).then_inc(hid_rdy, 1)
                    for m in range(8):
                        dve.wait_ge(dn_mm, e * 8 + (d0 + m + 1))
                        nc.vector.tensor_tensor(acc[:, m, 0:n], acc[:, m, 0:n], ps[:, 4 + m % 2, 0:n], ALU.add).then_inc(dn_free, 1)
                dve.wait_ge(dn_free, dc + 8 * EXPERTS)
                for m in range(KT):
                    for seg in range(t0 // SEQ, 2):
                        part = hT[:, m, seg * SEQ:(seg + 1) * SEQ]
                        last = nc.vector.scalar_tensor_tensor(part, acc[:, m, seg * SEQ - t0:(seg + 1) * SEQ - t0],
                                                              modc[:, layer, 40 + m, seg:seg + 1], part, ALU.mult, ALU.add)
                last.then_inc(res_done, 1)

            nc.vector.memset(tick[:, :], 0.0)
            nc.vector.memset(eps_col, EPS).then_inc(tick_ready, 1)
            dve.wait_ge(ld_ca, 16)
            dve.wait_ge(ld_rpb, 16 * ROWS * ROWS)
            for q in range(2):
                b = bias_na[:, q].rearrange("p h (r c) -> p (h r) c", c=GRID_W)
                shape = [P, NA_H * ROWS, GRID_W]
                link(nc.vector.tensor_tensor(b, b, ca[:, CA["keep8"]].unsqueeze(1).broadcast_to(shape), ALU.mult))
                last = nc.vector.tensor_tensor(b, b, ca[:, CA["shut8"]].unsqueeze(1).broadcast_to(shape), ALU.add)
            last.then_inc(bias_ready, 1)
            dve.wait_ge(ld_sm, 16)
            for layer in range(2):
                dve.wait_ge(w_free, 12 * (layer + 1))
                link(nc.vector.tensor_tensor(
                    modc[:, layer], ps[:, layer, 0:96].rearrange("p (m s) -> p m s", s=2),
                    sm[:, SM["ada_b"]][:, 48 * layer:48 * (layer + 1)].unsqueeze(2).broadcast_to([P, 48, 2]), ALU.add))
                for j in range(2):
                    n = 2 * layer + j
                    last = nc.vector.scalar_tensor_tensor(
                        gains[:, n], modc[:, layer, 24 * j + 8:24 * j + 16], 1.0,
                        sm[:, SM["norm_g"]][:, KT * n:KT * (n + 1)].unsqueeze(2).broadcast_to([P, KT, 2]), ALU.add, ALU.mult)
                last.then_inc(mod_ready, 1)
            dve.wait_ge(ld_h, 16)
            norm(0)

            for i in range(len(NA_UNITS) + 1):
                if i < len(NA_UNITS):
                    seg, h, q = NA_UNITS[i]
                    s = ps[:, i % 3, 0:(T if seg else SEQ)]
                    dve.wait_ge(na_s, i + 1)
                    link(nc.vector.tensor_reduce(stat[:, 4 * i:4 * i + 1], s, AX.X, ALU.max))
                    nc.vector.tensor_scalar(stat[:, 4 * i + 1:4 * i + 2], stat[:, 4 * i:4 * i + 1], -0.125, None,
                                            ALU.mult).then_inc(na_neg, 1)
                if i:
                    u = i - 1
                    nk = T if NA_UNITS[u][0] else SEQ
                    dve.wait_ge(na_e, u + 1)
                    link(nc.vector.reciprocal(stat[:, 4 * u + 3:4 * u + 4], stat[:, 4 * u + 2:4 * u + 3]))
                    nc.vector.tensor_scalar(probs0[:, u % 2, 0:nk], probs0[:, u % 2, 0:nk], stat[:, 4 * u + 3:4 * u + 4],
                                            None, ALU.mult).then_inc(na_p, 1)
            for m in range(8):
                dve.wait_ge(mo_mm, m + 1)
                for seg in range(2):
                    part = hT[:, m, seg * SEQ:(seg + 1) * SEQ]
                    last = nc.vector.scalar_tensor_tensor(part, ps[:, m % 4, seg * SEQ:(seg + 1) * SEQ],
                                                          modc[:, 0, 16 + m, seg:seg + 1], part, ALU.mult, ALU.add)
                last.then_inc(mo_ev if m < 7 else res_done, 1)
            norm(1)
            router(0)
            experts(0)

            norm(2)
            dve.wait_ge(lg_ready, 1)
            nc.vector.tensor_scalar(dec_t[:, 8:16], dec_t[:, 0:8], -1.0, 1.0, ALU.mult, ALU.add).then_inc(lg_ready, 1)
            dve.wait_ge(lg_ready, 3)
            link(nc.vector.tensor_scalar(dec_t[:, 24:32], dec_t[:, 8:16], -1.0, 1.0, ALU.mult, ALU.add))
            link(nc.vector.tensor_scalar(dec_t[:, 24:32], dec_t[:, 24:32], 1e-30, None, ALU.max))
            link(nc.vector.reciprocal(dec_t[:, 32:40], dec_t[:, 24:32]))
            link(nc.vector.tensor_tensor(dec_t[:, 40:48], dec_t[:, 32:40], dec_t[:, 0:8], ALU.mult))
            link(nc.vector.tensor_tensor(dec_t[:, 48:56], dec_t[:, 40:48], dec_t[:, 16:24], ALU.mult))
            dve.wait_ge(ld_cb, 16)
            cos = cb[:, CB["rcos"]].unsqueeze(1).broadcast_to([P, 4, SEQ])
            sin = cb[:, CB["rsin"]].unsqueeze(1).broadcast_to([P, 4, SEQ])
            for n, (x, units) in enumerate(((qR, 8), (kR[:, :, :, LAT], 16))):
                dve.wait_ge(rp_ev, units)
                x1, x2 = x[:, :, 0], x[:, :, 1]
                nc.vector.tensor_tensor(rope_t[:, 0], x2, sin, ALU.mult)
                link(nc.vector.tensor_tensor(rope_t[:, 1], x1, sin, ALU.mult))
                nc.vector.tensor_tensor(x1, x1, cos, ALU.mult)
                link(nc.vector.tensor_tensor(x2, x2, cos, ALU.mult))
                nc.vector.tensor_tensor(x1, x1, rope_t[:, 0], ALU.subtract)
                nc.vector.tensor_tensor(x2, x2, rope_t[:, 1], ALU.add).then_inc(rope_done, 1)
                dve.wait_ge(rope_done, n + 1)

            def decay_arg(h):
                lat = decayT[:, h % 2, 2:4].rearrange("p k t -> p (k t)")
                link(nc.vector.tensor_scalar(lat, cb[:, CB["lat_f"]], dec_t[:, 48 + h:49 + h], None, ALU.mult))
                nc.vector.scalar_tensor_tensor(lat, cb[:, CB["lat_b"]], dec_t[:, 52 + h:53 + h], lat, ALU.mult,
                                               ALU.add).then_inc(dk_arg, 1)

            decay_arg(0)
            for h in range(RET_H):
                if h + 1 < RET_H:
                    decay_arg(h + 1)
                dve.wait_ge(dk_exp, h + 1)
                ctxd = decayT[:, h % 2, 0:2].rearrange("p k t -> p (k t)")
                latd = decayT[:, h % 2, 2:4].rearrange("p k t -> p (k t)")
                nc.vector.tensor_tensor(ctxd, ctxd, rope_t[:, h % 2, 0:2].rearrange("p k t -> p (k t)"), ALU.add)
                link(nc.vector.tensor_tensor(latd, latd, cb[:, CB["twice"]], ALU.mult))
                dve.wait_ge(rs_mm, h + 1)
                if h >= 2:
                    dve.wait_ge(ro_mm, h - 1)
                for j in range(2):
                    nc.vector.scalar_tensor_tensor(
                        scoreT[:, h % 2, 2 * j:2 * j + 2].rearrange("p k t -> p (k t)"), ps[:, j, :], 0.0625,
                        (ctxd, latd)[j], ALU.mult, ALU.mult).then_inc(rs_rdy, 1)
                dve.wait_ge(rn_std, h + 1)
                link(nc.vector.reciprocal(irR, irR))
                g = gR[:, 4 * h:4 * h + 4]
                link(nc.vector.tensor_tensor(g, g, irR.unsqueeze(1).broadcast_to([P, 4, SEQ]), ALU.mult))
                nc.vector.tensor_tensor(g, g, oR, ALU.mult).then_inc(rn_rdy, 1)
            for m in range(8):
                dve.wait_ge(y_mm, m + 1)
                nc.vector.scalar_tensor_tensor(hT[:, m, LAT], ps[:, m % 4, 0:SEQ], modc[:, 1, 16 + m, 1:2], hT[:, m, LAT],
                                               ALU.mult, ALU.add).then_inc(y_ev if m < 7 else res_done, 1)
            norm(3)
            router(1)
            experts(1)

            norm(4)
            dve.wait_ge(nm_tmp, 5 * KT)
            norm(5)
            a = sm[:, SM["lb"]].rearrange("p (d l h) -> p l d h", d=2, l=2)
            v16 = lambda at: lbt[:, at:at + 16].rearrange("p (d h) -> p d h", d=2)
            link(nc.vector.tensor_tensor(v16(0), a[:, 0], a[:, 1], ALU.max))
            nc.vector.tensor_tensor(v16(16), a[:, 0], v16(0), ALU.subtract)
            nc.vector.tensor_tensor(v16(32), a[:, 1], v16(0), ALU.subtract).then_inc(lb_s, 1)
            dve.wait_ge(lb_e, 1)
            link(nc.vector.tensor_tensor(v16(80), v16(48), v16(64), ALU.add))
            link(nc.vector.reciprocal(v16(96), v16(80)))
            link(nc.vector.tensor_tensor(v16(112), v16(48), v16(96), ALU.mult))
            link(nc.vector.tensor_scalar(tiny[:, 0:16], lbt[:, 112:128], -1.0, 1.0, ALU.mult, ALU.add))
            for d in range(2):
                dve.wait_ge(z1_ev, 6 + 4 * (d + 1))
                for h in range(HG):
                    at = 8 * d + h
                    last = nc.vector.tensor_scalar(zf[:, d, h], zf[:, d, h], tiny[:, at:at + 1], lbt[:, 112 + at:113 + at],
                                                   ALU.mult, ALU.add)
                last.then_inc(f_rdy, 1)
            dve.wait_ge(ld_cc, 16)
            link(nc.vector.memset(toep, 0.0))
            dve.wait_ge(tz_mm, 1)
            nc.vector.scalar_tensor_tensor(toep[0:24, 0:511], ps[0:24, 6, 0:511], 8.0, cc[0:24, CC["shut8"]],
                                           ALU.mult, ALU.add).then_inc(tz_rdy, 1)
            for d in range(2):
                dve.wait_ge(lf_rdy, d + 1)
                flat = zf[:, d].rearrange("p h t -> p (h t)")
                nc.vector.tensor_scalar(flat, flat, -1.0, 1.0, ALU.mult, ALU.add)
                step = 1 if d == 0 else -1
                for h in range(HG):
                    last = nc.vector.tensor_tensor_scan(bc[:, d, h, ::step], cc[:, CC["runs"]], lf[:, d, h, ::step], 0.0,
                                                        ALU.mult, ALU.add)
                last.then_inc(b_rdy, 1)
            for d in range(2):
                dve.wait_ge(e_rdy, d + 1)
                dve.wait_ge(z1_ev, 6 + 12)
                end = CH - 1 if d == 0 else 0
                link(nc.vector.tensor_copy(decs[:, d], lf[:, d].rearrange("p h (c t) -> p h c t", t=CH)[:, :, :, end]))
                nc.vector.tensor_tensor(lf[:, d], lf[:, d], q_b, ALU.mult)
                link(nc.vector.tensor_tensor(bc[:, d], bc[:, d], zf[:, d], ALU.mult))
                link(nc.vector.memset(zf[:, d], 0.0))

            def gla_keys(h):
                for d in range(2):
                    if h:
                        dve.wait_ge(K_used, 2 * (h - 1) + d + 1)
                    K = zf[:, d]
                    diag = bass.AP(tensor=arena, offset=d * 2048, ap=[[30400, P], [SEQ + CH, NCH], [1, CH]])
                    link(nc.vector.tensor_copy(diag, bc[:, d, h].rearrange("p (c t) -> p c t", t=CH)))
                    for c in range(1, NCH):
                        if d == 0:
                            to, of = K[:, c, 0:CH * c], K[:, c - 1, 0:CH * c]
                            dec = decs[:, d, h, c - 1:c]
                        else:
                            to, of = K[:, NCH - 1 - c, CH * (NCH - c):SEQ], K[:, NCH - c, CH * (NCH - c):SEQ]
                            dec = decs[:, d, h, NCH - c:NCH - c + 1]
                        ins = nc.vector.tensor_scalar(to, of, dec, None, ALU.mult)
                        if c < NCH - 1:
                            link(ins)
                        else:
                            ins.then_inc(K_rdy, 1)

            gla_keys(0)
            for h in range(HG):
                if h + 1 < HG:
                    gla_keys(h + 1)
                dve.wait_ge(K_used, 2 * h + 2)
                if h >= 2:
                    dve.wait_ge(ho_mm, h - 1)
                F, B = ps[:, 2 * (h % 2)], ps[:, 2 * (h % 2) + 1]
                pt = pt_b[:, h % 2]
                nc.vector.tensor_tensor(mrg[:, 0:P], F[:, 0:P], cc[:, CC["mask_f"]], ALU.mult)
                nc.vector.tensor_tensor(mrg[:, P:2 * P], F[:, SEQ:SEQ + P], cc[:, CC["mask_f"]], ALU.mult)
                nc.vector.tensor_tensor(pt[:, 0, 0:P], B[:, SEQ:SEQ + P], cc[:, CC["mask_b"]], ALU.mult)
                nc.vector.tensor_tensor(pt[:, 1, P:SEQ], B[:, P:SEQ], cc[:, CC["mask_b"]], ALU.mult)
                nc.vector.tensor_copy(pt[:, 0, P:SEQ], F[:, P:SEQ])
                link(nc.vector.tensor_copy(pt[:, 1, 0:P], B[:, 0:P]))
                nc.vector.tensor_tensor(pt[:, 0, 0:P], pt[:, 0, 0:P], mrg[:, 0:P], ALU.add)
                nc.vector.tensor_tensor(pt[:, 1, P:SEQ], pt[:, 1, P:SEQ], mrg[:, P:2 * P], ALU.add).then_inc(pt_rdy, 1)
                dve.wait_ge(hn_std, h + 1)
                r = ir_b[:, h % 2]
                link(nc.vector.reciprocal(r, r))
                link(nc.vector.scalar_tensor_tensor(o_b[:, h % 2], o_b[:, h % 2], sm[:, SM["hgw"]], r, ALU.mult, ALU.mult))
                nc.vector.tensor_tensor(g_b[:, h], g_b[:, h], o_b[:, h % 2], ALU.mult).then_inc(hg_done, 1)

            for u in range(12):
                dve.wait_ge(qn_std, u + 1)
                r = ir2[:, u % 2]
                link(nc.vector.reciprocal(r, r))
                w = sm[:, SM["qn" if u % 4 < 2 else "kn"]][:, u // 4:u // 4 + 1]
                z = z2[:, 4 + 2 * u:6 + 2 * u]
                nc.vector.scalar_tensor_tensor(z, z, w, r.rearrange("p (m t) -> p m t", m=2), ALU.mult, ALU.mult).then_inc(qn_done, 1)
            for i in range(len(AT_UNITS) + 2):
                if i < len(AT_UNITS):
                    h, q = AT_UNITS[i]
                    s = ps[:, 2 * (i % 2):2 * (i % 2) + 2, :].rearrange("p b k -> p (b k)")[:, 0:768]
                    dve.wait_ge(at_s, i + 1)
                    link(nc.vector.tensor_reduce(stat2[:, 4 * i:4 * i + 1], s, AX.X, ALU.max))
                    nc.vector.tensor_scalar(stat2[:, 4 * i + 1:4 * i + 2], stat2[:, 4 * i:4 * i + 1], -0.125, None,
                                            ALU.mult).then_inc(at_neg, 1)
                if 0 <= i - 1 < len(AT_UNITS):
                    u = i - 1
                    dve.wait_ge(at_e, u + 1)
                    link(nc.vector.reciprocal(stat2[:, 4 * u + 3:4 * u + 4], stat2[:, 4 * u + 2:4 * u + 3]))
                    nc.vector.tensor_scalar(probs2[:, u % 2], probs2[:, u % 2], stat2[:, 4 * u + 3:4 * u + 4], None,
                                            ALU.mult).then_inc(at_p, 1)
                if i >= 2:
                    u = i - 2
                    h, q = AT_UNITS[u]
                    dve.wait_ge(at_o, u + 1)
                    part = z2[half(h), h // 2, q * P:(q + 1) * P]
                    nc.vector.tensor_tensor(part, part, ps[half(h), 6 + u % 2, 0:P], ALU.mult).then_inc(at_ev, 1)
            for m in range(8):
                dve.wait_ge(ya_mm, m + 1)
                nc.vector.tensor_tensor(zgA[:, m], zgA[:, m], ps[:, m % 4, 0:SEQ], ALU.mult).then_inc(ya_ev, 1)
            dve.wait_ge(ya_ev, KT)
            for m in range(8):
                dve.wait_ge(yb_mm, m + 1)
                link(nc.vector.tensor_tensor(zgB[:, m], zgB[:, m], ps[:, 4 + m % 2, 0:SEQ], ALU.mult))
                nc.vector.tensor_tensor(zgA[:, m], zgA[:, m], zgB[:, m], ALU.add).then_inc(yb_ev, 1)
            for m in range(8):
                dve.wait_ge(yo_mm, m + 1)
                nc.vector.tensor_tensor(XT[:, m, LAT], hT[:, m, LAT], ps[:, m % 4, 0:SEQ], ALU.add).then_inc(yo_ev, 1)


def columns_of(v):
    return np.ascontiguousarray(v.reshape(-1, P).T)


def weight_blocks(w, rows, cols):
    k, m = w.shape
    b = w.reshape(k // rows, rows // P, P, m // cols, cols)
    return b.transpose(0, 3, 2, 1, 4).reshape(-1, P, rows // P * cols)


def kernel(**inputs):
    import concourse.bacc as bacc
    from concourse.bass_utils import run_bass_kernel_spmd as run

    a = {k: np.asarray(v) for k, v in inputs.items()}
    blocks = []
    for layer in range(2):
        blocks.append(weight_blocks(a["ada_w"][layer], D, 512))
    blocks.append(weight_blocks(a["mixab_w_in"][0], D, 512))
    blocks.append(weight_blocks(a["mixab_w_out"][0], D, 512))

    def expert_blocks(layer):
        w1 = a["moe_w1"][layer].reshape(EXPERTS, KT, P, 512).transpose(0, 2, 1, 3).reshape(EXPERTS, P, BLK)
        w3 = a["moe_w3"][layer].reshape(EXPERTS, KT, P, 512).transpose(0, 2, 1, 3).reshape(EXPERTS, P, BLK)
        w2 = a["moe_w2"][layer].reshape(EXPERTS, 4, P, D).transpose(0, 2, 1, 3).reshape(EXPERTS, P, BLK)
        return np.stack([w1, w3, w2], 1).reshape(3 * EXPERTS, P, BLK)

    blocks.append(expert_blocks(0))
    rw = a["ret_w_in"][0]
    qk = rw[:, :2048].reshape(D, 8, 2, 2, 64).transpose(0, 1, 3, 2, 4).reshape(D, 2048)
    blocks.append(weight_blocks(qk, D, 512))
    blocks.append(weight_blocks(rw[:, 2048:], D, 512))
    blocks.append(weight_blocks(a["ret_w_out"][0], 2048, 256))
    blocks.append(expert_blocks(1))
    w2 = weight_blocks(a["w_in_2"][0], D, 512)
    order = [12, 13, 14, 15, 10, 11, 18, 19, 20, 21, 22, 23, 16, 17, 9, 0, 1, 3, 4, 6, 7, 2, 5, 8]
    blocks.append(w2[order])
    blocks.append(weight_blocks(a["w_proj_a_2"][0], 512, D))
    blocks.append(weight_blocks(a["w_proj_b_2"][0], D, 512))
    blocks.append(weight_blocks(a["w_out_2"][0], D, 512))
    w_all = np.concatenate(blocks)

    h0 = np.concatenate([a["ctx"][0], a["x"][0]]).T.reshape(KT, P, T).transpose(1, 0, 2)
    rows = lambda v: np.broadcast_to(v.reshape(1, -1), (P, v.size))
    c2 = np.stack([columns_of(a["c_ctx"]), columns_of(a["c"][0])], -1).reshape(P, 2 * KT)
    rel = np.zeros((P, 24), a["rel_bias_2"].dtype)
    rel[:BUCKETS] = a["rel_bias_2"]
    lb = np.concatenate([columns_of(a[n][r]) for n in ("lb_fwd_2", "lb_bwd_2") for r in range(2)], 1)
    smalls = np.concatenate([
        c2, columns_of(a["ada_b"].reshape(-1)), columns_of(a["norm_g"].reshape(-1)), columns_of(a["final_norm_g"]),
        columns_of(a["norm_w_2"].reshape(-1)),
        a["router_w"].reshape(KT, P, 16).transpose(1, 0, 2).reshape(P, KT * 16), rows(a["router_b"]),
        rows(a["ret_decay"]), np.tile(a["q_norm_w_2"][0].T, (2, 1)), np.tile(a["k_norm_w_2"][0].T, (2, 1)), lb,
        a["hg_norm_w_2"].reshape(P, 1), rel], 1)
    assert w_all.shape[0] == N_BLK and smalls.shape[1] == SM_N

    arrays = {"w_all": w_all, "h0": h0, "smalls": smalls, "rpb": a["na_rpb"][0]}
    arrays.update({k + "_d": v for k, v in constants().items()})
    arrays = {k: np.ascontiguousarray(v) for k, v in arrays.items()}
    nc = bacc.Bacc("TRN2", target_bir_lowering=False, num_devices=1)
    args = {k: nc.dram_tensor(k, v.shape, F32, kind="ExternalInput").ap() for k, v in arrays.items()}
    args["toep_d"] = nc.dram_tensor("toep_d", (24, 512), F32, kind="Internal").ap()
    args["out_d"] = nc.dram_tensor("out_d", (P, KT, SEQ), F32, kind="ExternalOutput").ap()
    build(nc, **args)
    r = run(nc, [arrays], core_ids=[0])
    return r.results[0]["out_d"].transpose(1, 0, 2).reshape(D, SEQ).T[None]
```

```python
from contextlib import ExitStack

import numpy as np
import concourse.bass as bass
from concourse import mybir

F32 = mybir.dt.float32
BF16 = mybir.dt.bfloat16
I32 = mybir.dt.int32
U32 = mybir.dt.uint32
ALU = mybir.AluOpType
ACT = mybir.ActivationFunctionType
AX = mybir.AxisListType

P = 128
D = 1024
KT = D // P
SEQ = 256
T = 2 * SEQ
CTX, LAT = slice(0, SEQ), slice(SEQ, T)
SLOTS = 3
BLK = 4096
BIG = 1e30
EPS = 1e-6

GRID_W = 64
ROWS = SEQ // GRID_W
NA_H = 12
NA_KH, NA_KW = 8, 16
RPB_W = 2 * NA_KW - 1
RPB_HEAD = (2 * NA_KH - 1) * RPB_W
HD = 64

RET_H = 4
EXPERTS = 16

AT_H = 8
AT_G = 3
GROUPS = ((128, 1), (512, 4), (2048, 16))
BUCKETS = 32
HG = 8
CH = 32
NCH = SEQ // CH

B_ADA = 0
B_MIX = B_ADA + 24
B_MIXO = B_MIX + 5
B_MOE0 = B_MIXO + 2
B_RET = B_MOE0 + 48
B_RETO = B_RET + 12
B_MOE1 = B_RETO + 4
B_Z1 = B_MOE1 + 48
B_IB = B_Z1 + 12
B_Z2 = B_IB + 2
B_V2 = B_Z2 + 7
B_PA = B_V2 + 3
B_PB = B_PA + 1
B_WO = B_PB + 2
N_BLK = B_WO + 2



def columns(*parts):
    at, out = 0, {}
    for name, n in parts:
        out[name] = slice(at, at + n)
        at += n
    return out, at


CST, CST_N = columns(("ident", P), ("ones", P), ("ones64", P), ("flip", P), ("flip64", P), ("tri", P), ("iota", P), ("tie", 16), ("tok", 8), ("row1", 16))
CA, CA_N = columns(("dft64", 2 * P), ("cos", 2 * SEQ), ("msin", 2 * SEQ), ("keep8", GRID_W), ("shut8", GRID_W))
CB, CB_N = columns(("rcos", SEQ), ("rsin", SEQ), ("ctx_f", 2 * SEQ), ("ctx_b", 2 * SEQ), ("lat_f", 2 * SEQ),
                   ("lat_b", 2 * SEQ), ("twice", 2 * SEQ))
CC, CC_N = columns(("runs", SEQ), ("mask_f", P), ("mask_b", P), ("onehot", 511), ("shut8", 511))
SM, SM_N = columns(("c2", 2 * KT), ("ada_b", 96), ("norm_g", 4 * KT), ("final_g", KT), ("norm_w2", KT),
                   ("router_w", KT * 16), ("router_b", 16), ("decay", 8), ("qn", 3), ("kn", 3), ("lb", 32),
                   ("hgw", 1), ("rel_bias", 24))


def t5_bucket(rel):
    half = BUCKETS // 2
    exact = half // 2
    n = np.abs(rel)
    large = exact + (np.log(np.maximum(n, 1) / exact) / np.log(1024 / exact) * (half - exact)).astype(np.int32)
    return np.where(rel > 0, half, 0) + np.where(n < exact, n, np.minimum(large, half - 1))


def constants():
    f = np.float32
    i128 = np.arange(P)
    cst = np.zeros((P, CST_N), f)
    cst[:, CST["ident"]] = np.eye(P)
    cst[:, CST["ones"]] = 1
    same64 = i128[:, None] // HD == i128[None] // HD
    cst[:, CST["ones64"]] = same64
    cst[:, CST["flip"]] = np.eye(P)[::-1]
    cst[:, CST["flip64"]] = same64 * (i128[:, None] % HD + i128[None] % HD == HD - 1)
    cst[:, CST["tri"]] = i128[:, None] < i128[None]
    cst[:, CST["iota"]] = i128[None]
    cst[:, CST["tok"]] = np.stack([np.tile(i128[:, None], (1, 4)), np.tile(np.arange(4)[None], (P, 1))], -1).reshape(P, 8)
    cst[:, CST["row1"]] = P * np.arange(EXPERTS)[None] + 1
    cst[:, CST["tie"]] = (np.arange(4)[None, :] < np.arange(4)[:, None]).reshape(1, 16)

    ca = np.zeros((P, CA_N), f)
    w64 = 2 * np.pi * np.outer(np.arange(64), np.arange(64)) / 64
    same = (i128[:, None] // 64 == i128[None] // 64)
    ca[:, CA["dft64"]] = np.concatenate([np.tile(np.cos(w64), (2, 2)) * same, np.tile(np.sin(w64), (2, 2)) * same], 1)
    w256 = 2 * np.pi * (np.outer(np.arange(256), np.arange(256)) % 256) / 256
    tiles = lambda m: m.reshape(2, P, SEQ).transpose(1, 0, 2).reshape(P, 2 * SEQ)
    ca[:, CA["cos"]] = tiles(np.cos(w256) / 128)
    ca[:, CA["msin"]] = tiles(-np.sin(w256) / 128)
    qc = (GRID_W - 1 - i128 % GRID_W)[:, None]
    kc = np.arange(GRID_W)[None]
    ws = np.clip(qc - NA_KW // 2, 0, GRID_W - NA_KW)
    inside = (kc >= ws) & (kc < ws + NA_KW)
    ca[:, CA["keep8"]] = inside * 8.0
    ca[:, CA["shut8"]] = np.where(inside, 0.0, -8.0 * BIG)

    cb = np.zeros((P, CB_N), f)
    t = np.arange(SEQ)
    inv = f(10000.0) ** (-np.arange(64, dtype=f) / f(64))
    ang = np.concatenate([inv[:, None] * (t // GRID_W).astype(f)[None], inv[:, None] * (t % GRID_W).astype(f)[None]], 0)
    cb[:, CB["rcos"]] = np.cos(ang.astype(f))
    cb[:, CB["rsin"]] = np.sin(ang.astype(f))
    m, n = np.arange(SEQ)[:, None], np.arange(SEQ)[None]
    cb[:, CB["ctx_f"]] = tiles(SEQ + n - m)
    cb[:, CB["ctx_b"]] = tiles(SEQ - n + m)
    cb[:, CB["lat_f"]] = tiles(np.maximum(n - m, 0))
    cb[:, CB["lat_b"]] = tiles(np.maximum(m - n, 0))
    cb[:, CB["twice"]] = tiles(1.0 + (m == n))

    cc = np.zeros((P, CC_N), f)
    cc[:, CC["runs"]] = (t % CH != 0)
    chunk = i128[:, None] // CH == i128[None] // CH
    cc[:, CC["mask_f"]] = (chunk & (i128[:, None] <= i128[None])) | (i128[:, None] // CH < i128[None] // CH)
    cc[:, CC["mask_b"]] = (chunk & (i128[:, None] >= i128[None])) | (i128[:, None] // CH > i128[None] // CH)
    delta = np.arange(-255, 256)
    for g, (window, dil) in enumerate(GROUPS):
        cc[g * AT_H:(g + 1) * AT_H, CC["shut8"]] = np.where(
            (delta % dil == 0) & (np.abs(delta) <= (window // 2) // dil * dil), 0.0, -8.0 * BIG)
    cc[:BUCKETS, CC["onehot"]] = t5_bucket(delta)[None] == np.arange(BUCKETS)[:, None]

    sel = np.zeros((EXPERTS, EXPERTS, P), f)
    sel[np.arange(EXPERTS), np.arange(EXPERTS)] = 1
    return dict(cst=cst, ca=ca, cb=cb, cc=cc, sel=sel.reshape(EXPERTS, EXPERTS * P))


def build(nc, w_all, h0, smalls, rpb, cst_d, ca_d, cb_d, cc_d, sel_d, toep_d, xtok_d, y_d, out_d):
    ctx = ExitStack()
    with ctx:
        def sb(name, cols):
            return ctx.enter_context(nc.sbuf_tensor(name, [P, cols], F32))

        def sem(name):
            return ctx.enter_context(nc.semaphore(name))

        ps = ctx.enter_context(nc.psum_tensor("ps", [P, 8, 512], F32))

        ring = sb("ring", SLOTS * BLK)
        hT = sb("hT", KT * T)[:, :].rearrange("p (k t) -> p k t", k=KT)
        XT = sb("XT", KT * T)[:, :].rearrange("p (k t) -> p k t", k=KT)
        cst = sb("cst", CST_N)
        sm = sb("sm", SM_N)
        c2s = sb("c2s", 2 * KT)
        modc = sb("modc", 2 * 96)[:, :].rearrange("p (l m s) -> p l m s", l=2, s=2)
        gains = sb("gains", 4 * 2 * KT)[:, :].rearrange("p (n m s) -> p n m s", n=4, s=2)
        inv_rms = sb("inv_rms", T)
        tiny = sb("tiny", 64)
        eps_col = tiny[:, 32:33]
        tick = ctx.enter_context(nc.sbuf_tensor("tick", [P, 32], mybir.dt.bfloat16))
        arena = sb("arena", 30400)

        def area(at, cols):
            assert at + cols <= 30400
            return arena[:, at:at + cols]

        ident = cst[:, CST["ident"]]
        ones = cst[:, CST["ones"]]
        ones64 = cst[:, CST["ones64"]]
        flip, flip64 = cst[:, CST["flip"]], cst[:, CST["flip64"]]

        fnT = area(0, 1024).rearrange("p (f t) -> p f t", f=2)
        qkT = area(1024, 6144).rearrange("p (m t) -> p m t", m=12)
        Vt = area(7168, 3072).rearrange("p (t c) -> p t c", t=4)
        bias_na = area(10240, 6144).rearrange("p (q h k) -> p q h k", q=2, h=NA_H)
        ca = area(16384, CA_N)
        acs = area(18560, 1024).rearrange("p (b t c) -> p b t c", b=2, t=2)
        probs0 = area(20000, 1024).rearrange("p (b k) -> p b k", b=2)
        probsT0 = area(21024, 1024).rearrange("p (b k q) -> p b k q", b=2, k=4)
        stat = area(22048, 8 * 48 + 8)

        acc = area(0, 4096).rearrange("p (k t) -> p k t", k=KT)
        Gt = area(4096, 8192).rearrange("p (e t) -> p e t", e=EXPERTS)
        silu_b = area(12288, 1024).rearrange("p (b t) -> p b t", b=2)
        gated = area(13312, 1024).rearrange("p (b t) -> p b t", b=2)
        hid = area(14336, 2048).rearrange("p (m t) -> p m t", m=4)
        sel = area(21504, 2048).rearrange("p (e m) -> p e m", e=EXPERTS)
        rt = area(18432, 1024)
        gateT = area(19456, 512)

        xtok = area(0, 4096).rearrange("p (t c) -> p t c", t=4)
        slots = area(4096, 4096).bitcast(BF16).rearrange("p (t e s) -> p t e s", t=4, e=EXPERTS)
        xg = area(8192, 2048).rearrange("p (b c) -> p b c", b=2)
        xeT = area(10240, 2048).rearrange("p (b k s) -> p b k s", b=2, k=KT)
        es = area(12288, 1024).rearrange("p (b f) -> p b f", b=2)
        eh = area(13312, 1024).rearrange("p (b f) -> p b f", b=2)
        ehT = area(14336, 1024).rearrange("p (b k s) -> p b k s", b=2, k=4)
        ey = area(15360, 2048).rearrange("p (b c) -> p b c", b=2)
        cg = area(0, 8192).rearrange("p (w t c) -> p w t c", w=2, t=4)
        rt2 = area(19968, 512)

        qR = area(0, 2048).rearrange("p (h ab t) -> p h ab t", h=4, ab=2)
        kR = area(2048, 4096).rearrange("p (h ab t) -> p h ab t", h=4, ab=2)
        vR = area(6144, 8192).rearrange("p (t c) -> p t c", t=4)
        gR = area(14336, 4096).rearrange("p (m t) -> p m t", m=16)
        cb = area(18432, CB_N)
        decayT = area(21504, 2048).rearrange("p (b k t) -> p b k t", b=2, k=4)
        scoreT = area(23552, 2048).rearrange("p (b k t) -> p b k t", b=2, k=4)
        oR = area(25600, 1024).rearrange("p (m t) -> p m t", m=4)
        sqR = area(26624, 1024).rearrange("p (m t) -> p m t", m=4)
        rope_t = area(27648, 2048).rearrange("p (b h t) -> p b h t", b=2, h=4)
        irR = area(29696, SEQ)
        dec_t = area(29952, 128)

        z1 = area(0, 12288).rearrange("p (s h t) -> p s h t", s=6, h=8)
        z1m = area(0, 12288).rearrange("p (m t) -> p m t", m=48)
        zf = z1[:, 0:2]
        q_b, g_b, zgA, zgB = z1[:, 2], z1[:, 3], z1[:, 4], z1[:, 5]
        ib = area(12288, 2048).rearrange("p (t c) -> p t c", t=2)
        lf = area(14336, 4096).rearrange("p (d h t) -> p d h t", d=2, h=8)
        bc = area(18432, 4096).rearrange("p (d h t) -> p d h t", d=2, h=8)
        cc = area(22528, CC_N)
        pt_b = area(24064, 1024).rearrange("p (b j i) -> p b j i", b=2, j=2)
        o_b = area(25088, 512).rearrange("p (b t) -> p b t", b=2)
        sq_b = area(25600, 512).rearrange("p (b t) -> p b t", b=2)
        ir_b = area(26112, 512).rearrange("p (b t) -> p b t", b=2)
        decs = area(26624, 128).rearrange("p (d h c) -> p d h c", d=2, h=8)
        lbt = area(26752, 128)
        toep = area(26880, 512)
        mrg = area(27392, 256)
        z2 = area(14336, 7168).rearrange("p (m t) -> p m t", m=28)
        v2 = area(21504, 3072).rearrange("p (g t c) -> p g t c", g=3, t=2)
        bias2 = area(24576, 3072).rearrange("p (b q g k) -> p b q g k", b=2, q=2, g=3)
        probs2 = area(27648, 1536).rearrange("p (b k) -> p b k", b=2)
        sq2 = area(29184, 1024).rearrange("p (b t) -> p b t", b=2)
        probsT2 = area(0, 768).rearrange("p (k q) -> p k q", k=6)
        ir2 = area(768, 1024).rearrange("p (b t) -> p b t", b=2)
        stat2 = area(1792, 64)

        slot_tok = ctx.enter_context(nc.sbuf_tensor("slot_tok", [P, EXPERTS], I32))
        tok_row = ctx.enter_context(nc.sbuf_tensor("tok_row", [P, 8], I32))
        fullest = ctx.enter_context(nc.sbuf_tensor("fullest", [P, 1], I32))
        tok_bf = ctx.enter_context(nc.sbuf_tensor("tok_bf", [P, 8], BF16))

        ld_cst, ld_sm, ld_h, ld_rpb, ld_ca, ld_cb, ld_cc, ld_sel = map(sem, (
            "ld_cst", "ld_sm", "ld_h", "ld_rpb", "ld_ca", "ld_cb", "ld_cc", "ld_sel"))
        ld_bias2 = [sem(f"ld_bias2{j}") for j in range(2)]
        w_full = [sem(f"w_full{j}") for j in range(SLOTS)]
        w_free = sem("w_free")
        c2_ready, mod_ready, tick_ready = sem("c2_ready"), sem("mod_ready"), sem("tick_ready")
        nm_sq, nm_ms, nm_std, nm_tmp, nm_x = map(sem, ("nm_sq", "nm_ms", "nm_std", "nm_tmp", "nm_x"))
        res_done = sem("res_done")
        dve_step, act_step = sem("dve_step"), sem("act_step")
        mx_mm, mx_ev = sem("mx_mm"), sem("mx_ev")
        fn_mm, fn_ev = sem("fn_mm"), sem("fn_ev")
        bias_ready = sem("bias_ready")
        na_s, na_neg, na_e, na_p, na_t, na_c, na_o, na_ev = map(sem, (
            "na_s", "na_neg", "na_e", "na_p", "na_t", "na_c", "na_o", "na_ev"))
        mo_mm, mo_ev = sem("mo_mm"), sem("mo_ev")
        rt_mm, rt_sig, gate_ready, gT_mm, gT_ev, gb_mm, gb_ev = map(sem, (
            "rt_mm", "rt_sig", "gate_ready", "gT_mm", "gT_ev", "gb_mm", "gb_ev"))
        up1, up3, silu_rdy, gated_rdy, hid_rdy, dn_mm, dn_free = map(sem, (
            "up1", "up3", "silu_rdy", "gated_rdy", "hid_rdy", "dn_mm", "dn_free"))
        xt_mm, xt_ev, x_st, sel_rdy, pos_mm, full_rdy, slots_rdy, ix_mm, ix_rdy = map(sem, (
            "xt_mm", "xt_ev", "x_st", "sel_rdy", "pos_mm", "full_rdy", "slots_rdy", "ix_mm", "ix_rdy"))
        f_x, f_xa, f_xd, f_u1, f_u3, f_s, f_h, f_ht, f_he, f_d, f_ya, f_yd, f_cmb, f_cT = map(sem, (
            "f_x", "f_xa", "f_xd", "f_u1", "f_u3", "f_s", "f_h", "f_ht", "f_he", "f_d", "f_ya", "f_yd", "f_cmb", "f_cT"))
        f_c = sem("f_c")
        xg_ld, y_st = ([[sem(f"{n}{i}{j}") for j in range(2)] for i in range(2)] for n in ("xg_ld", "y_st"))
        c_ld = [sem(f"c_ld{i}") for i in range(2)]
        rp_mm, rp_ev, rope_done, lg_ready, dk_arg, dk_exp, dk_rdy, rs_mm, rs_rdy, ro_mm, ro_ev, rn_mm, rn_std, rn_rdy = \
            map(sem, ("rp_mm", "rp_ev", "rope_done", "lg_ready", "dk_arg", "dk_exp", "dk_rdy", "rs_mm", "rs_rdy",
                      "ro_mm", "ro_ev", "rn_mm", "rn_std", "rn_rdy"))
        y_mm, y_ev = sem("y_mm"), sem("y_ev")
        z1_mm, z1_ev, ib_mm, ib_ev = map(sem, ("z1_mm", "z1_ev", "ib_mm", "ib_ev"))
        f_rdy, lf_rdy, b_rdy, e_rdy = map(sem, ("f_rdy", "lf_rdy", "b_rdy", "e_rdy"))
        K_rdy, K_used, pt_rdy, ho_mm, ho_ev, hn_mm, hn_std, hg_done = map(sem, (
            "K_rdy", "K_used", "pt_rdy", "ho_mm", "ho_ev", "hn_mm", "hn_std", "hg_done"))
        lb_e, lb_s, tz_mm, tz_rdy, tz_st = map(sem, ("lb_e", "lb_s", "tz_mm", "tz_rdy", "tz_st"))
        z2_mm, z2_ev, v2_mm, v2_ev = map(sem, ("z2_mm", "z2_ev", "v2_mm", "v2_ev"))
        qn_sq, qn_mm, qn_std, qn_done = map(sem, ("qn_sq", "qn_mm", "qn_std", "qn_done"))
        at_s, at_neg, at_e, at_p, at_t, at_c, at_o, at_ev = map(sem, (
            "at_s", "at_neg", "at_e", "at_p", "at_t", "at_c", "at_o", "at_ev"))
        ya_mm, ya_ev, yb_mm, yb_ev, yo_mm, yo_ev, out_done = map(sem, (
            "ya_mm", "ya_ev", "yb_mm", "yb_ev", "yo_mm", "yo_ev", "out_done"))

        def slot(n, pattern=None, **kw):
            s = ring[:, (n % SLOTS) * BLK:(n % SLOTS + 1) * BLK]
            return s.rearrange(pattern, **kw) if pattern else s

        NORM_COLS = [(0, T), (0, T), (0, T), (SEQ, T), (SEQ, T), (SEQ, T)]
        NA_UNITS = [(seg, h, q) for seg in (1, 0) for h in range(NA_H) for q in range(2)]
        AT_UNITS = [(h, q) for h in range(AT_H) for q in range(2)]

        def na_q(seg, q):
            return slice(seg * SEQ + q * P, seg * SEQ + (q + 1) * P)

        def half(h):
            return slice(HD * (h % 2), HD * (h % 2) + HD)

        def by_load(eng, layer, routed, dense):
            eng.wait_ge(full_rdy, layer + 1)
            load = eng.value_load(fullest[0:1, 0:1], min_val=0, max_val=T)
            with eng.If(load < P + 1):
                routed(layer)
            with eng.Else():
                dense(layer)

        block = ctx.enter_context(nc.Block())

        @block.sync
        def _(sp):
            sp.dma_start(sm[:, :], smalls).then_inc(ld_sm, 16)
            for j in range(SLOTS):
                sp.dma_start(slot(j), w_all[j]).then_inc(w_full[j], 16)
                if j == 0:
                    sp.dma_start(cst[:, :], cst_d).then_inc(ld_cst, 16)
                    sp.dma_start(hT, h0).then_inc(ld_h, 16)
            with sp.Fori(0, (N_BLK - SLOTS) // SLOTS) as i:
                for j in range(SLOTS):
                    sp.wait_ge(w_free, i * SLOTS + j + 1)
                    sp.dma_start(slot(j), w_all[i * SLOTS + SLOTS + j]).then_inc(w_full[j], 16)
            for n in range(N_BLK - (N_BLK - SLOTS) % SLOTS, N_BLK):
                sp.wait_ge(w_free, n - SLOTS + 1)
                sp.dma_start(slot(n), w_all[n]).then_inc(w_full[n % SLOTS], 16)
            sp.wait_ge(yo_ev, KT)
            sp.dma_start(out_d, XT[:, :, LAT]).then_inc(out_done, 16)
            sp.wait_ge(out_done, 16)

        @block.gpsimd
        def _(pool):
            def gather(layer):
                nt = 4 if layer == 0 else 2
                pool.wait_ge(ix_rdy, layer + 1)
                pool.wait_ge(x_st, 64 if layer == 0 else 96)
                for e in range(EXPERTS):
                    if e >= 2:
                        pool.wait_ge(f_x, EXPERTS * layer + e - 1)
                    pool.indirect_dma_start(xg[:, e % 2], None, xtok_d, bass.IndirectOffsetOnAxis(
                        ap=slot_tok[:, e:e + 1].bitcast(U32), axis=0)).then_inc(xg_ld[layer][e % 2], 16)
                for j in range(2):
                    pool.wait_ge(y_st[layer][j], 128)
                for t in range(nt):
                    for w in range(2):
                        pool.indirect_dma_start(cg[:, w, t], None, y_d, bass.IndirectOffsetOnAxis(
                            ap=tok_row[:, 4 * w + t:4 * w + t + 1].bitcast(U32), axis=0)).then_inc(c_ld[layer], 16)

            def ungather(layer):
                pool.nop()

            pool.dma_start(ca, ca_d).then_inc(ld_ca, 16)
            for layer in range(2):
                pool.wait_ge(res_done, 2 * layer + 1)
                pool.dma_start(sel[0:EXPERTS], sel_d).then_inc(ld_sel, 16)
                by_load(pool, layer, gather, ungather)
                pool.wait_ge(res_done, 2 * layer + 2)
                if layer == 0:
                    pool.dma_start(cb, cb_d).then_inc(ld_cb, 16)
            pool.dma_start(cc, cc_d).then_inc(ld_cc, 16)
            pool.wait_ge(tz_rdy, 1)
            pool.dma_start(toep_d, toep[0:24, :]).then_inc(tz_st, 16)
            pool.wait_ge(tz_st, 16)
            pool.wait_ge(hg_done, HG)
            for h in range(AT_H):
                if h >= 2:
                    pool.wait_ge(at_s, 2 * (h - 1))
                for q in range(2):
                    pool.dma_start(bias2[:, h % 2, q], bass.AP(
                        tensor=toep_d.tensor, offset=h * 512 + P - P * q,
                        ap=[[1, P], [AT_H * 512, AT_G], [1, SEQ]])).then_inc(ld_bias2[h % 2], 16)

        @block.tensor
        def _(pe):
            def arrive(n):
                pe.wait_ge(w_full[n % SLOTS], 16 * (n // SLOTS + 1))

            def chain(out, pairs):
                for i, (a, b) in enumerate(pairs):
                    last = nc.tensor.matmul(out, a, b, start=(i == 0), stop=(i == len(pairs) - 1))
                return last

            def release():
                nc.tensor.matmul(ps[0:32, 7, 0:2], tick[:, 0:32], tick[:, 0:2], start=True, stop=True).then_inc(w_free, 1)

            def norm(i):
                a, b = NORM_COLS[i]
                for k in range(KT):
                    pe.wait_ge(nm_sq, KT * i + k + 1)
                    last = nc.tensor.matmul(ps[:, 7, 0:b - a], ones, XT[:, k, a:b], start=(k == 0), stop=(k == KT - 1))
                last.then_inc(nm_ms, 1)

            def router(layer):
                tts = range(4) if layer == 0 else range(2)
                t0 = 0 if layer == 0 else SEQ
                w = sm[:, SM["router_w"]].rearrange("p (k e) -> p k e", k=KT)
                for tt in tts:
                    last = chain(ps[:, 0, tt * 16:tt * 16 + 16],
                                 [(XT[:, k, t0 + tt * P:t0 + (tt + 1) * P], w[:, k]) for k in range(KT)])
                last.then_inc(rt_mm, 1)
                for tt in tts:
                    if tt >= 2:
                        pe.wait_ge(xt_ev, 4 * layer + tt - 1)
                    for k in range(KT):
                        last = nc.tensor.transpose(ps[:, 1 + 2 * (tt % 2) + k // 4, (k % 4) * P:(k % 4 + 1) * P],
                                                   XT[:, k, t0 + tt * P:t0 + (tt + 1) * P], ident)
                    last.then_inc(xt_mm, 1)
                pe.wait_ge(sel_rdy, layer + 1)
                chosen = lambda tt: rt[:, 704 + tt * 16:720 + tt * 16]
                for tt in tts:
                    chain(ps[:, 5, tt * 16:tt * 16 + 16],
                          [(ones, chosen(j)) for j in range(tt)] + [(cst[:, CST["tri"]], chosen(tt))])
                chain(ps[:, 5, 64:80], [(ones, chosen(j)) for j in tts]).then_inc(pos_mm, 1)

            def spread_gates(layer):
                tts = range(4) if layer == 0 else range(2)
                pe.wait_ge(gate_ready, layer + 1)
                pe.wait_ge(xt_ev, 4 * layer + len(tts))
                for tt in tts:
                    last = nc.tensor.matmul(ps[0:16, 1, tt * P:(tt + 1) * P], rt[:, tt * 16:tt * 16 + 16], ident,
                                            start=True, stop=True)
                last.then_inc(gT_mm, 1)
                pe.wait_ge(gT_ev, layer + 1)
                pe.wait_ge(ld_sel, 16 * (layer + 1))
                n = len(tts) * P
                for e in range(EXPERTS):
                    if e >= 4:
                        pe.wait_ge(gb_ev, EXPERTS * layer + e - 3)
                    nc.tensor.matmul(ps[:, 2 + e % 4, 0:n], sel[0:EXPERTS, e], gateT[0:EXPERTS, 0:n],
                                     start=True, stop=True).then_inc(gb_mm, 1)
                pe.wait_ge(gb_ev, EXPERTS * (layer + 1))

            def routed(layer):
                for s_, n in ((up1, 64), (up3, 64), (hid_rdy, 2), (dn_free, 2), (dn_mm, 128), (gT_mm, 1), (gb_mm, 16)):
                    pe.sem_inc(s_, n)
                nt = 4 if layer == 0 else 2
                c = EXPERTS * layer
                base = B_MOE0 if layer == 0 else B_MOE1
                pe.wait_ge(slots_rdy, layer + 1)
                for e in range(EXPERTS):
                    last = chain(ps[:, 6, 2 * e:2 * e + 2],
                                 [(slots[:, t, e], tok_bf[:, 2 * t:2 * t + 2]) for t in range(nt)])
                last.then_inc(ix_mm, 1)
                w1, w3 = (slot(base + j, "p (k m) -> p k m", k=KT) for j in range(2))
                w2 = slot(base + 2, "p (k m) -> p k m", k=4)

                def arrive_e(e, n):
                    pe.wait_ge(w_full[n % SLOTS], e * 16 + 16 * (n // SLOTS + 1))

                def turn_rows(e, j, half_e, first):
                    pe.wait_ge(xg_ld[layer][j], half_e * 16 + 16)
                    if not first:
                        pe.wait_ge(f_xa, e + c)
                        pe.wait_ge(f_xd, e + c)
                    for k in range(KT):
                        last = nc.tensor.transpose(ps[:, k // 4, (k % 4) * P:(k % 4 + 1) * P],
                                                   xg[:, j, k * P:(k + 1) * P], ident)
                    last.then_inc(f_x, 1)

                def turn(e, j, first, last_e, half_e):
                    some = not (first and j == 0)
                    pe.wait_ge(f_xa, e + (c + 1))
                    pe.wait_ge(f_xd, e + (c + 1))
                    for n, w, bank, free, done in ((0, w1, 2, f_s, f_u1), (1, w3, 3, f_h, f_u3)):
                        arrive_e(e, base + n)
                        if some:
                            pe.wait_ge(free, e + c)
                        chain(ps[:, bank, :], [(xeT[:, j, k], w[:, k]) for k in range(KT)]).then_inc(done, 1)
                        release()
                    if not last_e:
                        turn_rows(e + 1, 1 - j, half_e + j, False)
                    pe.wait_ge(f_h, e + (c + 1))
                    if some:
                        pe.wait_ge(f_he, e + c)
                    for k in range(4):
                        last = nc.tensor.transpose(ps[:, 4, k * P:(k + 1) * P], eh[:, j, k * P:(k + 1) * P], ident)
                    last.then_inc(f_ht, 1)
                    arrive_e(e, base + 2)
                    pe.wait_ge(f_he, e + (c + 1))
                    for n, free in ((0, f_ya), (1, f_yd)):
                        if some:
                            pe.wait_ge(free, e + c)
                        chain(ps[:, 5 + n, :], [(ehT[:, j, k], w2[:, k, n * 512:(n + 1) * 512]) for k in range(4)]).then_inc(f_d, 1)
                    release()

                turn_rows(0, 0, 0, layer == 0)
                for j in range(2):
                    turn(j, j, True, False, 0)
                with pe.Fori(1, EXPERTS // 2 - 1) as i:
                    for j in range(2):
                        turn(i * 2 + j, j, False, False, i)
                for j in range(2):
                    turn(EXPERTS - 2 + j, j, False, j == 1, EXPERTS // 2 - 1)
                for m in range(KT):
                    if m >= 2:
                        pe.wait_ge(f_cT, KT * layer + m - 1)
                    for t in range(nt):
                        if m == 0:
                            pe.wait_ge(f_cmb, 4 * layer + t + 1)
                        last = nc.tensor.transpose(ps[:, m % 2, t * P:(t + 1) * P], cg[:, 0, t, m * P:(m + 1) * P], ident)
                    last.then_inc(f_c, 1)

            def dense(layer):
                for s_, n in ((f_x, 16), (f_u1, 16), (f_u3, 16), (f_ht, 16), (f_d, 32), (ix_mm, 1), (f_c, 8)):
                    pe.sem_inc(s_, n)
                spread_gates(layer)
                experts(layer)

            def experts(layer):
                base = B_MOE0 if layer == 0 else B_MOE1
                t0, n = (0, T) if layer == 0 else (SEQ, SEQ)
                pe.sem_inc(hid_rdy, 2)
                pe.sem_inc(dn_free, 2)
                u0, d0 = (4 * EXPERTS + 2) * layer, (8 * EXPERTS + 2) * layer
                w = [slot(base + j) for j in range(3)]
                w1, w3 = (x.rearrange("p (k m) -> p k m", k=KT) for x in w[:2])
                w2 = w[2].rearrange("p (k m) -> p k m", k=4)

                def arrive_e(e, n):
                    pe.wait_ge(w_full[n % SLOTS], e * 16 + 16 * (n // SLOTS + 1))

                with pe.Fori(0, EXPERTS) as e:
                    for m in range(4):
                        pe.wait_ge(hid_rdy, e * 4 + (u0 + m + 1))
                        for j, wj, done in ((0, w1, up1), (1, w3, up3)):
                            if m == 0:
                                arrive_e(e, base + j)
                            chain(ps[:, 2 * (m % 2) + j, 0:n],
                                  [(wj[:, k, m * P:(m + 1) * P], XT[:, k, t0:t0 + n]) for k in range(KT)]).then_inc(done, 1)
                            if m == 3:
                                release()
                    arrive_e(e, base + 2)
                    pe.wait_ge(hid_rdy, e * 4 + (u0 + 6))
                    for m in range(8):
                        pe.wait_ge(dn_free, e * 8 + (d0 + m + 1))
                        chain(ps[:, 4 + m % 2, 0:n],
                              [(w2[:, k, m * P:(m + 1) * P], hid[:, k, 0:n]) for k in range(4)]).then_inc(dn_mm, 1)
                    release()

            pe.wait_ge(ld_sm, 16)
            pe.wait_ge(c2_ready, 1)
            c2v = c2s[:, :].rearrange("p (k s) -> p k s", s=2)
            for layer in range(2):
                with pe.Fori(0, 4) as i:
                    for j in range(3):
                        n = B_ADA + 12 * layer + j
                        pe.wait_ge(w_full[n % SLOTS], i * 16 + 16 * (n // SLOTS + 1))
                        w = slot(n, "p (k m) -> p k m", k=KT)
                        for m in range(4):
                            last = chain(ps[:, layer, bass.ds(i * 24 + (8 * j + 2 * m), 2)],
                                         [(w[:, k, m * P:(m + 1) * P], c2v[:, k]) for k in range(KT)])
                        last.then_inc(w_free, 1)

            pe.wait_ge(ld_cst, 16)
            pe.wait_ge(tick_ready, 1)
            norm(0)
            pe.wait_ge(nm_x, KT)
            pe.wait_ge(mod_ready, 2)
            unit = 0
            for b in range(5):
                arrive(B_MIX + b)
                w = slot(B_MIX + b, "p (k m) -> p k m", k=KT)
                for m in range((4, 4, 4, 2, 0)[b]):
                    if unit >= 4:
                        pe.wait_ge(mx_ev, unit - 3)
                    chain(ps[:, unit % 4, :],
                          [(w[:, k, m * P:(m + 1) * P], XT[:, k, :]) for k in range(KT)]).then_inc(mx_mm, 1)
                    unit += 1
                if b >= 3:
                    cols = slice(256, 512) if b == 3 else slice(0, 512)
                    for tt in range(4):
                        pe.wait_ge(mx_ev, unit - 3)
                        chain(ps[:, unit % 4, 0:cols.stop - cols.start],
                              [(XT[:, k, tt * P:(tt + 1) * P], w[:, k, cols]) for k in range(KT)]).then_inc(mx_mm, 1)
                        unit += 1
                release()
            pe.wait_ge(mx_ev, unit)

            pe.wait_ge(ld_ca, 16)
            cosN = ca[:, CA["cos"]].rearrange("p (t n) -> p t n", t=2)
            msinN = ca[:, CA["msin"]].rearrange("p (t n) -> p t n", t=2)
            for n, (seg, f) in enumerate((s, f) for s in range(2) for f in range(2)):
                if n:
                    pe.wait_ge(fn_ev, 2 * n - 1)
                for tt in range(2):
                    last = nc.tensor.matmul(ps[:, 4, tt * 256:(tt + 1) * 256], fnT[:, f, na_q(seg, tt)],
                                            ca[:, CA["dft64"]], start=True, stop=True)
                last.then_inc(fn_mm, 1)
                pe.wait_ge(fn_ev, 2 * n + 1)
                chain(ps[:, 5, 0:SEQ], [(acs[:, 0, tt, c * P:(c + 1) * P], (cosN, msinN)[c][:, tt])
                                        for tt in range(2) for c in range(2)]).then_inc(fn_mm, 1)
            pe.wait_ge(fn_ev, 8)

            pe.wait_ge(bias_ready, 1)
            for i in range(len(NA_UNITS) + 2):
                if i < len(NA_UNITS):
                    seg, h, q = NA_UNITS[i]
                    nk = T if seg else SEQ
                    if i >= 3:
                        pe.wait_ge(na_e, i - 2)
                    last = nc.tensor.matmul(ps[:, i % 3, 0:nk], qkT[half(h), h // 2, na_q(seg, q)],
                                            qkT[half(h), 6 + h // 2, 0:nk], start=True, stop=not seg)
                    if seg:
                        last = nc.tensor.matmul(ps[:, i % 3, LAT], flip64, bias_na[:, q, h], start=False, stop=True)
                    last.then_inc(na_s, 1)
                if 0 <= i - 1 < len(NA_UNITS):
                    u = i - 1
                    pe.wait_ge(na_p, u + 1)
                    if u >= 2:
                        pe.wait_ge(na_c, u - 1)
                    for kt in range(4 if NA_UNITS[u][0] else 2):
                        last = nc.tensor.transpose(ps[:, 3 + u % 2, kt * P:(kt + 1) * P],
                                                   probs0[:, u % 2, kt * P:(kt + 1) * P], ident)
                    last.then_inc(na_t, 1)
                if i >= 2:
                    u = i - 2
                    seg, h, q = NA_UNITS[u]
                    pe.wait_ge(na_c, u + 1)
                    if u >= 2:
                        pe.wait_ge(na_ev, u - 1)
                    chain(ps[half(h), 5 + u % 2, 0:P],
                          [(Vt[:, kt, h * HD:(h + 1) * HD], probsT0[:, u % 2, kt])
                           for kt in range(4 if seg else 2)]).then_inc(na_o, 1)
            pe.wait_ge(na_ev, len(NA_UNITS))
            for b in range(2):
                arrive(B_MIXO + b)
                w = slot(B_MIXO + b, "p (k m) -> p k m", k=KT)
                for m in range(4):
                    u = 4 * b + m
                    if u >= 4:
                        pe.wait_ge(mo_ev, u - 3)
                    chain(ps[:, u % 4, :], [(w[:, k, m * P:(m + 1) * P], XT[:, k]) for k in range(KT)]).then_inc(mo_mm, 1)
                release()

            norm(1)
            pe.wait_ge(nm_x, 2 * KT)
            router(0)
            by_load(pe, 0, routed, dense)

            norm(2)
            pe.wait_ge(nm_x, 3 * KT)
            unit = 0
            for b in range(12):
                arrive(B_RET + b)
                w = slot(B_RET + b, "p (k m) -> p k m", k=KT)
                for m in range(4):
                    if unit >= 4:
                        pe.wait_ge(rp_ev, unit - 3)
                    if 4 <= b < 8:
                        pairs = [(XT[:, k, m * P:(m + 1) * P], w[:, k]) for k in range(KT)]
                    else:
                        pairs = [(w[:, k, m * P:(m + 1) * P], XT[:, k, (0 if 2 <= b < 4 else SEQ):T]) for k in range(KT)]
                    chain(ps[:, unit % 4, 0:(T if 2 <= b < 8 else SEQ)], pairs).then_inc(rp_mm, 1)
                    unit += 1
                release()
            pe.wait_ge(rp_ev, unit)
            pe.wait_ge(rope_done, 2)

            def ret_scores(h):
                if h:
                    pe.wait_ge(rs_rdy, 2 * h)
                for kt in range(4):
                    last = chain(ps[:, kt // 2, (kt % 2) * SEQ:(kt % 2 + 1) * SEQ],
                                 [(kR[:, h, ab, kt * P:(kt + 1) * P], qR[:, h, ab]) for ab in range(2)])
                last.then_inc(rs_mm, 1)

            ret_scores(0)
            for h in range(RET_H):
                pe.wait_ge(rs_rdy, 2 * h + 2)
                if h:
                    pe.wait_ge(ro_ev, h)
                for dv in range(4):
                    last = chain(ps[:, 2 + dv // 2, (dv % 2) * SEQ:(dv % 2 + 1) * SEQ],
                                 [(vR[:, kt, h * 512 + dv * P:h * 512 + (dv + 1) * P], scoreT[:, h % 2, kt])
                                  for kt in range(4)])
                last.then_inc(ro_mm, 1)
                if h + 1 < RET_H:
                    ret_scores(h + 1)
                pe.wait_ge(ro_ev, h + 1)
                chain(ps[:, 4, 0:SEQ], [(ones, sqR[:, m]) for m in range(4)]).then_inc(rn_mm, 1)
            pe.wait_ge(rn_rdy, RET_H)
            for b in range(4):
                arrive(B_RETO + b)
                w = slot(B_RETO + b, "p (k m) -> p k m", k=16)
                for m in range(2):
                    u = 2 * b + m
                    if u >= 4:
                        pe.wait_ge(y_ev, u - 3)
                    chain(ps[:, u % 4, 0:SEQ], [(w[:, k, m * P:(m + 1) * P], gR[:, k]) for k in range(16)]).then_inc(y_mm, 1)
                release()

            norm(3)
            pe.wait_ge(nm_x, 4 * KT)
            router(1)
            by_load(pe, 1, routed, dense)

            norm(4)
            norm(5)
            pe.wait_ge(nm_tmp, 6 * KT)
            pe.sem_inc(z1_ev, 6)
            with pe.Fori(0, 4) as i:
                for j in range(3):
                    n = B_Z1 + j
                    pe.wait_ge(w_full[n % SLOTS], i * 16 + 16 * (n // SLOTS + 1))
                    w = slot(n, "p (k m) -> p k m", k=KT)
                    for hf in range(2):
                        pe.wait_ge(z1_ev, i * 6 + (2 * j + hf + 1))
                        for m in range(2):
                            last = chain(ps[:, 2 * j + hf, m * SEQ:(m + 1) * SEQ],
                                         [(w[:, k, (2 * hf + m) * P:(2 * hf + m + 1) * P], XT[:, k, LAT]) for k in range(KT)])
                        last.then_inc(z1_mm, 1)
                    release()
            pe.wait_ge(z1_ev, 30)
            for b in range(2):
                arrive(B_IB + b)
                w = slot(B_IB + b, "p (k m) -> p k m", k=KT)
                for tt in range(2):
                    chain(ps[:, 2 * b + tt, :],
                          [(XT[:, k, SEQ + tt * P:SEQ + (tt + 1) * P], w[:, k]) for k in range(KT)]).then_inc(ib_mm, 1)
                release()
            pe.wait_ge(ld_cc, 16)
            nc.tensor.matmul(ps[0:24, 6, 0:511], sm[0:BUCKETS, SM["rel_bias"]], cc[0:BUCKETS, CC["onehot"]],
                             start=True, stop=True).then_inc(tz_mm, 1)
            pe.wait_ge(ib_ev, 4)

            def gla_scores(h):
                if h >= 2:
                    pe.wait_ge(pt_rdy, h - 1)
                for d in range(2):
                    pe.wait_ge(K_rdy, 2 * h + d + 1)
                    near, far = (0, 1) if d == 0 else (1, 0)
                    bank = 2 * (h % 2) + d
                    for c in range(NCH):
                        Kc = zf[:, d, c]
                        qc = lf[:, d, h, c * CH:(c + 1) * CH]
                        last = nc.tensor.matmul(ps[:, bank, c * CH:(c + 1) * CH], Kc[:, near * P:(near + 1) * P], qc,
                                                start=True, stop=True)
                        if c // 4 == far:
                            at = SEQ + (c % 4) * CH
                            last = nc.tensor.matmul(ps[:, bank, at:at + CH], Kc[:, far * P:(far + 1) * P], qc,
                                                    start=True, stop=True)
                    last.then_inc(K_used, 1)

            pe.wait_ge(tz_rdy, 1)
            gla_scores(0)
            for h in range(HG):
                if h + 1 < HG:
                    gla_scores(h + 1)
                pe.wait_ge(pt_rdy, h + 1)
                if h >= 2:
                    pe.wait_ge(ho_ev, h - 1)
                chain(ps[:, 4 + h % 2, 0:SEQ],
                      [(ib[:, j, h * P:(h + 1) * P], pt_b[:, h % 2, j]) for j in range(2)]).then_inc(ho_mm, 1)
                pe.wait_ge(ho_ev, h + 1)
                if h:
                    pe.wait_ge(hn_std, h)
                nc.tensor.matmul(ps[:, 6, 0:SEQ], ones, sq_b[:, h % 2], start=True, stop=True).then_inc(hn_mm, 1)
            pe.wait_ge(hg_done, HG)

            for b in range(10):
                arrive(B_Z2 + b)
                w = slot(B_Z2 + b, "p (k m) -> p k m", k=KT)
                for hf in range(2):
                    u = 2 * b + hf
                    if u >= 6:
                        pe.wait_ge(z2_ev, u - 5)
                    if b < 7:
                        for m in range(2):
                            last = chain(ps[:, u % 6, m * SEQ:(m + 1) * SEQ],
                                         [(w[:, k, (2 * hf + m) * P:(2 * hf + m + 1) * P], XT[:, k, LAT]) for k in range(KT)])
                    else:
                        last = chain(ps[:, u % 6, :],
                                     [(XT[:, k, SEQ + hf * P:SEQ + (hf + 1) * P], w[:, k]) for k in range(KT)])
                    last.then_inc(z2_mm, 1)
                release()
            for u in range(12):
                pe.wait_ge(qn_sq, u + 1)
                if u >= 2:
                    pe.wait_ge(qn_std, u - 1)
                nc.tensor.matmul(ps[:, 6 + u % 2, :], ones64, sq2[:, u % 2], start=True, stop=True).then_inc(qn_mm, 1)
            pe.wait_ge(qn_done, 12)
            pe.wait_ge(z2_ev, 20)

            for i in range(len(AT_UNITS) + 2):
                if i < len(AT_UNITS):
                    h, q = AT_UNITS[i]
                    if i >= 2:
                        pe.wait_ge(at_e, i - 1)
                    for g in range(AT_G):
                        last = nc.tensor.matmul(ps[:, 2 * (i % 2) + g // 2, (g % 2) * SEQ:(g % 2 + 1) * SEQ],
                                                z2[half(h), 4 + 8 * g + h // 2, q * P:(q + 1) * P],
                                                z2[half(h), 8 + 8 * g + h // 2, :], start=(g != 1), stop=False,
                                                skip_group_check=True)
                    pe.wait_ge(ld_bias2[h % 2], 32 * (h // 2 + 1))
                    for g in range(0, AT_G, 2):
                        last = nc.tensor.matmul(ps[:, 2 * (i % 2) + g // 2, 0:(2 * SEQ if g == 0 else SEQ)], flip,
                                                bias2[:, h % 2, q, g:min(g + 2, AT_G)], start=False, stop=True,
                                                skip_group_check=True)
                    last.then_inc(at_s, 1)
                if 0 <= i - 1 < len(AT_UNITS):
                    u = i - 1
                    pe.wait_ge(at_p, u + 1)
                    if u:
                        pe.wait_ge(at_c, u)
                    for kt in range(6):
                        last = nc.tensor.transpose(ps[:, 4 + kt // 4, (kt % 4) * P:(kt % 4 + 1) * P],
                                                   probs2[:, u % 2, kt * P:(kt + 1) * P], ident)
                    last.then_inc(at_t, 1)
                if i >= 2:
                    u = i - 2
                    h, q = AT_UNITS[u]
                    pe.wait_ge(at_c, u + 1)
                    if u >= 2:
                        pe.wait_ge(at_ev, u - 1)
                    chain(ps[half(h), 6 + u % 2, 0:P],
                          [(v2[:, kt // 2, kt % 2, h * HD:(h + 1) * HD], probsT2[:, kt]) for kt in range(6)]).then_inc(at_o, 1)
            pe.wait_ge(at_ev, len(AT_UNITS))

            arrive(B_PA)
            w = slot(B_PA, "p (k m) -> p k m", k=4)
            for m in range(8):
                if m >= 4:
                    pe.wait_ge(ya_ev, m - 3)
                chain(ps[:, m % 4, 0:SEQ], [(w[:, k, m * P:(m + 1) * P], z2[:, k]) for k in range(4)]).then_inc(ya_mm, 1)
            release()
            for m in range(8):
                if m % 4 == 0:
                    arrive(B_PB + m // 4)
                    w = slot(B_PB + m // 4, "p (k m) -> p k m", k=KT)
                if m >= 2:
                    pe.wait_ge(yb_ev, m - 1)
                chain(ps[:, 4 + m % 2, 0:SEQ],
                      [(w[:, k, (m % 4) * P:(m % 4 + 1) * P], g_b[:, k]) for k in range(KT)]).then_inc(yb_mm, 1)
                if m % 4 == 3:
                    release()
            pe.wait_ge(yb_ev, KT)
            for m in range(8):
                if m % 4 == 0:
                    arrive(B_WO + m // 4)
                    w = slot(B_WO + m // 4, "p (k m) -> p k m", k=KT)
                if m >= 4:
                    pe.wait_ge(yo_ev, m - 3)
                chain(ps[:, m % 4, 0:SEQ],
                      [(w[:, k, (m % 4) * P:(m % 4 + 1) * P], zgA[:, k]) for k in range(KT)]).then_inc(yo_mm, 1)

        @block.scalar
        def _(act):
            def norm_in(i):
                a, b = NORM_COLS[i]
                if i == 0:
                    act.wait_ge(ld_h, 16)
                elif i < 5:
                    act.wait_ge(res_done, i)
                else:
                    act.wait_ge(nm_tmp, 5 * KT)
                for k in range(KT):
                    nc.scalar.activation(XT[:, k, a:b], hT[:, k, a:b], ACT.Square).then_inc(nm_sq, 1)
                act.wait_ge(nm_ms, i + 1)
                nc.scalar.activation(inv_rms[:, 0:b - a], ps[:, 7, 0:b - a], ACT.Sqrt, bias=eps_col, scale=1.0 / D).then_inc(nm_std, 1)

            def norm_out(i):
                a, b = NORM_COLS[i]
                act.wait_ge(mod_ready, i // 2 + 1)
                for k in range(KT):
                    act.wait_ge(nm_tmp, KT * i + k + 1)
                    for seg in range(a // SEQ, 2):
                        part = XT[:, k, seg * SEQ:(seg + 1) * SEQ]
                        last = nc.scalar.activation(part, part, ACT.Identity, scale=gains[:, i, k, seg:seg + 1],
                                                    bias=modc[:, i // 2, 24 * (i % 2) + k, seg:seg + 1])
                    last.then_inc(nm_x, 1)

            def router(layer):
                nt = 4 if layer == 0 else 2
                act.wait_ge(rt_mm, layer + 1)
                nc.scalar.activation(rt[:, 64:64 + 16 * nt], ps[:, 0, 0:16 * nt], ACT.Sigmoid).then_inc(rt_sig, 1)
                for tt in range(nt):
                    act.wait_ge(xt_mm, 4 * layer + tt + 1)
                    nc.scalar.activation(xtok[:, tt], ps[:, 1 + 2 * (tt % 2):3 + 2 * (tt % 2), :].rearrange("p b c -> p (b c)"),
                                         ACT.Copy).then_inc(xt_ev, 1)
                    act.wait_ge(xt_ev, 4 * layer + tt + 1)
                    act.dma_start(xtok_d[tt * P:(tt + 1) * P], xtok[:, tt]).then_inc(x_st, 16)

            def routed(layer):
                for s_, n in ((silu_rdy, 64), (gT_ev, 1), (gb_ev, 16)):
                    act.sem_inc(s_, n)
                c = EXPERTS * layer

                def copy_rows(e, j):
                    act.wait_ge(f_x, e + (c + 1))
                    nc.scalar.activation(xeT[:, j, 0:4], ps[:, 0, :].rearrange("p (k s) -> p k s", k=4), ACT.Copy).then_inc(f_xa, 1)

                def turn(e, j, first, last_e, half_e):
                    act.wait_ge(f_u1, e + (c + 1))
                    nc.scalar.activation(es[:, j], ps[:, 2, :], ACT.Silu).then_inc(f_s, 1)
                    if not last_e:
                        copy_rows(e + 1, 1 - j)
                    act.wait_ge(f_d, e * 2 + (2 * c + 1))
                    if not first:
                        act.wait_ge(y_st[layer][j], half_e * 16)
                    nc.scalar.activation(ey[:, j, 0:512], ps[:, 5, :], ACT.Copy).then_inc(f_ya, 1)
                    act.wait_ge(f_ya, e + (c + 1))
                    act.wait_ge(f_yd, e + (c + 1))
                    act.dma_start(y_d[bass.ds(e * P, P)], ey[:, j]).then_inc(y_st[layer][j], 16)

                copy_rows(0, 0)
                for j in range(2):
                    turn(j, j, True, False, 0)
                with act.Fori(1, EXPERTS // 2 - 1) as i:
                    for j in range(2):
                        turn(i * 2 + j, j, False, False, i)
                for j in range(2):
                    turn(EXPERTS - 2 + j, j, False, j == 1, EXPERTS // 2 - 1)

            def dense(layer):
                for s_, n in ((f_xa, 16), (f_s, 16), (f_ya, 16)):
                    act.sem_inc(s_, n)
                nt = 4 if layer == 0 else 2
                act.wait_ge(gT_mm, layer + 1)
                nc.scalar.activation(gateT[0:EXPERTS, 0:nt * P], ps[0:EXPERTS, 1, 0:nt * P], ACT.Copy).then_inc(gT_ev, 1)
                for e in range(EXPERTS):
                    act.wait_ge(gb_mm, EXPERTS * layer + e + 1)
                    nc.scalar.activation(Gt[:, e, 0:nt * P], ps[:, 2 + e % 4, 0:nt * P], ACT.Copy).then_inc(gb_ev, 1)
                experts(layer)

            def experts(layer):
                n = T if layer == 0 else SEQ
                with act.Fori(0, EXPERTS) as e:
                    for m in range(4):
                        act.wait_ge(up1, e * 4 + (4 * EXPERTS * layer + m + 1))
                        nc.scalar.activation(silu_b[:, m % 2, 0:n], ps[:, 2 * (m % 2), 0:n], ACT.Silu).then_inc(silu_rdy, 1)

            for r in range(ROWS):
                for kr in range(ROWS):
                    act.dma_start(bias_na[(r % 2) * GRID_W:(r % 2 + 1) * GRID_W, r // 2, :, kr * GRID_W:(kr + 1) * GRID_W],
                                  bass.AP(tensor=rpb.tensor,
                                          offset=(kr - r + NA_KH - 1) * RPB_W + NA_KW - GRID_W,
                                          ap=[[1, GRID_W], [RPB_HEAD, NA_H], [1, GRID_W]])).then_inc(ld_rpb, 16)
            act.wait_ge(ld_sm, 16)
            nc.scalar.activation(c2s[:, :], sm[:, SM["c2"]], ACT.Silu).then_inc(c2_ready, 1)
            act.wait_ge(tick_ready, 1)
            norm_in(0)
            norm_out(0)
            for u in range(22):
                act.wait_ge(mx_mm, u + 1)
                if u < 2:
                    dst = fnT[:, u, :]
                elif u < 14:
                    dst = qkT[:, u - 2, :]
                elif u < 18:
                    dst = Vt[:, u - 14, 0:256]
                else:
                    dst = Vt[:, u - 18, 256:768]
                nc.scalar.activation(dst, ps[:, u % 4, 0:(256 if 14 <= u < 18 else 512)], ACT.Copy).then_inc(mx_ev, 1)
            for n, (seg, f) in enumerate((s, f) for s in range(2) for f in range(2)):
                act.wait_ge(fn_mm, 2 * n + 1)
                nc.scalar.activation(acs[:, 0], ps[:, 4, :].rearrange("p (t c) -> p t c", t=2), ACT.Copy).then_inc(fn_ev, 1)
                act.wait_ge(fn_mm, 2 * n + 2)
                nc.scalar.activation(XT[:, f, seg * SEQ:(seg + 1) * SEQ], ps[:, 5, 0:SEQ], ACT.Copy).then_inc(fn_ev, 1)
            for i in range(len(NA_UNITS) + 2):
                if i < len(NA_UNITS):
                    nk = T if NA_UNITS[i][0] else SEQ
                    act.wait_ge(na_neg, i + 1)
                    if i >= 2:
                        act.wait_ge(na_t, i - 1)
                    nc.scalar.activation(probs0[:, i % 2, 0:nk], ps[:, i % 3, 0:nk], ACT.Exp, scale=0.125,
                                         bias=stat[:, 4 * i + 1:4 * i + 2], accum_out=stat[:, 4 * i + 2:4 * i + 3]).then_inc(na_e, 1)
                if 0 <= i - 1 < len(NA_UNITS):
                    u = i - 1
                    nk = T if NA_UNITS[u][0] else SEQ
                    act.wait_ge(na_t, u + 1)
                    if u >= 2:
                        act.wait_ge(na_o, u - 1)
                    nc.scalar.activation(probsT0[:, u % 2, 0:nk // P],
                                         ps[:, 3 + u % 2, 0:nk].rearrange("p (k q) -> p k q", q=P), ACT.Copy).then_inc(na_c, 1)
                if i >= 2:
                    u = i - 2
                    seg, h, q = NA_UNITS[u]
                    act.wait_ge(na_o, u + 1)
                    nc.scalar.activation(XT[half(h), 2 + h // 2, na_q(seg, q)], ps[half(h), 5 + u % 2, 0:P],
                                         ACT.Copy).then_inc(na_ev, 1)
            norm_in(1)
            norm_out(1)
            router(0)
            by_load(act, 0, routed, dense)

            norm_in(2)
            norm_out(2)
            nc.scalar.activation(dec_t[:, 0:8], sm[:, SM["decay"]], ACT.Exp).then_inc(lg_ready, 1)
            act.wait_ge(lg_ready, 2)
            nc.scalar.activation(dec_t[:, 16:24], dec_t[:, 8:16], ACT.Ln).then_inc(lg_ready, 1)
            for u in range(48):
                act.wait_ge(rp_mm, u + 1)
                b, m = u // 4, u % 4
                if b < 2:
                    dst, n = qR.rearrange("p h ab t -> p (h ab) t")[:, u], SEQ
                elif b < 4:
                    dst, n = kR.rearrange("p h ab t -> p (h ab) t")[:, u - 8], T
                elif b < 8:
                    dst, n = vR[:, m, (b - 4) * 512:(b - 3) * 512], T
                else:
                    dst, n = gR[:, u - 32], SEQ
                nc.scalar.activation(dst, ps[:, u % 4, 0:n], ACT.Silu if b >= 8 else ACT.Copy).then_inc(rp_ev, 1)

            def decays(h):
                act.wait_ge(dk_arg, h + 1)
                act.wait_ge(ld_cb, 16)
                lat = decayT[:, h % 2, 2:4].rearrange("p k t -> p (k t)")
                nc.scalar.activation(lat, lat, ACT.Exp)
                nc.scalar.activation(decayT[:, h % 2, 0:2].rearrange("p k t -> p (k t)"), cb[:, CB["ctx_f"]], ACT.Exp,
                                     scale=dec_t[:, 48 + h:49 + h])
                nc.scalar.activation(rope_t[:, h % 2, 0:2].rearrange("p k t -> p (k t)"), cb[:, CB["ctx_b"]], ACT.Exp,
                                     scale=dec_t[:, 52 + h:53 + h]).then_inc(dk_exp, 1)

            decays(0)
            for h in range(RET_H):
                if h + 1 < RET_H:
                    decays(h + 1)
                act.wait_ge(ro_mm, h + 1)
                if h:
                    act.wait_ge(rn_rdy, h)
                o = ps[:, 2:4, :].rearrange("p b (m t) -> p (b m) t", m=2)
                nc.scalar.activation(oR, o, ACT.Copy)
                nc.scalar.activation(sqR, o, ACT.Square).then_inc(ro_ev, 1)
                act.wait_ge(rn_mm, h + 1)
                nc.scalar.activation(irR, ps[:, 4, 0:SEQ], ACT.Sqrt, bias=eps_col, scale=1.0 / 512).then_inc(rn_std, 1)
            norm_in(3)
            norm_out(3)
            router(1)
            by_load(act, 1, routed, dense)

            norm_in(4)
            norm_in(5)
            act.wait_ge(lb_s, 1)
            nc.scalar.activation(lbt[:, 48:80], lbt[:, 16:48], ACT.Exp).then_inc(lb_e, 1)
            funcs = (ACT.Sigmoid, ACT.Sigmoid, ACT.Copy, ACT.Silu, ACT.Sigmoid, ACT.Sigmoid)
            for u in range(24):
                act.wait_ge(z1_mm, u + 1)
                nc.scalar.activation(z1m[:, 2 * u:2 * u + 2], ps[:, u % 6, :].rearrange("p (m t) -> p m t", m=2),
                                     funcs[u // 4]).then_inc(z1_ev, 1)
            for u in range(4):
                act.wait_ge(ib_mm, u + 1)
                nc.scalar.activation(ib[:, u % 2, (u // 2) * 512:(u // 2 + 1) * 512], ps[:, u, :], ACT.Copy).then_inc(ib_ev, 1)
            for d in range(2):
                act.wait_ge(f_rdy, d + 1)
                nc.scalar.activation(lf[:, d], zf[:, d], ACT.Ln).then_inc(lf_rdy, 1)
            for d in range(2):
                act.wait_ge(b_rdy, d + 1)
                nc.scalar.activation(lf[:, d], bc[:, d], ACT.Exp)
                nc.scalar.activation(bc[:, d], bc[:, d], ACT.Exp, scale=-1.0).then_inc(e_rdy, 1)
            for h in range(HG):
                act.wait_ge(ho_mm, h + 1)
                if h >= 2:
                    act.wait_ge(hg_done, h - 1)
                nc.scalar.activation(o_b[:, h % 2], ps[:, 4 + h % 2, 0:SEQ], ACT.Copy)
                nc.scalar.activation(sq_b[:, h % 2], ps[:, 4 + h % 2, 0:SEQ], ACT.Square).then_inc(ho_ev, 1)
                act.wait_ge(hn_mm, h + 1)
                nc.scalar.activation(ir_b[:, h % 2], ps[:, 6, 0:SEQ], ACT.Sqrt, bias=eps_col, scale=1.0 / P).then_inc(hn_std, 1)
            act.wait_ge(hg_done, HG)
            for u in range(20):
                act.wait_ge(z2_mm, u + 1)
                src = ps[:, u % 6, :]
                if u < 14:
                    nc.scalar.activation(z2[:, 2 * u:2 * u + 2], src.rearrange("p (m t) -> p m t", m=2),
                                         ACT.Silu if u < 2 else ACT.Copy).then_inc(z2_ev, 1)
                else:
                    nc.scalar.activation(v2[:, (u - 14) // 2, u % 2], src, ACT.Copy).then_inc(z2_ev, 1)
            for u in range(13):
                if u < 12:
                    if u >= 2:
                        act.wait_ge(qn_mm, u - 1)
                    nc.scalar.activation(sq2[:, u % 2].rearrange("p (m t) -> p m t", m=2), z2[:, 4 + 2 * u:6 + 2 * u],
                                         ACT.Square).then_inc(qn_sq, 1)
                if u:
                    act.wait_ge(qn_mm, u)
                    if u >= 3:
                        act.wait_ge(qn_done, u - 2)
                    nc.scalar.activation(ir2[:, (u - 1) % 2], ps[:, 6 + (u - 1) % 2, :], ACT.Sqrt, bias=eps_col,
                                         scale=1.0 / HD).then_inc(qn_std, 1)
            for i in range(len(AT_UNITS) + 1):
                if i < len(AT_UNITS):
                    act.wait_ge(at_neg, i + 1)
                    if i >= 2:
                        act.wait_ge(at_t, i - 1)
                    src = ps[:, 2 * (i % 2):2 * (i % 2) + 2, :].rearrange("p b k -> p (b k)")[:, 0:768]
                    nc.scalar.activation(probs2[:, i % 2], src, ACT.Exp, scale=0.125, bias=stat2[:, 4 * (i % 16) + 1:4 * (i % 16) + 2],
                                         accum_out=stat2[:, 4 * (i % 16) + 2:4 * (i % 16) + 3]).then_inc(at_e, 1)
                if i:
                    u = i - 1
                    act.wait_ge(at_t, u + 1)
                    if u:
                        act.wait_ge(at_o, u)
                    src = ps[:, 4:6, :].rearrange("p b k -> p (b k)")[:, 0:768].rearrange("p (k q) -> p k q", q=P)
                    nc.scalar.activation(probsT2, src, ACT.Copy).then_inc(at_c, 1)

        @block.vector
        def _(dve):
            steps = [0]

            def link(ins):
                steps[0] += 1
                ins.then_inc(dve_step, 1)
                dve.wait_ge(dve_step, steps[0])

            def norm(i):
                a, b = NORM_COLS[i]
                r = inv_rms[:, 0:b - a]
                dve.wait_ge(nm_std, i + 1)
                link(nc.vector.reciprocal(r, r))
                for k in range(KT):
                    if i < 4:
                        nc.vector.tensor_tensor(XT[:, k, a:b], hT[:, k, a:b], r, ALU.mult).then_inc(nm_tmp, 1)
                    else:
                        g = sm[:, SM["final_g" if i == 4 else "norm_w2"]][:, k:k + 1]
                        nc.vector.scalar_tensor_tensor((hT if i == 4 else XT)[:, k, a:b], hT[:, k, a:b], g, r,
                                                       ALU.mult, ALU.mult).then_inc(nm_tmp, 1)

            def rank(src, out, q):
                bj = src.unsqueeze(2).broadcast_to([P, q, 4, 4])
                bi = src.unsqueeze(3).broadcast_to([P, q, 4, 4])
                gt = rt[:, 192:192 + 16 * q].rearrange("p (q i j) -> p q i j", q=q, i=4)
                eq = rt[:, 448:448 + 16 * q].rearrange("p (q i j) -> p q i j", q=q, i=4)
                tie = cst[:, CST["tie"]].unsqueeze(1).broadcast_to([P, q, 16])
                nc.vector.tensor_tensor(gt, bj, bi, ALU.is_gt)
                link(nc.vector.tensor_tensor(eq, bj, bi, ALU.is_equal))
                eqf = rt[:, 448:448 + 16 * q].rearrange("p (q x) -> p q x", q=q)
                link(nc.vector.tensor_tensor(eqf, eqf, tie, ALU.mult))
                link(nc.vector.tensor_tensor(eqf, eqf, rt[:, 192:192 + 16 * q].rearrange("p (q x) -> p q x", q=q), ALU.add))
                link(nc.vector.tensor_reduce(out, eq, AX.X, ALU.add))

            def router(layer):
                nt = 4 if layer == 0 else 2
                q = 4 * nt
                scores = rt[:, 64:64 + 16 * nt]
                biased = rt[:, 128:128 + 16 * nt]
                rk = rt[:, 704:704 + 4 * q]
                gs, grk, den = rt[:, 768:768 + q], rt[:, 800:800 + q], rt[:, 832:832 + nt]
                val = rt[:, 896:896 + 4 * q]
                v3 = lambda x: x.rearrange("p (q j) -> p q j", j=4)
                dve.wait_ge(rt_sig, layer + 1)
                link(nc.vector.tensor_tensor(biased.rearrange("p (t e) -> p t e", t=nt), scores.rearrange("p (t e) -> p t e", t=nt),
                                             sm[:, SM["router_b"]].unsqueeze(1).broadcast_to([P, nt, 16]), ALU.add))
                rank(v3(biased), v3(rk), q)
                link(nc.vector.tensor_scalar(rk, rk, 1.5, None, ALU.is_lt))
                link(nc.vector.tensor_tensor(val, rk, biased, ALU.mult))
                link(nc.vector.tensor_reduce(gs, v3(val), AX.X, ALU.add))
                rank(v3(gs), v3(grk), nt)
                link(nc.vector.tensor_scalar(grk, grk, 0.5, None, ALU.is_lt))
                nc.vector.tensor_tensor(v3(rk), v3(rk), grk.unsqueeze(2).broadcast_to([P, q, 4]), ALU.mult).then_inc(sel_rdy, 1)
                dve.wait_ge(sel_rdy, layer + 1)
                link(nc.vector.tensor_tensor(val, rk, scores, ALU.mult))
                link(nc.vector.tensor_reduce(den, val.rearrange("p (t e) -> p t e", t=nt), AX.X, ALU.add))
                link(nc.vector.reciprocal(den, den))
                nc.vector.tensor_tensor(rt[:, 0:16 * nt].rearrange("p (t e) -> p t e", t=nt), val.rearrange("p (t e) -> p t e", t=nt),
                                        den.unsqueeze(2).broadcast_to([P, nt, 16]), ALU.mult).then_inc(gate_ready, 1)
                dve.wait_ge(pos_mm, layer + 1)
                link(nc.vector.tensor_reduce(rt2[:, 448:449], ps[:, 5, 64:80], AX.X, ALU.max))
                nc.vector.tensor_copy(fullest[:, :], rt2[:, 448:449]).then_inc(full_rdy, 1)

            def routed(layer):
                steps.append(steps[0])
                for s_, n in ((gated_rdy, 64), (hid_rdy, 64), (dn_free, 128)):
                    dve.sem_inc(s_, n)
                nt = 4 if layer == 0 else 2
                c = EXPERTS * layer
                te = lambda x: x.rearrange("p (t e) -> p t e", t=nt)
                n16 = 16 * nt
                chosen, gates = rt[:, 704:704 + n16], rt[:, 0:n16]
                at, val, top = rt2[:, 0:n16], rt2[:, 64:64 + n16], rt2[:, 128:128 + n16]
                tmp, tmp2 = rt2[:, 192:192 + n16], rt2[:, 256:256 + n16]
                rmax, rsum, gmax, gmin = (rt2[:, 320 + 8 * j:320 + 8 * j + nt] for j in range(4))
                link(nc.vector.scalar_tensor_tensor(at, ps[:, 5, 0:n16], 1.0, chosen, ALU.add, ALU.mult))
                link(nc.vector.tensor_scalar(at, at, -1.0, None, ALU.add))
                iota = cst[:, CST["iota"]].unsqueeze(1).broadcast_to([P, EXPERTS, P])
                for t in range(nt):
                    last = nc.vector.tensor_tensor(slots[:, t], iota, at[:, 16 * t:16 * t + 16].unsqueeze(2).broadcast_to([P, EXPERTS, P]),
                                                   ALU.is_equal)
                last.then_inc(slots_rdy, 1)
                link(nc.vector.tensor_tensor(te(tmp), te(ps[:, 5, 0:n16]), cst[:, CST["row1"]].unsqueeze(1).broadcast_to([P, nt, 16]), ALU.add))
                link(nc.vector.tensor_tensor(val, tmp, chosen, ALU.mult))
                nc.vector.tensor_reduce(rsum, te(val), AX.X, ALU.add)
                link(nc.vector.tensor_reduce(rmax, te(val), AX.X, ALU.max))
                nc.vector.tensor_scalar(tok_row[:, 0:nt], rmax, -1.0, None, ALU.add)
                link(nc.vector.tensor_tensor(te(top), te(val), rmax.unsqueeze(2).broadcast_to([P, nt, 16]), ALU.is_equal))
                link(nc.vector.tensor_tensor(rsum, rsum, rmax, ALU.subtract))
                nc.vector.tensor_scalar(tok_row[:, 4:4 + nt], rsum, -1.0, None, ALU.add)
                link(nc.vector.tensor_tensor(tmp, top, gates, ALU.mult))
                link(nc.vector.tensor_tensor(tmp2, gates, tmp, ALU.subtract))
                nc.vector.tensor_reduce(gmax, te(tmp), AX.X, ALU.add)
                link(nc.vector.tensor_reduce(gmin, te(tmp2), AX.X, ALU.add))
                dve.wait_ge(ix_mm, layer + 1)
                pair = ps[:, 6, 0:32].rearrange("p (e h) -> p e h", h=2)
                link(nc.vector.tensor_copy(rt2[:, 384:416].rearrange("p (e h) -> p e h", h=2), pair))
                pair = rt2[:, 384:416].rearrange("p (e h) -> p e h", h=2)
                nc.vector.scalar_tensor_tensor(slot_tok[:, :], pair[:, :, 1], float(P), pair[:, :, 0], ALU.mult,
                                               ALU.add).then_inc(ix_rdy, 1)

                def copy_rows(e, j):
                    dve.wait_ge(f_x, e + (c + 1))
                    nc.vector.tensor_copy(xeT[:, j, 4:8], ps[:, 1, :].rearrange("p (k s) -> p k s", k=4)).then_inc(f_xd, 1)

                def turn(e, j, first, last_e, half_e):
                    dve.wait_ge(f_u3, e + (c + 1))
                    dve.wait_ge(f_s, e + (c + 1))
                    nc.vector.tensor_tensor(eh[:, j], es[:, j], ps[:, 3, :], ALU.mult).then_inc(f_h, 1)
                    if not last_e:
                        copy_rows(e + 1, 1 - j)
                    dve.wait_ge(f_ht, e + (c + 1))
                    nc.vector.tensor_copy(ehT[:, j], ps[:, 4, :].rearrange("p (k s) -> p k s", k=4)).then_inc(f_he, 1)
                    dve.wait_ge(f_d, e * 2 + (2 * c + 2))
                    if not first:
                        dve.wait_ge(y_st[layer][j], half_e * 16)
                    nc.vector.tensor_copy(ey[:, j, 512:1024], ps[:, 6, :]).then_inc(f_yd, 1)

                copy_rows(0, 0)
                for j in range(2):
                    turn(j, j, True, False, 0)
                with dve.Fori(1, EXPERTS // 2 - 1) as i:
                    for j in range(2):
                        turn(i * 2 + j, j, False, False, i)
                for j in range(2):
                    turn(EXPERTS - 2 + j, j, False, j == 1, EXPERTS // 2 - 1)
                dve.wait_ge(c_ld[layer], 32 * nt)
                for t in range(nt):
                    link(nc.vector.tensor_scalar(cg[:, 0, t], cg[:, 0, t], gmax[:, t:t + 1], None, ALU.mult))
                    nc.vector.scalar_tensor_tensor(cg[:, 0, t], cg[:, 1, t], gmin[:, t:t + 1], cg[:, 0, t], ALU.mult,
                                                   ALU.add).then_inc(f_cmb, 1)
                t0 = 0 if layer == 0 else SEQ
                for m in range(KT):
                    dve.wait_ge(f_c, KT * layer + m + 1)
                    for seg in range(t0 // SEQ, 2):
                        part = hT[:, m, seg * SEQ:(seg + 1) * SEQ]
                        last = nc.vector.scalar_tensor_tensor(part, ps[:, m % 2, seg * SEQ - t0:(seg + 1) * SEQ - t0],
                                                              modc[:, layer, 40 + m, seg:seg + 1], part, ALU.mult, ALU.add)
                    last.then_inc(f_cT if m < KT - 1 else res_done, 1)
                dve.sem_inc(f_cT, 1)
                steps.append(steps[0])

            def dense(layer):
                for s_, n in ((f_xd, 16), (f_h, 16), (f_he, 16), (f_yd, 16), (f_cT, 8), (f_cmb, 4 if layer == 0 else 2),
                              (ix_rdy, 1), (slots_rdy, 1)):
                    dve.sem_inc(s_, n)
                after, steps[0] = steps.pop(), steps.pop()
                experts(layer)
                dve.sem_inc(dve_step, after - steps[0])
                steps[0] = after

            def experts(layer):
                t0, n = (0, T) if layer == 0 else (SEQ, SEQ)
                u0, d0 = 4 * EXPERTS * layer, 8 * EXPERTS * layer
                dc = (8 * EXPERTS + 2) * layer + 2
                dve.wait_ge(x_st, 64 if layer == 0 else 96)
                for k in range(KT):
                    last = nc.vector.memset(acc[:, k, 0:n], 0.0)
                link(last)
                dve.wait_ge(gb_ev, EXPERTS * (layer + 1))
                with dve.Fori(0, EXPERTS) as e:
                    for m in range(4):
                        dve.wait_ge(up3, e * 4 + (u0 + m + 1))
                        nc.vector.tensor_tensor(gated[:, m % 2, 0:n], ps[:, 2 * (m % 2) + 1, 0:n],
                                                Gt[:, bass.ds(e, 1), 0:n].rearrange("p e t -> p (e t)"), ALU.mult).then_inc(gated_rdy, 1)
                        dve.wait_ge(gated_rdy, e * 4 + (u0 + m + 1))
                        dve.wait_ge(silu_rdy, e * 4 + (u0 + m + 1))
                        nc.vector.tensor_tensor(hid[:, m, 0:n], gated[:, m % 2, 0:n], silu_b[:, m % 2, 0:n],
                                                ALU.mult).then_inc(hid_rdy, 1)
                    for m in range(8):
                        dve.wait_ge(dn_mm, e * 8 + (d0 + m + 1))
                        nc.vector.tensor_tensor(acc[:, m, 0:n], acc[:, m, 0:n], ps[:, 4 + m % 2, 0:n], ALU.add).then_inc(dn_free, 1)
                dve.wait_ge(dn_free, dc + 8 * EXPERTS)
                for m in range(KT):
                    for seg in range(t0 // SEQ, 2):
                        part = hT[:, m, seg * SEQ:(seg + 1) * SEQ]
                        last = nc.vector.scalar_tensor_tensor(part, acc[:, m, seg * SEQ - t0:(seg + 1) * SEQ - t0],
                                                              modc[:, layer, 40 + m, seg:seg + 1], part, ALU.mult, ALU.add)
                last.then_inc(res_done, 1)

            nc.vector.memset(tick[:, :], 0.0)
            nc.vector.memset(eps_col, EPS).then_inc(tick_ready, 1)
            dve.wait_ge(ld_ca, 16)
            dve.wait_ge(ld_rpb, 16 * ROWS * ROWS)
            for q in range(2):
                b = bias_na[:, q].rearrange("p h (r c) -> p (h r) c", c=GRID_W)
                shape = [P, NA_H * ROWS, GRID_W]
                link(nc.vector.tensor_tensor(b, b, ca[:, CA["keep8"]].unsqueeze(1).broadcast_to(shape), ALU.mult))
                last = nc.vector.tensor_tensor(b, b, ca[:, CA["shut8"]].unsqueeze(1).broadcast_to(shape), ALU.add)
            last.then_inc(bias_ready, 1)
            dve.wait_ge(ld_sm, 16)
            for layer in range(2):
                dve.wait_ge(w_free, 12 * (layer + 1))
                link(nc.vector.tensor_tensor(
                    modc[:, layer], ps[:, layer, 0:96].rearrange("p (m s) -> p m s", s=2),
                    sm[:, SM["ada_b"]][:, 48 * layer:48 * (layer + 1)].unsqueeze(2).broadcast_to([P, 48, 2]), ALU.add))
                for j in range(2):
                    n = 2 * layer + j
                    last = nc.vector.scalar_tensor_tensor(
                        gains[:, n], modc[:, layer, 24 * j + 8:24 * j + 16], 1.0,
                        sm[:, SM["norm_g"]][:, KT * n:KT * (n + 1)].unsqueeze(2).broadcast_to([P, KT, 2]), ALU.add, ALU.mult)
                last.then_inc(mod_ready, 1)
            dve.wait_ge(ld_cst, 16)
            nc.vector.tensor_copy(tok_bf[:, :], cst[:, CST["tok"]])
            dve.wait_ge(ld_h, 16)
            norm(0)

            for i in range(len(NA_UNITS) + 1):
                if i < len(NA_UNITS):
                    seg, h, q = NA_UNITS[i]
                    s = ps[:, i % 3, 0:(T if seg else SEQ)]
                    dve.wait_ge(na_s, i + 1)
                    link(nc.vector.tensor_reduce(stat[:, 4 * i:4 * i + 1], s, AX.X, ALU.max))
                    nc.vector.tensor_scalar(stat[:, 4 * i + 1:4 * i + 2], stat[:, 4 * i:4 * i + 1], -0.125, None,
                                            ALU.mult).then_inc(na_neg, 1)
                if i:
                    u = i - 1
                    nk = T if NA_UNITS[u][0] else SEQ
                    dve.wait_ge(na_e, u + 1)
                    link(nc.vector.reciprocal(stat[:, 4 * u + 3:4 * u + 4], stat[:, 4 * u + 2:4 * u + 3]))
                    nc.vector.tensor_scalar(probs0[:, u % 2, 0:nk], probs0[:, u % 2, 0:nk], stat[:, 4 * u + 3:4 * u + 4],
                                            None, ALU.mult).then_inc(na_p, 1)
            for m in range(8):
                dve.wait_ge(mo_mm, m + 1)
                for seg in range(2):
                    part = hT[:, m, seg * SEQ:(seg + 1) * SEQ]
                    last = nc.vector.scalar_tensor_tensor(part, ps[:, m % 4, seg * SEQ:(seg + 1) * SEQ],
                                                          modc[:, 0, 16 + m, seg:seg + 1], part, ALU.mult, ALU.add)
                last.then_inc(mo_ev if m < 7 else res_done, 1)
            norm(1)
            router(0)
            by_load(dve, 0, routed, dense)

            norm(2)
            dve.wait_ge(lg_ready, 1)
            nc.vector.tensor_scalar(dec_t[:, 8:16], dec_t[:, 0:8], -1.0, 1.0, ALU.mult, ALU.add).then_inc(lg_ready, 1)
            dve.wait_ge(lg_ready, 3)
            link(nc.vector.tensor_scalar(dec_t[:, 24:32], dec_t[:, 8:16], -1.0, 1.0, ALU.mult, ALU.add))
            link(nc.vector.tensor_scalar(dec_t[:, 24:32], dec_t[:, 24:32], 1e-30, None, ALU.max))
            link(nc.vector.reciprocal(dec_t[:, 32:40], dec_t[:, 24:32]))
            link(nc.vector.tensor_tensor(dec_t[:, 40:48], dec_t[:, 32:40], dec_t[:, 0:8], ALU.mult))
            link(nc.vector.tensor_tensor(dec_t[:, 48:56], dec_t[:, 40:48], dec_t[:, 16:24], ALU.mult))
            dve.wait_ge(ld_cb, 16)
            cos = cb[:, CB["rcos"]].unsqueeze(1).broadcast_to([P, 4, SEQ])
            sin = cb[:, CB["rsin"]].unsqueeze(1).broadcast_to([P, 4, SEQ])
            for n, (x, units) in enumerate(((qR, 8), (kR[:, :, :, LAT], 16))):
                dve.wait_ge(rp_ev, units)
                x1, x2 = x[:, :, 0], x[:, :, 1]
                nc.vector.tensor_tensor(rope_t[:, 0], x2, sin, ALU.mult)
                link(nc.vector.tensor_tensor(rope_t[:, 1], x1, sin, ALU.mult))
                nc.vector.tensor_tensor(x1, x1, cos, ALU.mult)
                link(nc.vector.tensor_tensor(x2, x2, cos, ALU.mult))
                nc.vector.tensor_tensor(x1, x1, rope_t[:, 0], ALU.subtract)
                nc.vector.tensor_tensor(x2, x2, rope_t[:, 1], ALU.add).then_inc(rope_done, 1)
                dve.wait_ge(rope_done, n + 1)

            def decay_arg(h):
                lat = decayT[:, h % 2, 2:4].rearrange("p k t -> p (k t)")
                link(nc.vector.tensor_scalar(lat, cb[:, CB["lat_f"]], dec_t[:, 48 + h:49 + h], None, ALU.mult))
                nc.vector.scalar_tensor_tensor(lat, cb[:, CB["lat_b"]], dec_t[:, 52 + h:53 + h], lat, ALU.mult,
                                               ALU.add).then_inc(dk_arg, 1)

            decay_arg(0)
            for h in range(RET_H):
                if h + 1 < RET_H:
                    decay_arg(h + 1)
                dve.wait_ge(dk_exp, h + 1)
                ctxd = decayT[:, h % 2, 0:2].rearrange("p k t -> p (k t)")
                latd = decayT[:, h % 2, 2:4].rearrange("p k t -> p (k t)")
                nc.vector.tensor_tensor(ctxd, ctxd, rope_t[:, h % 2, 0:2].rearrange("p k t -> p (k t)"), ALU.add)
                link(nc.vector.tensor_tensor(latd, latd, cb[:, CB["twice"]], ALU.mult))
                dve.wait_ge(rs_mm, h + 1)
                if h >= 2:
                    dve.wait_ge(ro_mm, h - 1)
                for j in range(2):
                    nc.vector.scalar_tensor_tensor(
                        scoreT[:, h % 2, 2 * j:2 * j + 2].rearrange("p k t -> p (k t)"), ps[:, j, :], 0.0625,
                        (ctxd, latd)[j], ALU.mult, ALU.mult).then_inc(rs_rdy, 1)
                dve.wait_ge(rn_std, h + 1)
                link(nc.vector.reciprocal(irR, irR))
                g = gR[:, 4 * h:4 * h + 4]
                link(nc.vector.tensor_tensor(g, g, irR.unsqueeze(1).broadcast_to([P, 4, SEQ]), ALU.mult))
                nc.vector.tensor_tensor(g, g, oR, ALU.mult).then_inc(rn_rdy, 1)
            for m in range(8):
                dve.wait_ge(y_mm, m + 1)
                nc.vector.scalar_tensor_tensor(hT[:, m, LAT], ps[:, m % 4, 0:SEQ], modc[:, 1, 16 + m, 1:2], hT[:, m, LAT],
                                               ALU.mult, ALU.add).then_inc(y_ev if m < 7 else res_done, 1)
            norm(3)
            router(1)
            by_load(dve, 1, routed, dense)

            norm(4)
            dve.wait_ge(nm_tmp, 5 * KT)
            norm(5)
            a = sm[:, SM["lb"]].rearrange("p (d l h) -> p l d h", d=2, l=2)
            v16 = lambda at: lbt[:, at:at + 16].rearrange("p (d h) -> p d h", d=2)
            link(nc.vector.tensor_tensor(v16(0), a[:, 0], a[:, 1], ALU.max))
            nc.vector.tensor_tensor(v16(16), a[:, 0], v16(0), ALU.subtract)
            nc.vector.tensor_tensor(v16(32), a[:, 1], v16(0), ALU.subtract).then_inc(lb_s, 1)
            dve.wait_ge(lb_e, 1)
            link(nc.vector.tensor_tensor(v16(80), v16(48), v16(64), ALU.add))
            link(nc.vector.reciprocal(v16(96), v16(80)))
            link(nc.vector.tensor_tensor(v16(112), v16(48), v16(96), ALU.mult))
            link(nc.vector.tensor_scalar(tiny[:, 0:16], lbt[:, 112:128], -1.0, 1.0, ALU.mult, ALU.add))
            for d in range(2):
                dve.wait_ge(z1_ev, 6 + 4 * (d + 1))
                for h in range(HG):
                    at = 8 * d + h
                    last = nc.vector.tensor_scalar(zf[:, d, h], zf[:, d, h], tiny[:, at:at + 1], lbt[:, 112 + at:113 + at],
                                                   ALU.mult, ALU.add)
                last.then_inc(f_rdy, 1)
            dve.wait_ge(ld_cc, 16)
            link(nc.vector.memset(toep, 0.0))
            dve.wait_ge(tz_mm, 1)
            nc.vector.scalar_tensor_tensor(toep[0:24, 0:511], ps[0:24, 6, 0:511], 8.0, cc[0:24, CC["shut8"]],
                                           ALU.mult, ALU.add).then_inc(tz_rdy, 1)
            for d in range(2):
                dve.wait_ge(lf_rdy, d + 1)
                flat = zf[:, d].rearrange("p h t -> p (h t)")
                nc.vector.tensor_scalar(flat, flat, -1.0, 1.0, ALU.mult, ALU.add)
                step = 1 if d == 0 else -1
                for h in range(HG):
                    last = nc.vector.tensor_tensor_scan(bc[:, d, h, ::step], cc[:, CC["runs"]], lf[:, d, h, ::step], 0.0,
                                                        ALU.mult, ALU.add)
                last.then_inc(b_rdy, 1)
            for d in range(2):
                dve.wait_ge(e_rdy, d + 1)
                dve.wait_ge(z1_ev, 6 + 12)
                end = CH - 1 if d == 0 else 0
                link(nc.vector.tensor_copy(decs[:, d], lf[:, d].rearrange("p h (c t) -> p h c t", t=CH)[:, :, :, end]))
                nc.vector.tensor_tensor(lf[:, d], lf[:, d], q_b, ALU.mult)
                link(nc.vector.tensor_tensor(bc[:, d], bc[:, d], zf[:, d], ALU.mult))
                link(nc.vector.memset(zf[:, d], 0.0))

            def gla_keys(h):
                for d in range(2):
                    if h:
                        dve.wait_ge(K_used, 2 * (h - 1) + d + 1)
                    K = zf[:, d]
                    diag = bass.AP(tensor=arena, offset=d * 2048, ap=[[30400, P], [SEQ + CH, NCH], [1, CH]])
                    link(nc.vector.tensor_copy(diag, bc[:, d, h].rearrange("p (c t) -> p c t", t=CH)))
                    for c in range(1, NCH):
                        if d == 0:
                            to, of = K[:, c, 0:CH * c], K[:, c - 1, 0:CH * c]
                            dec = decs[:, d, h, c - 1:c]
                        else:
                            to, of = K[:, NCH - 1 - c, CH * (NCH - c):SEQ], K[:, NCH - c, CH * (NCH - c):SEQ]
                            dec = decs[:, d, h, NCH - c:NCH - c + 1]
                        ins = nc.vector.tensor_scalar(to, of, dec, None, ALU.mult)
                        if c < NCH - 1:
                            link(ins)
                        else:
                            ins.then_inc(K_rdy, 1)

            gla_keys(0)
            for h in range(HG):
                if h + 1 < HG:
                    gla_keys(h + 1)
                dve.wait_ge(K_used, 2 * h + 2)
                if h >= 2:
                    dve.wait_ge(ho_mm, h - 1)
                F, B = ps[:, 2 * (h % 2)], ps[:, 2 * (h % 2) + 1]
                pt = pt_b[:, h % 2]
                nc.vector.tensor_tensor(mrg[:, 0:P], F[:, 0:P], cc[:, CC["mask_f"]], ALU.mult)
                nc.vector.tensor_tensor(mrg[:, P:2 * P], F[:, SEQ:SEQ + P], cc[:, CC["mask_f"]], ALU.mult)
                nc.vector.tensor_tensor(pt[:, 0, 0:P], B[:, SEQ:SEQ + P], cc[:, CC["mask_b"]], ALU.mult)
                nc.vector.tensor_tensor(pt[:, 1, P:SEQ], B[:, P:SEQ], cc[:, CC["mask_b"]], ALU.mult)
                nc.vector.tensor_copy(pt[:, 0, P:SEQ], F[:, P:SEQ])
                link(nc.vector.tensor_copy(pt[:, 1, 0:P], B[:, 0:P]))
                nc.vector.tensor_tensor(pt[:, 0, 0:P], pt[:, 0, 0:P], mrg[:, 0:P], ALU.add)
                nc.vector.tensor_tensor(pt[:, 1, P:SEQ], pt[:, 1, P:SEQ], mrg[:, P:2 * P], ALU.add).then_inc(pt_rdy, 1)
                dve.wait_ge(hn_std, h + 1)
                r = ir_b[:, h % 2]
                link(nc.vector.reciprocal(r, r))
                link(nc.vector.scalar_tensor_tensor(o_b[:, h % 2], o_b[:, h % 2], sm[:, SM["hgw"]], r, ALU.mult, ALU.mult))
                nc.vector.tensor_tensor(g_b[:, h], g_b[:, h], o_b[:, h % 2], ALU.mult).then_inc(hg_done, 1)

            for u in range(12):
                dve.wait_ge(qn_std, u + 1)
                r = ir2[:, u % 2]
                link(nc.vector.reciprocal(r, r))
                w = sm[:, SM["qn" if u % 4 < 2 else "kn"]][:, u // 4:u // 4 + 1]
                z = z2[:, 4 + 2 * u:6 + 2 * u]
                nc.vector.scalar_tensor_tensor(z, z, w, r.rearrange("p (m t) -> p m t", m=2), ALU.mult, ALU.mult).then_inc(qn_done, 1)
            for i in range(len(AT_UNITS) + 2):
                if i < len(AT_UNITS):
                    h, q = AT_UNITS[i]
                    s = ps[:, 2 * (i % 2):2 * (i % 2) + 2, :].rearrange("p b k -> p (b k)")[:, 0:768]
                    dve.wait_ge(at_s, i + 1)
                    link(nc.vector.tensor_reduce(stat2[:, 4 * i:4 * i + 1], s, AX.X, ALU.max))
                    nc.vector.tensor_scalar(stat2[:, 4 * i + 1:4 * i + 2], stat2[:, 4 * i:4 * i + 1], -0.125, None,
                                            ALU.mult).then_inc(at_neg, 1)
                if 0 <= i - 1 < len(AT_UNITS):
                    u = i - 1
                    dve.wait_ge(at_e, u + 1)
                    link(nc.vector.reciprocal(stat2[:, 4 * u + 3:4 * u + 4], stat2[:, 4 * u + 2:4 * u + 3]))
                    nc.vector.tensor_scalar(probs2[:, u % 2], probs2[:, u % 2], stat2[:, 4 * u + 3:4 * u + 4], None,
                                            ALU.mult).then_inc(at_p, 1)
                if i >= 2:
                    u = i - 2
                    h, q = AT_UNITS[u]
                    dve.wait_ge(at_o, u + 1)
                    part = z2[half(h), h // 2, q * P:(q + 1) * P]
                    nc.vector.tensor_tensor(part, part, ps[half(h), 6 + u % 2, 0:P], ALU.mult).then_inc(at_ev, 1)
            for m in range(8):
                dve.wait_ge(ya_mm, m + 1)
                nc.vector.tensor_tensor(zgA[:, m], zgA[:, m], ps[:, m % 4, 0:SEQ], ALU.mult).then_inc(ya_ev, 1)
            dve.wait_ge(ya_ev, KT)
            for m in range(8):
                dve.wait_ge(yb_mm, m + 1)
                link(nc.vector.tensor_tensor(zgB[:, m], zgB[:, m], ps[:, 4 + m % 2, 0:SEQ], ALU.mult))
                nc.vector.tensor_tensor(zgA[:, m], zgA[:, m], zgB[:, m], ALU.add).then_inc(yb_ev, 1)
            for m in range(8):
                dve.wait_ge(yo_mm, m + 1)
                nc.vector.tensor_tensor(XT[:, m, LAT], hT[:, m, LAT], ps[:, m % 4, 0:SEQ], ALU.add).then_inc(yo_ev, 1)


def columns_of(v):
    return np.ascontiguousarray(v.reshape(-1, P).T)


def weight_blocks(w, rows, cols):
    k, m = w.shape
    b = w.reshape(k // rows, rows // P, P, m // cols, cols)
    return b.transpose(0, 3, 2, 1, 4).reshape(-1, P, rows // P * cols)


def kernel(**inputs):
    import concourse.bacc as bacc
    from concourse.bass_utils import run_bass_kernel_spmd as run

    a = {k: np.asarray(v) for k, v in inputs.items()}
    blocks = []
    for layer in range(2):
        blocks.append(weight_blocks(a["ada_w"][layer], D, 512))
    blocks.append(weight_blocks(a["mixab_w_in"][0], D, 512))
    blocks.append(weight_blocks(a["mixab_w_out"][0], D, 512))

    def expert_blocks(layer):
        w1 = a["moe_w1"][layer].reshape(EXPERTS, KT, P, 512).transpose(0, 2, 1, 3).reshape(EXPERTS, P, BLK)
        w3 = a["moe_w3"][layer].reshape(EXPERTS, KT, P, 512).transpose(0, 2, 1, 3).reshape(EXPERTS, P, BLK)
        w2 = a["moe_w2"][layer].reshape(EXPERTS, 4, P, D).transpose(0, 2, 1, 3).reshape(EXPERTS, P, BLK)
        return np.stack([w1, w3, w2], 1).reshape(3 * EXPERTS, P, BLK)

    blocks.append(expert_blocks(0))
    rw = a["ret_w_in"][0]
    qk = rw[:, :2048].reshape(D, 8, 2, 2, 64).transpose(0, 1, 3, 2, 4).reshape(D, 2048)
    blocks.append(weight_blocks(qk, D, 512))
    blocks.append(weight_blocks(rw[:, 2048:], D, 512))
    blocks.append(weight_blocks(a["ret_w_out"][0], 2048, 256))
    blocks.append(expert_blocks(1))
    w2 = weight_blocks(a["w_in_2"][0], D, 512)
    order = [12, 13, 14, 15, 10, 11, 18, 19, 20, 21, 22, 23, 16, 17, 9, 0, 1, 3, 4, 6, 7, 2, 5, 8]
    blocks.append(w2[order])
    blocks.append(weight_blocks(a["w_proj_a_2"][0], 512, D))
    blocks.append(weight_blocks(a["w_proj_b_2"][0], D, 512))
    blocks.append(weight_blocks(a["w_out_2"][0], D, 512))
    w_all = np.concatenate(blocks)

    h0 = np.concatenate([a["ctx"][0], a["x"][0]]).T.reshape(KT, P, T).transpose(1, 0, 2)
    rows = lambda v: np.broadcast_to(v.reshape(1, -1), (P, v.size))
    c2 = np.stack([columns_of(a["c_ctx"]), columns_of(a["c"][0])], -1).reshape(P, 2 * KT)
    rel = np.zeros((P, 24), a["rel_bias_2"].dtype)
    rel[:BUCKETS] = a["rel_bias_2"]
    lb = np.concatenate([columns_of(a[n][r]) for n in ("lb_fwd_2", "lb_bwd_2") for r in range(2)], 1)
    smalls = np.concatenate([
        c2, columns_of(a["ada_b"].reshape(-1)), columns_of(a["norm_g"].reshape(-1)), columns_of(a["final_norm_g"]),
        columns_of(a["norm_w_2"].reshape(-1)),
        a["router_w"].reshape(KT, P, 16).transpose(1, 0, 2).reshape(P, KT * 16), rows(a["router_b"]),
        rows(a["ret_decay"]), np.tile(a["q_norm_w_2"][0].T, (2, 1)), np.tile(a["k_norm_w_2"][0].T, (2, 1)), lb,
        a["hg_norm_w_2"].reshape(P, 1), rel], 1)
    assert w_all.shape[0] == N_BLK and smalls.shape[1] == SM_N

    arrays = {"w_all": w_all, "h0": h0, "smalls": smalls, "rpb": a["na_rpb"][0]}
    arrays.update({k + "_d": v for k, v in constants().items()})
    arrays = {k: np.ascontiguousarray(v) for k, v in arrays.items()}
    nc = bacc.Bacc("TRN2", target_bir_lowering=False, num_devices=1)
    args = {k: nc.dram_tensor(k, v.shape, F32, kind="ExternalInput").ap() for k, v in arrays.items()}
    args["toep_d"] = nc.dram_tensor("toep_d", (24, 512), F32, kind="Internal").ap()
    args["xtok_d"] = nc.dram_tensor("xtok_d", (T, D), F32, kind="Internal").ap()
    args["y_d"] = nc.dram_tensor("y_d", (EXPERTS * P, D), F32, kind="Internal").ap()
    args["out_d"] = nc.dram_tensor("out_d", (P, KT, SEQ), F32, kind="ExternalOutput").ap()
    build(nc, **args)
    r = run(nc, [arrays], core_ids=[0])
    return r.results[0]["out_d"].transpose(1, 0, 2).reshape(D, SEQ).T[None]
```

```python
from contextlib import ExitStack

import numpy as np
import concourse.bass as bass
from concourse import mybir

F32 = mybir.dt.float32
BF16 = mybir.dt.bfloat16
F32R = mybir.dt.float32r
I32 = mybir.dt.int32
U32 = mybir.dt.uint32
ALU = mybir.AluOpType
ACT = mybir.ActivationFunctionType
AX = mybir.AxisListType

P = 128
D = 1024
KT = D // P
SEQ = 256
T = 2 * SEQ
CTX, LAT = slice(0, SEQ), slice(SEQ, T)
SLOTS = 3
BLK = 4096
BIG = 1e30
EPS = 1e-6

GRID_W = 64
ROWS = SEQ // GRID_W
NA_H = 12
NA_KH, NA_KW = 8, 16
RPB_W = 2 * NA_KW - 1
RPB_HEAD = (2 * NA_KH - 1) * RPB_W
HD = 64

RET_H = 4
EXPERTS = 16

AT_H = 8
AT_G = 3
GROUPS = ((128, 1), (512, 4), (2048, 16))
BUCKETS = 32
HG = 8
CH = 32
NCH = SEQ // CH

B_ADA = 0
B_MIX = B_ADA + 24
B_MIXO = B_MIX + 5
B_MOE0 = B_MIXO + 2
B_RET = B_MOE0 + 48
B_RETO = B_RET + 12
B_MOE1 = B_RETO + 4
B_Z1 = B_MOE1 + 48
B_IB = B_Z1 + 12
B_Z2 = B_IB + 2
B_V2 = B_Z2 + 7
B_PA = B_V2 + 3
B_PB = B_PA + 1
B_WO = B_PB + 2
N_BLK = B_WO + 2



def columns(*parts):
    at, out = 0, {}
    for name, n in parts:
        out[name] = slice(at, at + n)
        at += n
    return out, at


CST, CST_N = columns(("ident", P), ("ones", P), ("ones64", P), ("flip", P), ("flip64", P), ("tri", P), ("iota", P), ("tie", 16), ("tok", 8), ("row1", 16))
CA, CA_N = columns(("dft64", 2 * P), ("cos", 2 * SEQ), ("msin", 2 * SEQ), ("keep8", GRID_W), ("shut8", GRID_W))
CB, CB_N = columns(("rcos", SEQ), ("rsin", SEQ), ("ctx_f", 2 * SEQ), ("ctx_b", 2 * SEQ), ("lat_f", 2 * SEQ),
                   ("lat_b", 2 * SEQ), ("twice", 2 * SEQ))
CC, CC_N = columns(("runs", SEQ), ("mask_f", P), ("mask_b", P), ("onehot", 511), ("shut8", 511))
SM, SM_N = columns(("c2", 2 * KT), ("ada_b", 96), ("norm_g", 4 * KT), ("final_g", KT), ("norm_w2", KT),
                   ("router_w", KT * 16), ("router_b", 16), ("decay", 8), ("qn", 3), ("kn", 3), ("lb", 32),
                   ("hgw", 1), ("rel_bias", 24))


def t5_bucket(rel):
    half = BUCKETS // 2
    exact = half // 2
    n = np.abs(rel)
    large = exact + (np.log(np.maximum(n, 1) / exact) / np.log(1024 / exact) * (half - exact)).astype(np.int32)
    return np.where(rel > 0, half, 0) + np.where(n < exact, n, np.minimum(large, half - 1))


def constants():
    f = np.float32
    i128 = np.arange(P)
    cst = np.zeros((P, CST_N), f)
    cst[:, CST["ident"]] = np.eye(P)
    cst[:, CST["ones"]] = 1
    same64 = i128[:, None] // HD == i128[None] // HD
    cst[:, CST["ones64"]] = same64
    cst[:, CST["flip"]] = np.eye(P)[::-1]
    cst[:, CST["flip64"]] = same64 * (i128[:, None] % HD + i128[None] % HD == HD - 1)
    cst[:, CST["tri"]] = i128[:, None] < i128[None]
    cst[:, CST["iota"]] = i128[None]
    cst[:, CST["tok"]] = np.stack([np.tile(i128[:, None], (1, 4)), np.tile(np.arange(4)[None], (P, 1))], -1).reshape(P, 8)
    cst[:, CST["row1"]] = P * np.arange(EXPERTS)[None] + 1
    cst[:, CST["tie"]] = (np.arange(4)[None, :] < np.arange(4)[:, None]).reshape(1, 16)

    ca = np.zeros((P, CA_N), f)
    w64 = 2 * np.pi * np.outer(np.arange(64), np.arange(64)) / 64
    same = (i128[:, None] // 64 == i128[None] // 64)
    ca[:, CA["dft64"]] = np.concatenate([np.tile(np.cos(w64), (2, 2)) * same, np.tile(np.sin(w64), (2, 2)) * same], 1)
    w256 = 2 * np.pi * (np.outer(np.arange(256), np.arange(256)) % 256) / 256
    tiles = lambda m: m.reshape(2, P, SEQ).transpose(1, 0, 2).reshape(P, 2 * SEQ)
    ca[:, CA["cos"]] = tiles(np.cos(w256) / 128)
    ca[:, CA["msin"]] = tiles(-np.sin(w256) / 128)
    qc = (GRID_W - 1 - i128 % GRID_W)[:, None]
    kc = np.arange(GRID_W)[None]
    ws = np.clip(qc - NA_KW // 2, 0, GRID_W - NA_KW)
    inside = (kc >= ws) & (kc < ws + NA_KW)
    ca[:, CA["keep8"]] = inside * 8.0
    ca[:, CA["shut8"]] = np.where(inside, 0.0, -8.0 * BIG)

    cb = np.zeros((P, CB_N), f)
    t = np.arange(SEQ)
    inv = f(10000.0) ** (-np.arange(64, dtype=f) / f(64))
    ang = np.concatenate([inv[:, None] * (t // GRID_W).astype(f)[None], inv[:, None] * (t % GRID_W).astype(f)[None]], 0)
    cb[:, CB["rcos"]] = np.cos(ang.astype(f))
    cb[:, CB["rsin"]] = np.sin(ang.astype(f))
    m, n = np.arange(SEQ)[:, None], np.arange(SEQ)[None]
    cb[:, CB["ctx_f"]] = tiles(SEQ + n - m)
    cb[:, CB["ctx_b"]] = tiles(SEQ - n + m)
    cb[:, CB["lat_f"]] = tiles(np.maximum(n - m, 0))
    cb[:, CB["lat_b"]] = tiles(np.maximum(m - n, 0))
    cb[:, CB["twice"]] = tiles(1.0 + (m == n))

    cc = np.zeros((P, CC_N), f)
    cc[:, CC["runs"]] = (t % CH != 0)
    chunk = i128[:, None] // CH == i128[None] // CH
    cc[:, CC["mask_f"]] = (chunk & (i128[:, None] <= i128[None])) | (i128[:, None] // CH < i128[None] // CH)
    cc[:, CC["mask_b"]] = (chunk & (i128[:, None] >= i128[None])) | (i128[:, None] // CH > i128[None] // CH)
    delta = np.arange(-255, 256)
    for g, (window, dil) in enumerate(GROUPS):
        cc[g * AT_H:(g + 1) * AT_H, CC["shut8"]] = np.where(
            (delta % dil == 0) & (np.abs(delta) <= (window // 2) // dil * dil), 0.0, -8.0 * BIG)
    cc[:BUCKETS, CC["onehot"]] = t5_bucket(delta)[None] == np.arange(BUCKETS)[:, None]

    sel = np.zeros((EXPERTS, EXPERTS, P), f)
    sel[np.arange(EXPERTS), np.arange(EXPERTS)] = 1
    return dict(cst=cst, ca=ca, cb=cb, cc=cc, sel=sel.reshape(EXPERTS, EXPERTS * P))


def build(nc, w_all, h0, smalls, rpb, cst_d, ca_d, cb_d, cc_d, sel_d, toep_d, xtok_d, y_d, out_d):
    ctx = ExitStack()
    with ctx:
        def sb(name, cols):
            return ctx.enter_context(nc.sbuf_tensor(name, [P, cols], F32))

        def sem(name):
            return ctx.enter_context(nc.semaphore(name))

        ps = ctx.enter_context(nc.psum_tensor("ps", [P, 8, 512], F32))

        ring = sb("ring", SLOTS * BLK)
        hT = sb("hT", KT * T)[:, :].rearrange("p (k t) -> p k t", k=KT)
        XT = sb("XT", KT * T)[:, :].rearrange("p (k t) -> p k t", k=KT)
        cst = sb("cst", CST_N)
        sm = sb("sm", SM_N)
        c2s = sb("c2s", 2 * KT)
        modc = sb("modc", 2 * 96)[:, :].rearrange("p (l m s) -> p l m s", l=2, s=2)
        gains = sb("gains", 4 * 2 * KT)[:, :].rearrange("p (n m s) -> p n m s", n=4, s=2)
        inv_rms = sb("inv_rms", T)
        tiny = sb("tiny", 64)
        eps_col = tiny[:, 32:33]
        tick = ctx.enter_context(nc.sbuf_tensor("tick", [P, 32], mybir.dt.bfloat16))
        with nc.sbuf_tensor("arena", [P, 30400], F32) as arena:
            pass
        lower = ctx.enter_context(nc.sbuf_tensor("lower", [P, 16064], F32))
        w_hi, w_lo = (ctx.enter_context(nc.sbuf_tensor(n, [P, BLK], F32R))[:, :].rearrange("p (q c) -> p q c", q=4)
                      for n in ("w_hi", "w_lo"))
        x_hi, x_lo = (ctx.enter_context(nc.sbuf_tensor(n, [P, 2 * D], F32R))[:, :].rearrange("p (b k s) -> p b k s", b=2, k=KT)
                      for n in ("x_hi", "x_lo"))
        last_part = sb("last_part", 30400 - 16064 - 2 * BLK - 2 * 2 * D)

        def area(at, cols):
            assert at + cols <= 30400
            return arena[:, at:at + cols]

        ident = cst[:, CST["ident"]]
        ones = cst[:, CST["ones"]]
        ones64 = cst[:, CST["ones64"]]
        flip, flip64 = cst[:, CST["flip"]], cst[:, CST["flip64"]]

        def as_f32(rounded):
            return rounded.bitcast(F32)

        mod_rows = area(0, 12288)

        fnT = area(0, 1024).rearrange("p (f t) -> p f t", f=2)
        qkT = area(1024, 6144).rearrange("p (m t) -> p m t", m=12)
        bias_na = area(7168, 6144).rearrange("p (q h k) -> p q h k", q=2, h=NA_H)
        Vt = area(16384, 3072).rearrange("p (t c) -> p t c", t=4)
        ca = area(19456, CA_N)
        acs = area(21632, 1024).rearrange("p (b t c) -> p b t c", b=2, t=2)
        probs0 = area(22656, 1024).rearrange("p (b k) -> p b k", b=2)
        probsT0 = area(23680, 1024).rearrange("p (b k q) -> p b k q", b=2, k=4)
        stat = area(24704, 8 * 48 + 8)

        acc = area(0, 4096).rearrange("p (k t) -> p k t", k=KT)
        Gt = area(4096, 8192).rearrange("p (e t) -> p e t", e=EXPERTS)
        silu_b = area(12288, 1024).rearrange("p (b t) -> p b t", b=2)
        gated = area(13312, 1024).rearrange("p (b t) -> p b t", b=2)
        hid = area(16384, 2048).rearrange("p (m t) -> p m t", m=4)
        sel = area(18432, 2048).rearrange("p (e m) -> p e m", e=EXPERTS)
        gateT = area(20480, 512)
        xtok = area(0, 4096).rearrange("p (t c) -> p t c", t=4)
        slots = area(4096, 4096).bitcast(BF16).rearrange("p (t e s) -> p t e s", t=4, e=EXPERTS)
        xg = area(8192, 2048).rearrange("p (b c) -> p b c", b=2)
        es = area(10240, 1024).rearrange("p (b f) -> p b f", b=2)
        eh = area(11264, 1024).rearrange("p (b f) -> p b f", b=2)
        ey = area(12288, 2048).rearrange("p (b c) -> p b c", b=2)
        ehT = area(28352, 1024).rearrange("p (b k s) -> p b k s", b=2, k=4)
        cg = area(0, 8192).rearrange("p (w t c) -> p w t c", w=2, t=4)
        rt = area(14336, 1024)
        rt2 = area(15360, 512)

        qR = area(0, 2048).rearrange("p (h ab t) -> p h ab t", h=4, ab=2)
        kR = area(2048, 4096).rearrange("p (h ab t) -> p h ab t", h=4, ab=2)
        vR = area(6144, 8192).rearrange("p (t c) -> p t c", t=4)
        gR = area(14336, 4096).rearrange("p (m t) -> p m t", m=16)
        cb = area(18432, CB_N)
        decayT = area(21504, 2048).rearrange("p (b k t) -> p b k t", b=2, k=4)
        scoreT = area(23552, 2048).rearrange("p (b k t) -> p b k t", b=2, k=4)
        oR = area(25600, 1024).rearrange("p (m t) -> p m t", m=4)
        sqR = area(26624, 1024).rearrange("p (m t) -> p m t", m=4)
        rope_t = area(27648, 2048).rearrange("p (b h t) -> p b h t", b=2, h=4)
        irR = area(29696, SEQ)
        dec_t = area(29952, 128)

        z1 = area(0, 12288).rearrange("p (s h t) -> p s h t", s=6, h=8)
        z1m = area(0, 12288).rearrange("p (m t) -> p m t", m=48)
        zf = z1[:, 0:2]
        q_b, g_b, zgA, zgB = z1[:, 2], z1[:, 3], z1[:, 4], z1[:, 5]
        ib = area(12288, 2048).rearrange("p (t c) -> p t c", t=2)
        lf = area(14336, 4096).rearrange("p (d h t) -> p d h t", d=2, h=8)
        bc = area(18432, 4096).rearrange("p (d h t) -> p d h t", d=2, h=8)
        cc = area(22528, CC_N)
        pt_b = area(24064, 1024).rearrange("p (b j i) -> p b j i", b=2, j=2)
        o_b = area(25088, 512).rearrange("p (b t) -> p b t", b=2)
        sq_b = area(25600, 512).rearrange("p (b t) -> p b t", b=2)
        ir_b = area(26112, 512).rearrange("p (b t) -> p b t", b=2)
        decs = area(26624, 128).rearrange("p (d h c) -> p d h c", d=2, h=8)
        lbt = area(26752, 128)
        toep = area(26880, 512)
        mrg = area(27392, 256)
        z2 = area(14336, 7168).rearrange("p (m t) -> p m t", m=28)
        v2 = area(21504, 3072).rearrange("p (g t c) -> p g t c", g=3, t=2)
        bias2 = area(24576, 3072).rearrange("p (b q g k) -> p b q g k", b=2, q=2, g=3)
        probs2 = area(27648, 1536).rearrange("p (b k) -> p b k", b=2)
        sq2 = area(29184, 1024).rearrange("p (b t) -> p b t", b=2)
        probsT2 = area(0, 768).rearrange("p (k q) -> p k q", k=6)
        ir2 = area(768, 1024).rearrange("p (b t) -> p b t", b=2)
        stat2 = area(1792, 64)

        slot_tok = ctx.enter_context(nc.sbuf_tensor("slot_tok", [P, EXPERTS], I32))
        tok_row = ctx.enter_context(nc.sbuf_tensor("tok_row", [P, 8], I32))
        fullest = ctx.enter_context(nc.sbuf_tensor("fullest", [P, 1], I32))
        tok_bf = ctx.enter_context(nc.sbuf_tensor("tok_bf", [P, 8], BF16))

        ld_cst, ld_sm, ld_h, ld_rpb, ld_ca, ld_cb, ld_cc = map(sem, (
            "ld_cst", "ld_sm", "ld_h", "ld_rpb", "ld_ca", "ld_cb", "ld_cc"))
        ld_sel = [sem(f"ld_sel{i}") for i in range(2)]
        ld_bias2 = [sem(f"ld_bias2{j}") for j in range(2)]
        w_full = [sem(f"w_full{j}") for j in range(SLOTS)]
        w_free = [sem(f"w_free{j}") for j in range(SLOTS)]
        c2_ready, mod_ready, tick_ready = sem("c2_ready"), sem("mod_ready"), sem("tick_ready")
        nm_sq, nm_ms, nm_std, nm_tmp, nm_x = map(sem, ("nm_sq", "nm_ms", "nm_std", "nm_tmp", "nm_x"))
        res_done = sem("res_done")
        dve_step, act_step = sem("dve_step"), sem("act_step")
        mx_mm, mx_ev = sem("mx_mm"), sem("mx_ev")
        fn_mm, fn_ev = sem("fn_mm"), sem("fn_ev")
        bias_ready = sem("bias_ready")
        na_s, na_neg, na_e, na_p, na_t, na_c, na_o, na_ev = map(sem, (
            "na_s", "na_neg", "na_e", "na_p", "na_t", "na_c", "na_o", "na_ev"))
        mo_mm, mo_ev = sem("mo_mm"), sem("mo_ev")
        rt_mm, rt_sig, gate_ready, gT_mm, gT_ev, gb_mm, gb_ev = map(sem, (
            "rt_mm", "rt_sig", "gate_ready", "gT_mm", "gT_ev", "gb_mm", "gb_ev"))
        up1, up3, silu_rdy, gated_rdy, hid_rdy, dn_mm, dn_free = map(sem, (
            "up1", "up3", "silu_rdy", "gated_rdy", "hid_rdy", "dn_mm", "dn_free"))
        xt_mm, xt_ev, x_st, sel_rdy, pos_mm, full_rdy, slots_rdy, ix_mm, ix_rdy = map(sem, (
            "xt_mm", "xt_ev", "x_st", "sel_rdy", "pos_mm", "full_rdy", "slots_rdy", "ix_mm", "ix_rdy"))
        f_x, f_xa, f_xd, f_u1, f_u3, f_s, f_h, f_ht, f_he, f_d, f_ya, f_yd, f_cmb, f_cT = map(sem, (
            "f_x", "f_xa", "f_xd", "f_u1", "f_u3", "f_s", "f_h", "f_ht", "f_he", "f_d", "f_ya", "f_yd", "f_cmb", "f_cT"))
        f_c = sem("f_c")
        hi_rdy, lo_rdy, split_used, mr_mm, mr_ev, mt_mm = map(sem, (
            "hi_rdy", "lo_rdy", "split_used", "mr_mm", "mr_ev", "mt_mm"))
        xg_ld, y_st = ([[sem(f"{n}{i}{j}") for j in range(2)] for i in range(2)] for n in ("xg_ld", "y_st"))
        c_ld = [sem(f"c_ld{i}") for i in range(2)]
        rp_mm, rp_ev, rope_done, lg_ready, dk_arg, dk_exp, dk_rdy, rs_mm, rs_rdy, ro_mm, ro_ev, rn_mm, rn_std, rn_rdy = \
            map(sem, ("rp_mm", "rp_ev", "rope_done", "lg_ready", "dk_arg", "dk_exp", "dk_rdy", "rs_mm", "rs_rdy",
                      "ro_mm", "ro_ev", "rn_mm", "rn_std", "rn_rdy"))
        y_mm, y_ev = sem("y_mm"), sem("y_ev")
        z1_mm, z1_ev, ib_mm, ib_ev = map(sem, ("z1_mm", "z1_ev", "ib_mm", "ib_ev"))
        f_rdy, lf_rdy, b_rdy, e_rdy = map(sem, ("f_rdy", "lf_rdy", "b_rdy", "e_rdy"))
        K_rdy, K_used, pt_rdy, ho_mm, ho_ev, hn_mm, hn_std, hg_done = map(sem, (
            "K_rdy", "K_used", "pt_rdy", "ho_mm", "ho_ev", "hn_mm", "hn_std", "hg_done"))
        lb_e, lb_s, tz_mm, tz_rdy, tz_st = map(sem, ("lb_e", "lb_s", "tz_mm", "tz_rdy", "tz_st"))
        z2_mm, z2_ev, v2_mm, v2_ev = map(sem, ("z2_mm", "z2_ev", "v2_mm", "v2_ev"))
        qn_sq, qn_mm, qn_std, qn_done = map(sem, ("qn_sq", "qn_mm", "qn_std", "qn_done"))
        at_s, at_neg, at_e, at_p, at_t, at_c, at_o, at_ev = map(sem, (
            "at_s", "at_neg", "at_e", "at_p", "at_t", "at_c", "at_o", "at_ev"))
        ya_mm, ya_ev, yb_mm, yb_ev, yo_mm, yo_ev, out_done = map(sem, (
            "ya_mm", "ya_ev", "yb_mm", "yb_ev", "yo_mm", "yo_ev", "out_done"))

        def slot(n, pattern=None, **kw):
            s = ring[:, (n % SLOTS) * BLK:(n % SLOTS + 1) * BLK]
            return s.rearrange(pattern, **kw) if pattern else s

        MOE_ORDER = {1: (1, 0, 2), 2: (0, 2, 1)}
        NORM_COLS = [(0, T), (0, T), (0, T), (SEQ, T), (SEQ, T), (SEQ, T)]
        NA_UNITS = [(seg, h, q) for seg in (1, 0) for h in range(NA_H) for q in range(2)]
        AT_UNITS = [(h, q) for h in range(AT_H) for q in range(2)]

        def na_q(seg, q):
            return slice(seg * SEQ + q * P, seg * SEQ + (q + 1) * P)

        def half(h):
            return slice(HD * (h % 2), HD * (h % 2) + HD)

        def by_load(eng, layer, routed, dense):
            eng.wait_ge(full_rdy, layer + 1)
            load = eng.value_load(fullest[0:1, 0:1], min_val=0, max_val=T)
            with eng.If(load < P + 1):
                routed(layer)
            with eng.Else():
                dense(layer)

        def split_signal(n, q):
            return (lo_rdy if q < 3 else w_free[n % SLOTS]), 1

        block = ctx.enter_context(nc.Block())

        @block.sync
        def _(sp):
            sp.dma_start(sm[:, :], smalls).then_inc(ld_sm, 16)
            for j in range(SLOTS):
                sp.dma_start(slot(j), w_all[j]).then_inc(w_full[j], 16)
                if j == 0:
                    sp.dma_start(cst[:, :], cst_d).then_inc(ld_cst, 16)
                    sp.dma_start(hT, h0).then_inc(ld_h, 16)

            def turns(first, last, order):
                with sp.Fori(first, last) as i:
                    for j in order:
                        sp.wait_ge(w_free[j], i)
                        sp.dma_start(slot(j), w_all[i * SLOTS + j]).then_inc(w_full[j], 16)

            moe0, moe1 = B_MOE0 // SLOTS + 1, B_MOE1 // SLOTS + 1
            in_order = (0, 1, 2)
            turns(1, moe0, in_order)
            turns(moe0, moe0 + EXPERTS - 1, MOE_ORDER[B_MOE0 % SLOTS])
            turns(moe0 + EXPERTS - 1, moe1, in_order)
            turns(moe1, moe1 + EXPERTS - 1, MOE_ORDER[B_MOE1 % SLOTS])
            turns(moe1 + EXPERTS - 1, N_BLK // SLOTS, in_order)
            for n in range(N_BLK - (N_BLK - SLOTS) % SLOTS, N_BLK):
                sp.wait_ge(w_free[n % SLOTS], n // SLOTS)
                sp.dma_start(slot(n), w_all[n]).then_inc(w_full[n % SLOTS], 16)
            sp.wait_ge(yo_ev, KT)
            sp.dma_start(out_d, XT[:, :, LAT]).then_inc(out_done, 16)
            sp.wait_ge(out_done, 16)

        @block.gpsimd
        def _(pool):
            def gather(layer):
                nt = 4 if layer == 0 else 2
                pool.wait_ge(ix_rdy, layer + 1)
                pool.wait_ge(x_st, 64 if layer == 0 else 96)
                for e in range(EXPERTS):
                    if e >= 2:
                        pool.wait_ge(f_x, EXPERTS * layer + e - 1)
                    pool.indirect_dma_start(xg[:, e % 2], None, xtok_d, bass.IndirectOffsetOnAxis(
                        ap=slot_tok[:, e:e + 1].bitcast(U32), axis=0)).then_inc(xg_ld[layer][e % 2], 16)
                for j in range(2):
                    pool.wait_ge(y_st[layer][j], 128)
                for t in range(nt):
                    for w in range(2):
                        pool.indirect_dma_start(cg[:, w, t], None, y_d, bass.IndirectOffsetOnAxis(
                            ap=tok_row[:, 4 * w + t:4 * w + t + 1].bitcast(U32), axis=0)).then_inc(c_ld[layer], 16)

            def ungather(layer):
                pool.dma_start(sel[0:EXPERTS], sel_d).then_inc(ld_sel[layer], 16)

            pool.wait_ge(mod_ready, 2)
            pool.dma_start(ca, ca_d).then_inc(ld_ca, 16)
            for layer in range(2):
                pool.wait_ge(res_done, 2 * layer + 1)
                by_load(pool, layer, gather, ungather)
                pool.wait_ge(res_done, 2 * layer + 2)
                if layer == 0:
                    pool.dma_start(cb, cb_d).then_inc(ld_cb, 16)
            pool.dma_start(cc, cc_d).then_inc(ld_cc, 16)
            pool.wait_ge(tz_rdy, 1)
            pool.dma_start(toep_d, toep[0:24, :]).then_inc(tz_st, 16)
            pool.wait_ge(tz_st, 16)
            pool.wait_ge(hg_done, HG)
            for h in range(AT_H):
                if h >= 2:
                    pool.wait_ge(at_s, 2 * (h - 1))
                for q in range(2):
                    pool.dma_start(bias2[:, h % 2, q], bass.AP(
                        tensor=toep_d.tensor, offset=h * 512 + P - P * q,
                        ap=[[1, P], [AT_H * 512, AT_G], [1, SEQ]])).then_inc(ld_bias2[h % 2], 16)

        @block.tensor
        def _(pe):
            def arrive(n):
                pe.wait_ge(w_full[n % SLOTS], 16 * (n // SLOTS + 1))

            def chain(out, pairs):
                for i, (a, b) in enumerate(pairs):
                    last = nc.tensor.matmul(out, a, b, start=(i == 0), stop=(i == len(pairs) - 1))
                return last

            def release(n):
                nc.tensor.matmul(ps[0:32, 7, 0:2], tick[:, 0:32], tick[:, 0:2], start=True, stop=True).then_inc(
                    w_free[n % SLOTS], 1)

            def used():
                nc.tensor.matmul(ps[0:32, 7, 0:2], tick[:, 0:32], tick[:, 0:2], start=True, stop=True).then_inc(split_used, 1)

            def warm(bank, n):
                some = cst[:, 0:256].bitcast(BF16)
                for _ in range(n):
                    nc.tensor.matmul(ps[:, bank, :], some[:, 0:P], some, start=True, stop=True)

            def norm(i):
                a, b = NORM_COLS[i]
                for k in range(KT):
                    pe.wait_ge(nm_sq, KT * i + k + 1)
                    last = nc.tensor.matmul(ps[:, 7, 0:b - a], ones, XT[:, k, a:b], start=(k == 0), stop=(k == KT - 1))
                last.then_inc(nm_ms, 1)

            def router(layer):
                tts = range(4) if layer == 0 else range(2)
                t0 = 0 if layer == 0 else SEQ
                w = sm[:, SM["router_w"]].rearrange("p (k e) -> p k e", k=KT)
                for tt in tts:
                    last = chain(ps[:, 0, tt * 16:tt * 16 + 16],
                                 [(XT[:, k, t0 + tt * P:t0 + (tt + 1) * P], w[:, k]) for k in range(KT)])
                last.then_inc(rt_mm, 1)
                for tt in tts:
                    if tt >= 2:
                        pe.wait_ge(xt_ev, 4 * layer + tt - 1)
                    for k in range(KT):
                        last = nc.tensor.transpose(ps[:, 1 + 2 * (tt % 2) + k // 4, (k % 4) * P:(k % 4 + 1) * P],
                                                   XT[:, k, t0 + tt * P:t0 + (tt + 1) * P], ident)
                    last.then_inc(xt_mm, 1)
                pe.wait_ge(sel_rdy, layer + 1)
                chosen = lambda tt: rt[:, 704 + tt * 16:720 + tt * 16]
                for tt in tts:
                    chain(ps[:, 5, tt * 16:tt * 16 + 16],
                          [(ones, chosen(j)) for j in range(tt)] + [(cst[:, CST["tri"]], chosen(tt))])
                chain(ps[:, 5, 64:80], [(ones, chosen(j)) for j in tts]).then_inc(pos_mm, 1)

            def spread_gates(layer):
                tts = range(4) if layer == 0 else range(2)
                pe.wait_ge(gate_ready, layer + 1)
                pe.wait_ge(xt_ev, 4 * layer + len(tts))
                for tt in tts:
                    last = nc.tensor.matmul(ps[0:16, 1, tt * P:(tt + 1) * P], rt[:, tt * 16:tt * 16 + 16], ident,
                                            start=True, stop=True)
                last.then_inc(gT_mm, 1)
                pe.wait_ge(gT_ev, layer + 1)
                pe.wait_ge(ld_sel[layer], 16)
                n = len(tts) * P
                for e in range(EXPERTS):
                    if e >= 4:
                        pe.wait_ge(gb_ev, EXPERTS * layer + e - 3)
                    nc.tensor.matmul(ps[:, 2 + e % 4, 0:n], sel[0:EXPERTS, e], gateT[0:EXPERTS, 0:n],
                                     start=True, stop=True).then_inc(gb_mm, 1)
                pe.wait_ge(gb_ev, EXPERTS * (layer + 1))

            def routed(layer):
                for s_, n in ((up1, 64), (up3, 64), (hid_rdy, 2), (dn_free, 2), (dn_mm, 128), (gT_mm, 1), (gb_mm, 16)):
                    pe.sem_inc(s_, n)
                nt = 4 if layer == 0 else 2
                c = EXPERTS * layer
                base = B_MOE0 if layer == 0 else B_MOE1
                pe.wait_ge(slots_rdy, layer + 1)
                for e in range(EXPERTS):
                    last = chain(ps[:, 6, 2 * e:2 * e + 2],
                                 [(slots[:, t, e], tok_bf[:, 2 * t:2 * t + 2]) for t in range(nt)])
                last.then_inc(ix_mm, 1)
                q0 = 96 + 8 * c

                def quarter(e, j, n, q, to, ks, cols, first, final, done=None):
                    b = base + n
                    if q < 3:
                        pe.wait_ge(lo_rdy, e * 6 + (72 + 6 * c + 3 * n + q + 1))
                    else:
                        pe.wait_ge(w_free[b % SLOTS], e + (b // SLOTS + 1))
                    for i, k in enumerate(ks):
                        for m, (x, w) in enumerate(((x_hi, w_hi), (x_lo, w_hi), (x_hi, w_lo))):
                            last = nc.tensor.matmul(to, x[:, j, k], w[:, q, i * cols:(i + 1) * cols],
                                                    start=(first and i == 0 and m == 0), stop=(final and i == len(ks) - 1 and m == 2))
                    if done is None:
                        last.then_inc(split_used, 1)
                    else:
                        last.then_inc(done, 1)
                        used()

                def turn_rows(e, j, half_e, first):
                    pe.wait_ge(xg_ld[layer][j], half_e * 16 + 16)
                    if not first:
                        pe.wait_ge(f_xa, e + c)
                        pe.wait_ge(f_xd, e + c)
                    for k in range(KT):
                        last = nc.tensor.transpose(ps[:, k // 4, (k % 4) * P:(k % 4 + 1) * P],
                                                   xg[:, j, k * P:(k + 1) * P], ident)
                    last.then_inc(f_x, 1)

                def turn_hidden(j, c2):
                    for k in (2 * c2, 2 * c2 + 1):
                        last = nc.tensor.transpose(ps[:, 4, k * P:(k + 1) * P], eh[:, j, k * P:(k + 1) * P], ident)
                    last.then_inc(f_ht, 1)

                def turn(e, j, first, last_e, half_e):
                    some = not (first and j == 0)
                    pe.wait_ge(f_xa, e + (c + 1))
                    pe.wait_ge(f_xd, e + (c + 1))
                    if some:
                        pe.wait_ge(f_s, e + c)
                    for q in range(4):
                        quarter(e, j, 0, q, ps[:, 2, :], (2 * q, 2 * q + 1), 512, q == 0, q == 3, f_u1 if q == 3 else None)
                    if some:
                        pe.wait_ge(f_h, e * 2 + 2 * c)
                    for q in range(4):
                        half, ks = q // 2, range(4 * (q % 2), 4 * (q % 2) + 4)
                        quarter(e, j, 1, q, ps[:, (1, 3)[half], 0:256], ks, 256, q % 2 == 0, q % 2 == 1,
                                f_u3 if q % 2 else None)
                        if q == 2:
                            pe.wait_ge(f_h, e * 2 + (2 * c + 1))
                            if some:
                                pe.wait_ge(f_he, e * 2 + 2 * c)
                            turn_hidden(j, 0)
                    if not last_e:
                        turn_rows(e + 1, 1 - j, half_e + j, False)
                    pe.wait_ge(f_h, e * 2 + (2 * c + 2))
                    pe.wait_ge(f_he, e * 2 + (2 * c + 1))
                    turn_hidden(j, 1)
                    b = base + 2
                    pe.wait_ge(w_full[b % SLOTS], e * 16 + 16 * (b // SLOTS + 1))
                    w2 = slot(b, "p (k m) -> p k m", k=4)
                    if some:
                        pe.wait_ge(f_ya, e + c)
                        pe.wait_ge(f_yd, e + c)
                    for c2 in range(2):
                        if c2:
                            pe.wait_ge(f_he, e * 2 + (2 * c + 2))
                        for n in range(2):
                            for k in (2 * c2, 2 * c2 + 1):
                                last = nc.tensor.matmul(ps[:, 5 + n, :], ehT[:, j, k], w2[:, k, n * 512:(n + 1) * 512],
                                                        start=(k == 0), stop=(k == 3))
                            if c2:
                                last.then_inc(f_d, 1)
                    release(b)

                turn_rows(0, 0, 0, layer == 0)
                for j in range(2):
                    turn(j, j, True, False, 0)
                with pe.Fori(1, EXPERTS // 2 - 1) as i:
                    for j in range(2):
                        turn(i * 2 + j, j, False, False, i)
                for j in range(2):
                    turn(EXPERTS - 2 + j, j, False, j == 1, EXPERTS // 2 - 1)
                for m in range(KT):
                    if m >= 2:
                        pe.wait_ge(f_cT, KT * layer + m - 1)
                    for t in range(nt):
                        if m == 0:
                            pe.wait_ge(f_cmb, 4 * layer + t + 1)
                        last = nc.tensor.transpose(ps[:, m % 2, t * P:(t + 1) * P], cg[:, 0, t, m * P:(m + 1) * P], ident)
                    last.then_inc(f_c, 1)

            def dense(layer):
                for s_, n in ((f_x, 16), (f_u1, 16), (f_u3, 32), (f_ht, 32), (f_d, 32), (ix_mm, 1), (f_c, 8),
                              (split_used, 128)):
                    pe.sem_inc(s_, n)
                spread_gates(layer)
                experts(layer)

            def experts(layer):
                base = B_MOE0 if layer == 0 else B_MOE1
                t0, n = (0, T) if layer == 0 else (SEQ, SEQ)
                pe.sem_inc(hid_rdy, 2)
                pe.sem_inc(dn_free, 2)
                u0, d0 = (4 * EXPERTS + 2) * layer, (8 * EXPERTS + 2) * layer
                w = [slot(base + j) for j in range(3)]
                w1 = w[0].rearrange("p (k m) -> p k m", k=KT)
                w1 = [w1[:, :, m * P:(m + 1) * P] for m in range(4)]
                w3 = w[1].rearrange("p (c k m) -> p c k m", c=2, k=KT)
                w3 = [w3[:, m // 2, :, m % 2 * P:(m % 2 + 1) * P] for m in range(4)]
                w2 = w[2].rearrange("p (k m) -> p k m", k=4)

                def arrive_e(e, n):
                    pe.wait_ge(w_full[n % SLOTS], e * 16 + 16 * (n // SLOTS + 1))

                with pe.Fori(0, EXPERTS) as e:
                    for m in range(4):
                        pe.wait_ge(hid_rdy, e * 4 + (u0 + m + 1))
                        for j, wj, done in ((0, w1, up1), (1, w3, up3)):
                            if m == 0:
                                arrive_e(e, base + j)
                            chain(ps[:, 2 * (m % 2) + j, 0:n],
                                  [(wj[m][:, k], XT[:, k, t0:t0 + n]) for k in range(KT)]).then_inc(done, 1)
                            if m == 3:
                                release(base + j)
                    arrive_e(e, base + 2)
                    pe.wait_ge(hid_rdy, e * 4 + (u0 + 6))
                    for m in range(8):
                        pe.wait_ge(dn_free, e * 8 + (d0 + m + 1))
                        chain(ps[:, 4 + m % 2, 0:n],
                              [(w2[:, k, m * P:(m + 1) * P], hid[:, k, 0:n]) for k in range(4)]).then_inc(dn_mm, 1)
                    release(base + 2)

            pe.wait_ge(ld_sm, 16)
            pe.wait_ge(c2_ready, 3)
            pe.wait_ge(tick_ready, 1)
            pe.sem_inc(split_used, 4)
            pe.sem_inc(mr_ev, 3)
            with pe.Fori(0, 8) as i:
                for j in range(3):
                    pe.wait_ge(mr_ev, i * 3 + (j + 1))
                    for q in range(4):
                        if q < 3:
                            pe.wait_ge(lo_rdy, i * 9 + (3 * j + q + 1))
                        else:
                            pe.wait_ge(w_free[j], i + 1)
                        for k in range(2):
                            for part in (w_hi, w_lo):
                                last = nc.tensor.matmul(ps[:, j, :], x_hi[:, 0, 2 * q + k],
                                                        part[:, q, 512 * k:512 * k + 512],
                                                        start=(q == 0 and k == 0 and part is w_hi),
                                                        stop=(q == 3 and k == 1 and part is w_lo))
                        if q < 3:
                            last.then_inc(split_used, 1)
                        else:
                            last.then_inc(mr_mm, 1)
                            used()
            pe.wait_ge(ld_cst, 16)
            pe.wait_ge(mr_ev, 24 + 3)
            for m in range(96):
                last = nc.tensor.transpose(ps[:, 3, 4 * m:4 * m + 4], mod_rows[0:4, m * P:(m + 1) * P], ident[0:4, 0:4])
            last.then_inc(mt_mm, 1)

            norm(0)
            pe.wait_ge(nm_x, KT)
            pe.wait_ge(mod_ready, 2)
            unit = 0
            for b in range(5):
                arrive(B_MIX + b)
                w = slot(B_MIX + b, "p (k m) -> p k m", k=KT)
                for m in range((4, 4, 4, 2, 0)[b]):
                    if unit >= 4:
                        pe.wait_ge(mx_ev, unit - 3)
                    chain(ps[:, unit % 4, :],
                          [(w[:, k, m * P:(m + 1) * P], XT[:, k, :]) for k in range(KT)]).then_inc(mx_mm, 1)
                    unit += 1
                if b >= 3:
                    cols = slice(256, 512) if b == 3 else slice(0, 512)
                    for tt in range(4):
                        pe.wait_ge(mx_ev, unit - 3)
                        chain(ps[:, unit % 4, 0:cols.stop - cols.start],
                              [(XT[:, k, tt * P:(tt + 1) * P], w[:, k, cols]) for k in range(KT)]).then_inc(mx_mm, 1)
                        unit += 1
                release(B_MIX + b)
            pe.wait_ge(mx_ev, unit)

            pe.wait_ge(ld_ca, 16)
            cosN = ca[:, CA["cos"]].rearrange("p (t n) -> p t n", t=2)
            msinN = ca[:, CA["msin"]].rearrange("p (t n) -> p t n", t=2)
            for n, (seg, f) in enumerate((s, f) for s in range(2) for f in range(2)):
                if n:
                    pe.wait_ge(fn_ev, 2 * n - 1)
                for tt in range(2):
                    last = nc.tensor.matmul(ps[:, 4, tt * 256:(tt + 1) * 256], fnT[:, f, na_q(seg, tt)],
                                            ca[:, CA["dft64"]], start=True, stop=True)
                last.then_inc(fn_mm, 1)
                pe.wait_ge(fn_ev, 2 * n + 1)
                chain(ps[:, 5, 0:SEQ], [(acs[:, 0, tt, c * P:(c + 1) * P], (cosN, msinN)[c][:, tt])
                                        for tt in range(2) for c in range(2)]).then_inc(fn_mm, 1)
            pe.wait_ge(fn_ev, 8)

            pe.wait_ge(bias_ready, 1)
            for i in range(len(NA_UNITS) + 2):
                if i < len(NA_UNITS):
                    seg, h, q = NA_UNITS[i]
                    nk = T if seg else SEQ
                    if i >= 3:
                        pe.wait_ge(na_e, i - 2)
                    last = nc.tensor.matmul(ps[:, i % 3, 0:nk], qkT[half(h), h // 2, na_q(seg, q)],
                                            qkT[half(h), 6 + h // 2, 0:nk], start=True, stop=not seg)
                    if seg:
                        last = nc.tensor.matmul(ps[:, i % 3, LAT], flip64, bias_na[:, q, h], start=False, stop=True)
                    last.then_inc(na_s, 1)
                if 0 <= i - 1 < len(NA_UNITS):
                    u = i - 1
                    warm(7, 2)
                    pe.wait_ge(na_p, u + 1)
                    if u >= 2:
                        pe.wait_ge(na_c, u - 1)
                    for kt in range(4 if NA_UNITS[u][0] else 2):
                        last = nc.tensor.transpose(ps[:, 3 + u % 2, kt * P:(kt + 1) * P],
                                                   probs0[:, u % 2, kt * P:(kt + 1) * P], ident)
                    last.then_inc(na_t, 1)
                if i >= 2:
                    u = i - 2
                    seg, h, q = NA_UNITS[u]
                    pe.wait_ge(na_c, u + 1)
                    if u >= 2:
                        pe.wait_ge(na_ev, u - 1)
                    chain(ps[half(h), 5 + u % 2, 0:P],
                          [(Vt[:, kt, h * HD:(h + 1) * HD], probsT0[:, u % 2, kt])
                           for kt in range(4 if seg else 2)]).then_inc(na_o, 1)
            pe.wait_ge(na_ev, len(NA_UNITS))
            for b in range(2):
                arrive(B_MIXO + b)
                w = slot(B_MIXO + b, "p (k m) -> p k m", k=KT)
                for m in range(4):
                    u = 4 * b + m
                    if u >= 4:
                        pe.wait_ge(mo_ev, u - 3)
                    chain(ps[:, u % 4, :], [(w[:, k, m * P:(m + 1) * P], XT[:, k]) for k in range(KT)]).then_inc(mo_mm, 1)
                release(B_MIXO + b)

            norm(1)
            pe.wait_ge(nm_x, 2 * KT)
            router(0)
            by_load(pe, 0, routed, dense)

            norm(2)
            pe.wait_ge(nm_x, 3 * KT)
            unit = 0
            for b in range(12):
                arrive(B_RET + b)
                w = slot(B_RET + b, "p (k m) -> p k m", k=KT)
                for m in range(4):
                    if unit >= 4:
                        pe.wait_ge(rp_ev, unit - 3)
                    if 4 <= b < 8:
                        pairs = [(XT[:, k, m * P:(m + 1) * P], w[:, k]) for k in range(KT)]
                    else:
                        pairs = [(w[:, k, m * P:(m + 1) * P], XT[:, k, (0 if 2 <= b < 4 else SEQ):T]) for k in range(KT)]
                    chain(ps[:, unit % 4, 0:(T if 2 <= b < 8 else SEQ)], pairs).then_inc(rp_mm, 1)
                    unit += 1
                release(B_RET + b)
            pe.wait_ge(rp_ev, unit)
            pe.wait_ge(rope_done, 2)

            def ret_scores(h):
                if h:
                    pe.wait_ge(rs_rdy, 2 * h)
                for kt in range(4):
                    last = chain(ps[:, kt // 2, (kt % 2) * SEQ:(kt % 2 + 1) * SEQ],
                                 [(kR[:, h, ab, kt * P:(kt + 1) * P], qR[:, h, ab]) for ab in range(2)])
                last.then_inc(rs_mm, 1)

            ret_scores(0)
            for h in range(RET_H):
                pe.wait_ge(rs_rdy, 2 * h + 2)
                if h:
                    pe.wait_ge(ro_ev, h)
                for dv in range(4):
                    last = chain(ps[:, 2 + dv // 2, (dv % 2) * SEQ:(dv % 2 + 1) * SEQ],
                                 [(vR[:, kt, h * 512 + dv * P:h * 512 + (dv + 1) * P], scoreT[:, h % 2, kt])
                                  for kt in range(4)])
                last.then_inc(ro_mm, 1)
                if h + 1 < RET_H:
                    ret_scores(h + 1)
                warm(7, 4)
                pe.wait_ge(ro_ev, h + 1)
                chain(ps[:, 4, 0:SEQ], [(ones, sqR[:, m]) for m in range(4)]).then_inc(rn_mm, 1)
            pe.wait_ge(rn_rdy, RET_H)
            for b in range(4):
                arrive(B_RETO + b)
                w = slot(B_RETO + b, "p (k m) -> p k m", k=16)
                for m in range(2):
                    u = 2 * b + m
                    if u >= 4:
                        pe.wait_ge(y_ev, u - 3)
                    chain(ps[:, u % 4, 0:SEQ], [(w[:, k, m * P:(m + 1) * P], gR[:, k]) for k in range(16)]).then_inc(y_mm, 1)
                release(B_RETO + b)

            norm(3)
            pe.wait_ge(nm_x, 4 * KT)
            router(1)
            by_load(pe, 1, routed, dense)

            norm(4)
            norm(5)
            pe.wait_ge(nm_tmp, 6 * KT)
            pe.sem_inc(z1_ev, 6)
            with pe.Fori(0, 4) as i:
                for j in range(3):
                    n = B_Z1 + j
                    pe.wait_ge(w_full[n % SLOTS], i * 16 + 16 * (n // SLOTS + 1))
                    w = slot(n, "p (k m) -> p k m", k=KT)
                    for hf in range(2):
                        pe.wait_ge(z1_ev, i * 6 + (2 * j + hf + 1))
                        for m in range(2):
                            last = chain(ps[:, 2 * j + hf, m * SEQ:(m + 1) * SEQ],
                                         [(w[:, k, (2 * hf + m) * P:(2 * hf + m + 1) * P], XT[:, k, LAT]) for k in range(KT)])
                        last.then_inc(z1_mm, 1)
                    release(n)
            pe.wait_ge(z1_ev, 30)
            for b in range(2):
                arrive(B_IB + b)
                w = slot(B_IB + b, "p (k m) -> p k m", k=KT)
                for tt in range(2):
                    chain(ps[:, 2 * b + tt, :],
                          [(XT[:, k, SEQ + tt * P:SEQ + (tt + 1) * P], w[:, k]) for k in range(KT)]).then_inc(ib_mm, 1)
                release(B_IB + b)
            pe.wait_ge(ld_cc, 16)
            nc.tensor.matmul(ps[0:24, 6, 0:511], sm[0:BUCKETS, SM["rel_bias"]], cc[0:BUCKETS, CC["onehot"]],
                             start=True, stop=True).then_inc(tz_mm, 1)
            pe.wait_ge(ib_ev, 4)

            def gla_scores(h):
                if h >= 2:
                    pe.wait_ge(pt_rdy, h - 1)
                for d in range(2):
                    pe.wait_ge(K_rdy, 2 * h + d + 1)
                    near, far = (0, 1) if d == 0 else (1, 0)
                    bank = 2 * (h % 2) + d
                    for c in range(NCH):
                        Kc = zf[:, d, c]
                        qc = lf[:, d, h, c * CH:(c + 1) * CH]
                        last = nc.tensor.matmul(ps[:, bank, c * CH:(c + 1) * CH], Kc[:, near * P:(near + 1) * P], qc,
                                                start=True, stop=True)
                        if c // 4 == far:
                            at = SEQ + (c % 4) * CH
                            last = nc.tensor.matmul(ps[:, bank, at:at + CH], Kc[:, far * P:(far + 1) * P], qc,
                                                    start=True, stop=True)
                    last.then_inc(K_used, 1)

            pe.wait_ge(tz_rdy, 1)
            gla_scores(0)
            for h in range(HG):
                if h + 1 < HG:
                    gla_scores(h + 1)
                pe.wait_ge(pt_rdy, h + 1)
                if h >= 2:
                    pe.wait_ge(ho_ev, h - 1)
                chain(ps[:, 4 + h % 2, 0:SEQ],
                      [(ib[:, j, h * P:(h + 1) * P], pt_b[:, h % 2, j]) for j in range(2)]).then_inc(ho_mm, 1)
                pe.wait_ge(ho_ev, h + 1)
                if h:
                    pe.wait_ge(hn_std, h)
                nc.tensor.matmul(ps[:, 6, 0:SEQ], ones, sq_b[:, h % 2], start=True, stop=True).then_inc(hn_mm, 1)
            pe.wait_ge(hg_done, HG)

            for b in range(10):
                arrive(B_Z2 + b)
                w = slot(B_Z2 + b, "p (k m) -> p k m", k=KT)
                for hf in range(2):
                    u = 2 * b + hf
                    if u >= 6:
                        pe.wait_ge(z2_ev, u - 5)
                    if b < 7:
                        for m in range(2):
                            last = chain(ps[:, u % 6, m * SEQ:(m + 1) * SEQ],
                                         [(w[:, k, (2 * hf + m) * P:(2 * hf + m + 1) * P], XT[:, k, LAT]) for k in range(KT)])
                    else:
                        last = chain(ps[:, u % 6, :],
                                     [(XT[:, k, SEQ + hf * P:SEQ + (hf + 1) * P], w[:, k]) for k in range(KT)])
                    last.then_inc(z2_mm, 1)
                release(B_Z2 + b)
            for u in range(12):
                pe.wait_ge(qn_sq, u + 1)
                if u >= 2:
                    pe.wait_ge(qn_std, u - 1)
                nc.tensor.matmul(ps[:, 6 + u % 2, :], ones64, sq2[:, u % 2], start=True, stop=True).then_inc(qn_mm, 1)
            pe.wait_ge(qn_done, 12)
            pe.wait_ge(z2_ev, 20)

            for i in range(len(AT_UNITS) + 2):
                if i < len(AT_UNITS):
                    h, q = AT_UNITS[i]
                    if i >= 2:
                        pe.wait_ge(at_e, i - 1)
                    for g in range(AT_G):
                        last = nc.tensor.matmul(ps[:, 2 * (i % 2) + g // 2, (g % 2) * SEQ:(g % 2 + 1) * SEQ],
                                                z2[half(h), 4 + 8 * g + h // 2, q * P:(q + 1) * P],
                                                z2[half(h), 8 + 8 * g + h // 2, :], start=(g != 1), stop=False,
                                                skip_group_check=True)
                    pe.wait_ge(ld_bias2[h % 2], 32 * (h // 2 + 1))
                    for g in range(0, AT_G, 2):
                        last = nc.tensor.matmul(ps[:, 2 * (i % 2) + g // 2, 0:(2 * SEQ if g == 0 else SEQ)], flip,
                                                bias2[:, h % 2, q, g:min(g + 2, AT_G)], start=False, stop=True,
                                                skip_group_check=True)
                    last.then_inc(at_s, 1)
                if 0 <= i - 1 < len(AT_UNITS):
                    u = i - 1
                    if u:
                        pe.wait_ge(at_c, u)
                    warm(4, 3)
                    pe.wait_ge(at_p, u + 1)
                    for kt in range(6):
                        last = nc.tensor.transpose(ps[:, 4 + kt // 4, (kt % 4) * P:(kt % 4 + 1) * P],
                                                   probs2[:, u % 2, kt * P:(kt + 1) * P], ident)
                    last.then_inc(at_t, 1)
                if i >= 2:
                    u = i - 2
                    h, q = AT_UNITS[u]
                    pe.wait_ge(at_c, u + 1)
                    if u >= 2:
                        pe.wait_ge(at_ev, u - 1)
                    chain(ps[half(h), 6 + u % 2, 0:P],
                          [(v2[:, kt // 2, kt % 2, h * HD:(h + 1) * HD], probsT2[:, kt]) for kt in range(6)]).then_inc(at_o, 1)
            pe.wait_ge(at_ev, len(AT_UNITS))

            arrive(B_PA)
            w = slot(B_PA, "p (k m) -> p k m", k=4)
            for m in range(8):
                if m >= 4:
                    pe.wait_ge(ya_ev, m - 3)
                chain(ps[:, m % 4, 0:SEQ], [(w[:, k, m * P:(m + 1) * P], z2[:, k]) for k in range(4)]).then_inc(ya_mm, 1)
            release(B_PA)
            for m in range(8):
                if m % 4 == 0:
                    arrive(B_PB + m // 4)
                    w = slot(B_PB + m // 4, "p (k m) -> p k m", k=KT)
                if m >= 2:
                    pe.wait_ge(yb_ev, m - 1)
                chain(ps[:, 4 + m % 2, 0:SEQ],
                      [(w[:, k, (m % 4) * P:(m % 4 + 1) * P], g_b[:, k]) for k in range(KT)]).then_inc(yb_mm, 1)
                if m % 4 == 3:
                    release(B_PB + m // 4)
            pe.wait_ge(yb_ev, KT)
            for m in range(8):
                if m % 4 == 0:
                    arrive(B_WO + m // 4)
                    w = slot(B_WO + m // 4, "p (k m) -> p k m", k=KT)
                if m >= 4:
                    pe.wait_ge(yo_ev, m - 3)
                chain(ps[:, m % 4, 0:SEQ],
                      [(w[:, k, (m % 4) * P:(m % 4 + 1) * P], zgA[:, k]) for k in range(KT)]).then_inc(yo_mm, 1)

        @block.scalar
        def _(act):
            def norm_in(i):
                a, b = NORM_COLS[i]
                if i == 0:
                    act.wait_ge(ld_h, 16)
                elif i < 5:
                    act.wait_ge(res_done, i)
                else:
                    act.wait_ge(nm_tmp, 5 * KT)
                for k in range(KT):
                    nc.scalar.activation(XT[:, k, a:b], hT[:, k, a:b], ACT.Square).then_inc(nm_sq, 1)
                act.wait_ge(nm_ms, i + 1)
                nc.scalar.activation(inv_rms[:, 0:b - a], ps[:, 7, 0:b - a], ACT.Sqrt, bias=eps_col, scale=1.0 / D).then_inc(nm_std, 1)

            def norm_out(i):
                a, b = NORM_COLS[i]
                act.wait_ge(mod_ready, i // 2 + 1)
                for k in range(KT):
                    act.wait_ge(nm_tmp, KT * i + k + 1)
                    for seg in range(a // SEQ, 2):
                        part = XT[:, k, seg * SEQ:(seg + 1) * SEQ]
                        last = nc.scalar.activation(part, part, ACT.Identity, scale=gains[:, i, k, seg:seg + 1],
                                                    bias=modc[:, i // 2, 24 * (i % 2) + k, seg:seg + 1])
                    last.then_inc(nm_x, 1)

            def router(layer):
                nt = 4 if layer == 0 else 2
                act.wait_ge(rt_mm, layer + 1)
                nc.scalar.activation(rt[:, 64:64 + 16 * nt], ps[:, 0, 0:16 * nt], ACT.Sigmoid).then_inc(rt_sig, 1)
                for tt in range(nt):
                    act.wait_ge(xt_mm, 4 * layer + tt + 1)
                    nc.scalar.activation(xtok[:, tt], ps[:, 1 + 2 * (tt % 2):3 + 2 * (tt % 2), :].rearrange("p b c -> p (b c)"),
                                         ACT.Copy).then_inc(xt_ev, 1)
                    act.wait_ge(xt_ev, 4 * layer + tt + 1)
                    act.dma_start(xtok_d[tt * P:(tt + 1) * P], xtok[:, tt]).then_inc(x_st, 16)

            def routed(layer):
                for s_, n in ((silu_rdy, 64), (gT_ev, 1), (gb_ev, 16)):
                    act.sem_inc(s_, n)
                c = EXPERTS * layer

                q0 = 96 + 8 * c
                base = B_MOE0 if layer == 0 else B_MOE1

                def copy_rows(e, j):
                    act.wait_ge(f_x, e + (c + 1))
                    nc.scalar.activation(x_hi[:, j], ps[:, 0:2, :].rearrange("p b (k s) -> p (b k) s", k=4), ACT.Copy).then_inc(f_xa, 1)

                def split(e, n, qs):
                    b = base + n
                    for q in qs:
                        if q == 0:
                            act.wait_ge(w_full[b % SLOTS], e * 16 + 16 * (b // SLOTS + 1))
                        act.wait_ge(split_used, e * 8 + (q0 + 4 * n + q + 1))
                        nc.scalar.activation(w_hi[:, q], slot(b, "p (q c) -> p q c", q=4)[:, q], ACT.Copy).then_inc(hi_rdy, 1)

                def turn(e, j, first, last_e, half_e):
                    split(e, 1, range(4))
                    act.wait_ge(f_u1, e + (c + 1))
                    nc.scalar.activation(es[:, j], ps[:, 2, :], ACT.Silu).then_inc(f_s, 1)
                    if not last_e:
                        split(e + 1, 0, (0, 1))
                        copy_rows(e + 1, 1 - j)
                        split(e + 1, 0, (2, 3))
                    act.wait_ge(f_d, e * 2 + (2 * c + 1))
                    if not first:
                        act.wait_ge(y_st[layer][j], half_e * 16)
                    nc.scalar.activation(ey[:, j, 0:512], ps[:, 5, :], ACT.Copy).then_inc(f_ya, 1)
                    act.wait_ge(f_ya, e + (c + 1))
                    act.wait_ge(f_yd, e + (c + 1))
                    act.dma_start(y_d[bass.ds(e * P, P)], ey[:, j]).then_inc(y_st[layer][j], 16)

                split(0, 0, range(4))
                copy_rows(0, 0)
                for j in range(2):
                    turn(j, j, True, False, 0)
                with act.Fori(1, EXPERTS // 2 - 1) as i:
                    for j in range(2):
                        turn(i * 2 + j, j, False, False, i)
                for j in range(2):
                    turn(EXPERTS - 2 + j, j, False, j == 1, EXPERTS // 2 - 1)

            def dense(layer):
                for s_, n in ((f_xa, 16), (f_s, 16), (f_ya, 16), (hi_rdy, 128)):
                    act.sem_inc(s_, n)
                nt = 4 if layer == 0 else 2
                act.wait_ge(gT_mm, layer + 1)
                nc.scalar.activation(gateT[0:EXPERTS, 0:nt * P], ps[0:EXPERTS, 1, 0:nt * P], ACT.Copy).then_inc(gT_ev, 1)
                for e in range(EXPERTS):
                    act.wait_ge(gb_mm, EXPERTS * layer + e + 1)
                    nc.scalar.activation(Gt[:, e, 0:nt * P], ps[:, 2 + e % 4, 0:nt * P], ACT.Copy).then_inc(gb_ev, 1)
                experts(layer)

            def experts(layer):
                n = T if layer == 0 else SEQ
                with act.Fori(0, EXPERTS) as e:
                    for m in range(4):
                        act.wait_ge(up1, e * 4 + (4 * EXPERTS * layer + m + 1))
                        nc.scalar.activation(silu_b[:, m % 2, 0:n], ps[:, 2 * (m % 2), 0:n], ACT.Silu).then_inc(silu_rdy, 1)

            act.wait_ge(ld_sm, 16)
            nc.scalar.activation(c2s[:, :], sm[:, SM["c2"]], ACT.Silu).then_inc(c2_ready, 1)
            act.wait_ge(c2_ready, 1)
            act.wait_ge(tick_ready, 1)
            nc.scalar.activation(x_hi[:, 0, :, 0:2], c2s[:, :].rearrange("p (k s) -> p k s", s=2), ACT.Copy).then_inc(c2_ready, 1)

            def rows_out(i, j):
                act.wait_ge(mr_mm, i * 3 + (j + 1))
                nc.scalar.activation(mod_rows[0:4, bass.ds(i * 1536 + 512 * j, 512)], ps[0:4, j, :], ACT.Copy).then_inc(mr_ev, 1)

            def ada_turn(i, first):
                for j in range(3):
                    act.wait_ge(w_full[j], i * 16 + 16)
                    for q in range(4):
                        act.wait_ge(split_used, i * 12 + (4 * j + q + 1))
                        nc.scalar.activation(w_hi[:, q], slot(j, "p (q c) -> p q c", q=4)[:, q], ACT.Copy).then_inc(hi_rdy, 1)
                    if j:
                        rows_out(i, j - 1)
                    elif not first:
                        rows_out(i - 1, 2)

            ada_turn(0, True)
            with act.Fori(1, 8) as i:
                ada_turn(i, False)
            rows_out(7, 2)
            act.wait_ge(mt_mm, 1)
            for r in range(ROWS):
                for kr in range(ROWS):
                    act.dma_start(bias_na[(r % 2) * GRID_W:(r % 2 + 1) * GRID_W, r // 2, :, kr * GRID_W:(kr + 1) * GRID_W],
                                  bass.AP(tensor=rpb.tensor,
                                          offset=(kr - r + NA_KH - 1) * RPB_W + NA_KW - GRID_W,
                                          ap=[[1, GRID_W], [RPB_HEAD, NA_H], [1, GRID_W]])).then_inc(ld_rpb, 16)
            norm_in(0)
            norm_out(0)
            for u in range(22):
                act.wait_ge(mx_mm, u + 1)
                if u < 2:
                    dst = fnT[:, u, :]
                elif u < 14:
                    dst = qkT[:, u - 2, :]
                elif u < 18:
                    dst = Vt[:, u - 14, 0:256]
                else:
                    dst = Vt[:, u - 18, 256:768]
                nc.scalar.activation(dst, ps[:, u % 4, 0:(256 if 14 <= u < 18 else 512)], ACT.Copy).then_inc(mx_ev, 1)
            for n, (seg, f) in enumerate((s, f) for s in range(2) for f in range(2)):
                act.wait_ge(fn_mm, 2 * n + 1)
                nc.scalar.activation(acs[:, 0], ps[:, 4, :].rearrange("p (t c) -> p t c", t=2), ACT.Copy).then_inc(fn_ev, 1)
                act.wait_ge(fn_mm, 2 * n + 2)
                nc.scalar.activation(XT[:, f, seg * SEQ:(seg + 1) * SEQ], ps[:, 5, 0:SEQ], ACT.Copy).then_inc(fn_ev, 1)
            for i in range(len(NA_UNITS) + 2):
                if i < len(NA_UNITS):
                    nk = T if NA_UNITS[i][0] else SEQ
                    act.wait_ge(na_neg, i + 1)
                    if i >= 2:
                        act.wait_ge(na_t, i - 1)
                    nc.scalar.activation(probs0[:, i % 2, 0:nk], ps[:, i % 3, 0:nk], ACT.Exp, scale=0.125,
                                         bias=stat[:, 4 * i + 1:4 * i + 2], accum_out=stat[:, 4 * i + 2:4 * i + 3]).then_inc(na_e, 1)
                if 0 <= i - 1 < len(NA_UNITS):
                    u = i - 1
                    nk = T if NA_UNITS[u][0] else SEQ
                    act.wait_ge(na_t, u + 1)
                    if u >= 2:
                        act.wait_ge(na_o, u - 1)
                    nc.scalar.activation(probsT0[:, u % 2, 0:nk // P],
                                         ps[:, 3 + u % 2, 0:nk].rearrange("p (k q) -> p k q", q=P), ACT.Copy).then_inc(na_c, 1)
                if i >= 2:
                    u = i - 2
                    seg, h, q = NA_UNITS[u]
                    act.wait_ge(na_o, u + 1)
                    nc.scalar.activation(XT[half(h), 2 + h // 2, na_q(seg, q)], ps[half(h), 5 + u % 2, 0:P],
                                         ACT.Copy).then_inc(na_ev, 1)
            norm_in(1)
            norm_out(1)
            router(0)
            by_load(act, 0, routed, dense)

            norm_in(2)
            norm_out(2)
            nc.scalar.activation(dec_t[:, 0:8], sm[:, SM["decay"]], ACT.Exp).then_inc(lg_ready, 1)
            act.wait_ge(lg_ready, 2)
            nc.scalar.activation(dec_t[:, 16:24], dec_t[:, 8:16], ACT.Ln).then_inc(lg_ready, 1)
            for u in range(48):
                act.wait_ge(rp_mm, u + 1)
                b, m = u // 4, u % 4
                if b < 2:
                    dst, n = qR.rearrange("p h ab t -> p (h ab) t")[:, u], SEQ
                elif b < 4:
                    dst, n = kR.rearrange("p h ab t -> p (h ab) t")[:, u - 8], T
                elif b < 8:
                    dst, n = vR[:, m, (b - 4) * 512:(b - 3) * 512], T
                else:
                    dst, n = gR[:, u - 32], SEQ
                nc.scalar.activation(dst, ps[:, u % 4, 0:n], ACT.Silu if b >= 8 else ACT.Copy).then_inc(rp_ev, 1)

            def decays(h):
                act.wait_ge(dk_arg, h + 1)
                act.wait_ge(ld_cb, 16)
                lat = decayT[:, h % 2, 2:4].rearrange("p k t -> p (k t)")
                nc.scalar.activation(lat, lat, ACT.Exp)
                nc.scalar.activation(decayT[:, h % 2, 0:2].rearrange("p k t -> p (k t)"), cb[:, CB["ctx_f"]], ACT.Exp,
                                     scale=dec_t[:, 48 + h:49 + h])
                nc.scalar.activation(rope_t[:, h % 2, 0:2].rearrange("p k t -> p (k t)"), cb[:, CB["ctx_b"]], ACT.Exp,
                                     scale=dec_t[:, 52 + h:53 + h]).then_inc(dk_exp, 1)

            decays(0)
            for h in range(RET_H):
                if h + 1 < RET_H:
                    decays(h + 1)
                act.wait_ge(ro_mm, h + 1)
                if h:
                    act.wait_ge(rn_rdy, h)
                o = ps[:, 2:4, :].rearrange("p b (m t) -> p (b m) t", m=2)
                nc.scalar.activation(oR, o, ACT.Copy)
                nc.scalar.activation(sqR, o, ACT.Square).then_inc(ro_ev, 1)
                act.wait_ge(rn_mm, h + 1)
                nc.scalar.activation(irR, ps[:, 4, 0:SEQ], ACT.Sqrt, bias=eps_col, scale=1.0 / 512).then_inc(rn_std, 1)
            norm_in(3)
            norm_out(3)
            router(1)
            by_load(act, 1, routed, dense)

            norm_in(4)
            norm_in(5)
            act.wait_ge(lb_s, 1)
            nc.scalar.activation(lbt[:, 48:80], lbt[:, 16:48], ACT.Exp).then_inc(lb_e, 1)
            funcs = (ACT.Sigmoid, ACT.Sigmoid, ACT.Copy, ACT.Silu, ACT.Sigmoid, ACT.Sigmoid)
            for u in range(24):
                act.wait_ge(z1_mm, u + 1)
                nc.scalar.activation(z1m[:, 2 * u:2 * u + 2], ps[:, u % 6, :].rearrange("p (m t) -> p m t", m=2),
                                     funcs[u // 4]).then_inc(z1_ev, 1)
            for u in range(4):
                act.wait_ge(ib_mm, u + 1)
                nc.scalar.activation(ib[:, u % 2, (u // 2) * 512:(u // 2 + 1) * 512], ps[:, u, :], ACT.Copy).then_inc(ib_ev, 1)
            for d in range(2):
                act.wait_ge(f_rdy, d + 1)
                nc.scalar.activation(lf[:, d], zf[:, d], ACT.Ln).then_inc(lf_rdy, 1)
            for d in range(2):
                act.wait_ge(b_rdy, d + 1)
                nc.scalar.activation(lf[:, d], bc[:, d], ACT.Exp)
                nc.scalar.activation(bc[:, d], bc[:, d], ACT.Exp, scale=-1.0).then_inc(e_rdy, 1)
            for h in range(HG):
                act.wait_ge(ho_mm, h + 1)
                if h >= 2:
                    act.wait_ge(hg_done, h - 1)
                nc.scalar.activation(o_b[:, h % 2], ps[:, 4 + h % 2, 0:SEQ], ACT.Copy)
                nc.scalar.activation(sq_b[:, h % 2], ps[:, 4 + h % 2, 0:SEQ], ACT.Square).then_inc(ho_ev, 1)
                act.wait_ge(hn_mm, h + 1)
                nc.scalar.activation(ir_b[:, h % 2], ps[:, 6, 0:SEQ], ACT.Sqrt, bias=eps_col, scale=1.0 / P).then_inc(hn_std, 1)
            act.wait_ge(hg_done, HG)
            for u in range(20):
                act.wait_ge(z2_mm, u + 1)
                src = ps[:, u % 6, :]
                if u < 14:
                    nc.scalar.activation(z2[:, 2 * u:2 * u + 2], src.rearrange("p (m t) -> p m t", m=2),
                                         ACT.Silu if u < 2 else ACT.Copy).then_inc(z2_ev, 1)
                else:
                    nc.scalar.activation(v2[:, (u - 14) // 2, u % 2], src, ACT.Copy).then_inc(z2_ev, 1)
            for u in range(13):
                if u < 12:
                    if u >= 2:
                        act.wait_ge(qn_mm, u - 1)
                    nc.scalar.activation(sq2[:, u % 2].rearrange("p (m t) -> p m t", m=2), z2[:, 4 + 2 * u:6 + 2 * u],
                                         ACT.Square).then_inc(qn_sq, 1)
                if u:
                    act.wait_ge(qn_mm, u)
                    if u >= 3:
                        act.wait_ge(qn_done, u - 2)
                    nc.scalar.activation(ir2[:, (u - 1) % 2], ps[:, 6 + (u - 1) % 2, :], ACT.Sqrt, bias=eps_col,
                                         scale=1.0 / HD).then_inc(qn_std, 1)
            for i in range(len(AT_UNITS) + 1):
                if i < len(AT_UNITS):
                    act.wait_ge(at_neg, i + 1)
                    if i >= 2:
                        act.wait_ge(at_t, i - 1)
                    src = ps[:, 2 * (i % 2):2 * (i % 2) + 2, :].rearrange("p b k -> p (b k)")[:, 0:768]
                    nc.scalar.activation(probs2[:, i % 2], src, ACT.Exp, scale=0.125, bias=stat2[:, 4 * (i % 16) + 1:4 * (i % 16) + 2],
                                         accum_out=stat2[:, 4 * (i % 16) + 2:4 * (i % 16) + 3]).then_inc(at_e, 1)
                if i:
                    u = i - 1
                    act.wait_ge(at_t, u + 1)
                    if u:
                        act.wait_ge(at_o, u)
                    src = ps[:, 4:6, :].rearrange("p b k -> p (b k)")[:, 0:768].rearrange("p (k q) -> p k q", q=P)
                    nc.scalar.activation(probsT2, src, ACT.Copy).then_inc(at_c, 1)

        @block.vector
        def _(dve):
            steps = [0]

            def link(ins):
                steps[0] += 1
                ins.then_inc(dve_step, 1)
                dve.wait_ge(dve_step, steps[0])

            def norm(i):
                a, b = NORM_COLS[i]
                r = inv_rms[:, 0:b - a]
                dve.wait_ge(nm_std, i + 1)
                link(nc.vector.reciprocal(r, r))
                for k in range(KT):
                    if i < 4:
                        nc.vector.tensor_tensor(XT[:, k, a:b], hT[:, k, a:b], r, ALU.mult).then_inc(nm_tmp, 1)
                    else:
                        g = sm[:, SM["final_g" if i == 4 else "norm_w2"]][:, k:k + 1]
                        nc.vector.scalar_tensor_tensor((hT if i == 4 else XT)[:, k, a:b], hT[:, k, a:b], g, r,
                                                       ALU.mult, ALU.mult).then_inc(nm_tmp, 1)

            def rank(src, out, q):
                bj = src.unsqueeze(2).broadcast_to([P, q, 4, 4])
                bi = src.unsqueeze(3).broadcast_to([P, q, 4, 4])
                gt = rt[:, 192:192 + 16 * q].rearrange("p (q i j) -> p q i j", q=q, i=4)
                eq = rt[:, 448:448 + 16 * q].rearrange("p (q i j) -> p q i j", q=q, i=4)
                tie = cst[:, CST["tie"]].unsqueeze(1).broadcast_to([P, q, 16])
                nc.vector.tensor_tensor(gt, bj, bi, ALU.is_gt)
                link(nc.vector.tensor_tensor(eq, bj, bi, ALU.is_equal))
                eqf = rt[:, 448:448 + 16 * q].rearrange("p (q x) -> p q x", q=q)
                link(nc.vector.tensor_tensor(eqf, eqf, tie, ALU.mult))
                link(nc.vector.tensor_tensor(eqf, eqf, rt[:, 192:192 + 16 * q].rearrange("p (q x) -> p q x", q=q), ALU.add))
                link(nc.vector.tensor_reduce(out, eq, AX.X, ALU.add))

            def router(layer):
                nt = 4 if layer == 0 else 2
                q = 4 * nt
                scores = rt[:, 64:64 + 16 * nt]
                biased = rt[:, 128:128 + 16 * nt]
                rk = rt[:, 704:704 + 4 * q]
                gs, grk, den = rt[:, 768:768 + q], rt[:, 800:800 + q], rt[:, 832:832 + nt]
                val = rt[:, 896:896 + 4 * q]
                v3 = lambda x: x.rearrange("p (q j) -> p q j", j=4)
                dve.wait_ge(rt_sig, layer + 1)
                link(nc.vector.tensor_tensor(biased.rearrange("p (t e) -> p t e", t=nt), scores.rearrange("p (t e) -> p t e", t=nt),
                                             sm[:, SM["router_b"]].unsqueeze(1).broadcast_to([P, nt, 16]), ALU.add))
                rank(v3(biased), v3(rk), q)
                link(nc.vector.tensor_scalar(rk, rk, 1.5, None, ALU.is_lt))
                link(nc.vector.tensor_tensor(val, rk, biased, ALU.mult))
                link(nc.vector.tensor_reduce(gs, v3(val), AX.X, ALU.add))
                rank(v3(gs), v3(grk), nt)
                link(nc.vector.tensor_scalar(grk, grk, 0.5, None, ALU.is_lt))
                nc.vector.tensor_tensor(v3(rk), v3(rk), grk.unsqueeze(2).broadcast_to([P, q, 4]), ALU.mult).then_inc(sel_rdy, 1)
                dve.wait_ge(sel_rdy, layer + 1)
                link(nc.vector.tensor_tensor(val, rk, scores, ALU.mult))
                link(nc.vector.tensor_reduce(den, val.rearrange("p (t e) -> p t e", t=nt), AX.X, ALU.add))
                link(nc.vector.reciprocal(den, den))
                nc.vector.tensor_tensor(rt[:, 0:16 * nt].rearrange("p (t e) -> p t e", t=nt), val.rearrange("p (t e) -> p t e", t=nt),
                                        den.unsqueeze(2).broadcast_to([P, nt, 16]), ALU.mult).then_inc(gate_ready, 1)
                dve.wait_ge(pos_mm, layer + 1)
                link(nc.vector.tensor_reduce(rt2[:, 448:449], ps[:, 5, 64:80], AX.X, ALU.max))
                nc.vector.tensor_copy(fullest[:, :], rt2[:, 448:449]).then_inc(full_rdy, 1)

            def routed(layer):
                steps.append(steps[0])
                for s_, n in ((gated_rdy, 64), (hid_rdy, 64), (dn_free, 128)):
                    dve.sem_inc(s_, n)
                nt = 4 if layer == 0 else 2
                c = EXPERTS * layer
                te = lambda x: x.rearrange("p (t e) -> p t e", t=nt)
                n16 = 16 * nt
                chosen, gates = rt[:, 704:704 + n16], rt[:, 0:n16]
                at, val, top = rt2[:, 0:n16], rt2[:, 64:64 + n16], rt2[:, 128:128 + n16]
                tmp, tmp2 = rt2[:, 192:192 + n16], rt2[:, 256:256 + n16]
                rmax, rsum, gmax, gmin = (rt2[:, 320 + 8 * j:320 + 8 * j + nt] for j in range(4))
                link(nc.vector.scalar_tensor_tensor(at, ps[:, 5, 0:n16], 1.0, chosen, ALU.add, ALU.mult))
                link(nc.vector.tensor_scalar(at, at, -1.0, None, ALU.add))
                iota = cst[:, CST["iota"]].unsqueeze(1).broadcast_to([P, EXPERTS, P])
                for t in range(nt):
                    last = nc.vector.tensor_tensor(slots[:, t], iota, at[:, 16 * t:16 * t + 16].unsqueeze(2).broadcast_to([P, EXPERTS, P]),
                                                   ALU.is_equal)
                last.then_inc(slots_rdy, 1)
                link(nc.vector.tensor_tensor(te(tmp), te(ps[:, 5, 0:n16]), cst[:, CST["row1"]].unsqueeze(1).broadcast_to([P, nt, 16]), ALU.add))
                link(nc.vector.tensor_tensor(val, tmp, chosen, ALU.mult))
                nc.vector.tensor_reduce(rsum, te(val), AX.X, ALU.add)
                link(nc.vector.tensor_reduce(rmax, te(val), AX.X, ALU.max))
                nc.vector.tensor_scalar(tok_row[:, 0:nt], rmax, -1.0, None, ALU.add)
                link(nc.vector.tensor_tensor(te(top), te(val), rmax.unsqueeze(2).broadcast_to([P, nt, 16]), ALU.is_equal))
                link(nc.vector.tensor_tensor(rsum, rsum, rmax, ALU.subtract))
                nc.vector.tensor_scalar(tok_row[:, 4:4 + nt], rsum, -1.0, None, ALU.add)
                link(nc.vector.tensor_tensor(tmp, top, gates, ALU.mult))
                link(nc.vector.tensor_tensor(tmp2, gates, tmp, ALU.subtract))
                nc.vector.tensor_reduce(gmax, te(tmp), AX.X, ALU.add)
                link(nc.vector.tensor_reduce(gmin, te(tmp2), AX.X, ALU.add))
                dve.wait_ge(ix_mm, layer + 1)
                pair = ps[:, 6, 0:32].rearrange("p (e h) -> p e h", h=2)
                link(nc.vector.tensor_copy(rt2[:, 384:416].rearrange("p (e h) -> p e h", h=2), pair))
                pair = rt2[:, 384:416].rearrange("p (e h) -> p e h", h=2)
                nc.vector.scalar_tensor_tensor(slot_tok[:, :], pair[:, :, 1], float(P), pair[:, :, 0], ALU.mult,
                                               ALU.add).then_inc(ix_rdy, 1)

                q0 = 96 + 8 * c
                base = B_MOE0 if layer == 0 else B_MOE1

                def copy_rows(e, j):
                    dve.wait_ge(f_xa, e + (c + 1))
                    nc.vector.tensor_tensor(x_lo[:, j], ps[:, 0:2, :].rearrange("p b (k s) -> p (b k) s", k=4),
                                            as_f32(x_hi[:, j]), ALU.subtract).then_inc(f_xd, 1)

                def split(e, n, qs):
                    for q in qs:
                        dve.wait_ge(hi_rdy, e * 8 + (q0 + 4 * n + q + 1))
                        nc.vector.tensor_tensor(w_lo[:, q], slot(base + n, "p (q c) -> p q c", q=4)[:, q], as_f32(w_hi[:, q]),
                                                ALU.subtract).then_inc(*split_signal(base + n, q))

                def gate_half(e, j, c2):
                    cols = slice(c2 * 256, c2 * 256 + 256)
                    dve.wait_ge(f_u3, e * 2 + (2 * c + 1 + c2))
                    if c2 == 0:
                        dve.wait_ge(f_s, e + (c + 1))
                    nc.vector.tensor_tensor(eh[:, j, cols], es[:, j, cols], ps[:, (1, 3)[c2], 0:256], ALU.mult).then_inc(f_h, 1)
                    dve.wait_ge(f_ht, e * 2 + (2 * c + 1 + c2))
                    nc.vector.tensor_copy(ehT[:, j, 2 * c2:2 * c2 + 2], ps[:, 4, cols].rearrange("p (k s) -> p k s", k=2)).then_inc(f_he, 1)

                def turn(e, j, first, last_e, half_e):
                    split(e, 1, range(4))
                    gate_half(e, j, 0)
                    if not last_e:
                        split(e + 1, 0, (0,))
                    gate_half(e, j, 1)
                    if not last_e:
                        split(e + 1, 0, (1,))
                        copy_rows(e + 1, 1 - j)
                        split(e + 1, 0, (2, 3))
                    dve.wait_ge(f_d, e * 2 + (2 * c + 2))
                    if not first:
                        dve.wait_ge(y_st[layer][j], half_e * 16)
                    nc.vector.tensor_copy(ey[:, j, 512:1024], ps[:, 6, :]).then_inc(f_yd, 1)

                split(0, 0, range(4))
                copy_rows(0, 0)
                for j in range(2):
                    turn(j, j, True, False, 0)
                with dve.Fori(1, EXPERTS // 2 - 1) as i:
                    for j in range(2):
                        turn(i * 2 + j, j, False, False, i)
                for j in range(2):
                    turn(EXPERTS - 2 + j, j, False, j == 1, EXPERTS // 2 - 1)
                dve.wait_ge(c_ld[layer], 32 * nt)
                for t in range(nt):
                    link(nc.vector.tensor_scalar(cg[:, 0, t], cg[:, 0, t], gmax[:, t:t + 1], None, ALU.mult))
                    nc.vector.scalar_tensor_tensor(cg[:, 0, t], cg[:, 1, t], gmin[:, t:t + 1], cg[:, 0, t], ALU.mult,
                                                   ALU.add).then_inc(f_cmb, 1)
                t0 = 0 if layer == 0 else SEQ
                for m in range(KT):
                    dve.wait_ge(f_c, KT * layer + m + 1)
                    for seg in range(t0 // SEQ, 2):
                        part = hT[:, m, seg * SEQ:(seg + 1) * SEQ]
                        last = nc.vector.scalar_tensor_tensor(part, ps[:, m % 2, seg * SEQ - t0:(seg + 1) * SEQ - t0],
                                                              modc[:, layer, 40 + m, seg:seg + 1], part, ALU.mult, ALU.add)
                    last.then_inc(f_cT if m < KT - 1 else res_done, 1)
                dve.sem_inc(f_cT, 1)
                steps.append(steps[0])

            def dense(layer):
                for s_, n in ((f_xd, 16), (f_h, 32), (f_he, 32), (f_yd, 16), (f_cT, 8), (f_cmb, 4 if layer == 0 else 2),
                              (ix_rdy, 1), (slots_rdy, 1), (lo_rdy, 96)):
                    dve.sem_inc(s_, n)
                after, steps[0] = steps.pop(), steps.pop()
                experts(layer)
                dve.sem_inc(dve_step, after - steps[0])
                steps[0] = after

            def experts(layer):
                t0, n = (0, T) if layer == 0 else (SEQ, SEQ)
                u0, d0 = 4 * EXPERTS * layer, 8 * EXPERTS * layer
                dc = (8 * EXPERTS + 2) * layer + 2
                dve.wait_ge(x_st, 64 if layer == 0 else 96)
                for k in range(KT):
                    last = nc.vector.memset(acc[:, k, 0:n], 0.0)
                link(last)
                dve.wait_ge(gb_ev, EXPERTS * (layer + 1))
                with dve.Fori(0, EXPERTS) as e:
                    for m in range(4):
                        dve.wait_ge(up3, e * 4 + (u0 + m + 1))
                        nc.vector.tensor_tensor(gated[:, m % 2, 0:n], ps[:, 2 * (m % 2) + 1, 0:n],
                                                Gt[:, bass.ds(e, 1), 0:n].rearrange("p e t -> p (e t)"), ALU.mult).then_inc(gated_rdy, 1)
                        dve.wait_ge(gated_rdy, e * 4 + (u0 + m + 1))
                        dve.wait_ge(silu_rdy, e * 4 + (u0 + m + 1))
                        nc.vector.tensor_tensor(hid[:, m, 0:n], gated[:, m % 2, 0:n], silu_b[:, m % 2, 0:n],
                                                ALU.mult).then_inc(hid_rdy, 1)
                    for m in range(8):
                        dve.wait_ge(dn_mm, e * 8 + (d0 + m + 1))
                        nc.vector.tensor_tensor(acc[:, m, 0:n], acc[:, m, 0:n], ps[:, 4 + m % 2, 0:n], ALU.add).then_inc(dn_free, 1)
                dve.wait_ge(dn_free, dc + 8 * EXPERTS)
                for m in range(KT):
                    for seg in range(t0 // SEQ, 2):
                        part = hT[:, m, seg * SEQ:(seg + 1) * SEQ]
                        last = nc.vector.scalar_tensor_tensor(part, acc[:, m, seg * SEQ - t0:(seg + 1) * SEQ - t0],
                                                              modc[:, layer, 40 + m, seg:seg + 1], part, ALU.mult, ALU.add)
                last.then_inc(res_done, 1)

            nc.vector.memset(tick[:, :], 0.0)
            nc.vector.memset(as_f32(x_hi[:, 0]), 0.0)
            nc.vector.memset(eps_col, EPS).then_inc(tick_ready, 1)
            dve.wait_ge(c2_ready, 2)
            nc.vector.tensor_tensor(x_hi[:, 0, :, 2:4], c2s[:, :].rearrange("p (k s) -> p k s", s=2), as_f32(x_hi[:, 0, :, 0:2]),
                                    ALU.subtract).then_inc(c2_ready, 1)
            with dve.Fori(0, 8) as i:
                for j in range(3):
                    for q in range(4):
                        dve.wait_ge(hi_rdy, i * 12 + (4 * j + q + 1))
                        nc.vector.tensor_tensor(w_lo[:, q], slot(j, "p (q c) -> p q c", q=4)[:, q], as_f32(w_hi[:, q]),
                                                ALU.subtract).then_inc(*split_signal(j, q))
            dve.wait_ge(ld_sm, 16)
            dve.wait_ge(mt_mm, 1)
            parts = area(13312, 384).rearrange("p (m s) -> p m s", s=4)
            link(nc.vector.tensor_copy(parts, ps[:, 3, 0:384].rearrange("p (m s) -> p m s", s=4)))
            for layer in range(2):
                part = parts[:, 48 * layer:48 * (layer + 1)]
                link(nc.vector.tensor_tensor(modc[:, layer], part[:, :, 0:2], part[:, :, 2:4], ALU.add))
                link(nc.vector.tensor_tensor(modc[:, layer], modc[:, layer],
                                             sm[:, SM["ada_b"]][:, 48 * layer:48 * (layer + 1)].unsqueeze(2).broadcast_to([P, 48, 2]), ALU.add))
                for j in range(2):
                    n = 2 * layer + j
                    last = nc.vector.scalar_tensor_tensor(
                        gains[:, n], modc[:, layer, 24 * j + 8:24 * j + 16], 1.0,
                        sm[:, SM["norm_g"]][:, KT * n:KT * (n + 1)].unsqueeze(2).broadcast_to([P, KT, 2]), ALU.add, ALU.mult)
                last.then_inc(mod_ready, 1)
            dve.wait_ge(ld_cst, 16)
            nc.vector.tensor_copy(tok_bf[:, :], cst[:, CST["tok"]])
            dve.wait_ge(ld_h, 16)
            norm(0)
            dve.wait_ge(ld_ca, 16)
            dve.wait_ge(ld_rpb, 16 * ROWS * ROWS)
            for q in range(2):
                b = bias_na[:, q].rearrange("p h (r c) -> p (h r) c", c=GRID_W)
                shape = [P, NA_H * ROWS, GRID_W]
                link(nc.vector.tensor_tensor(b, b, ca[:, CA["keep8"]].unsqueeze(1).broadcast_to(shape), ALU.mult))
                last = nc.vector.tensor_tensor(b, b, ca[:, CA["shut8"]].unsqueeze(1).broadcast_to(shape), ALU.add)
            last.then_inc(bias_ready, 1)

            for i in range(len(NA_UNITS) + 1):
                if i < len(NA_UNITS):
                    seg, h, q = NA_UNITS[i]
                    s = ps[:, i % 3, 0:(T if seg else SEQ)]
                    dve.wait_ge(na_s, i + 1)
                    link(nc.vector.tensor_reduce(stat[:, 4 * i:4 * i + 1], s, AX.X, ALU.max))
                    nc.vector.tensor_scalar(stat[:, 4 * i + 1:4 * i + 2], stat[:, 4 * i:4 * i + 1], -0.125, None,
                                            ALU.mult).then_inc(na_neg, 1)
                if i:
                    u = i - 1
                    nk = T if NA_UNITS[u][0] else SEQ
                    dve.wait_ge(na_e, u + 1)
                    link(nc.vector.reciprocal(stat[:, 4 * u + 3:4 * u + 4], stat[:, 4 * u + 2:4 * u + 3]))
                    nc.vector.tensor_scalar(probs0[:, u % 2, 0:nk], probs0[:, u % 2, 0:nk], stat[:, 4 * u + 3:4 * u + 4],
                                            None, ALU.mult).then_inc(na_p, 1)
            for m in range(8):
                dve.wait_ge(mo_mm, m + 1)
                for seg in range(2):
                    part = hT[:, m, seg * SEQ:(seg + 1) * SEQ]
                    last = nc.vector.scalar_tensor_tensor(part, ps[:, m % 4, seg * SEQ:(seg + 1) * SEQ],
                                                          modc[:, 0, 16 + m, seg:seg + 1], part, ALU.mult, ALU.add)
                last.then_inc(mo_ev if m < 7 else res_done, 1)
            norm(1)
            router(0)
            by_load(dve, 0, routed, dense)

            norm(2)
            dve.wait_ge(lg_ready, 1)
            nc.vector.tensor_scalar(dec_t[:, 8:16], dec_t[:, 0:8], -1.0, 1.0, ALU.mult, ALU.add).then_inc(lg_ready, 1)
            dve.wait_ge(lg_ready, 3)
            link(nc.vector.tensor_scalar(dec_t[:, 24:32], dec_t[:, 8:16], -1.0, 1.0, ALU.mult, ALU.add))
            link(nc.vector.tensor_scalar(dec_t[:, 24:32], dec_t[:, 24:32], 1e-30, None, ALU.max))
            link(nc.vector.reciprocal(dec_t[:, 32:40], dec_t[:, 24:32]))
            link(nc.vector.tensor_tensor(dec_t[:, 40:48], dec_t[:, 32:40], dec_t[:, 0:8], ALU.mult))
            link(nc.vector.tensor_tensor(dec_t[:, 48:56], dec_t[:, 40:48], dec_t[:, 16:24], ALU.mult))
            dve.wait_ge(ld_cb, 16)
            cos = cb[:, CB["rcos"]].unsqueeze(1).broadcast_to([P, 4, SEQ])
            sin = cb[:, CB["rsin"]].unsqueeze(1).broadcast_to([P, 4, SEQ])
            for n, (x, units) in enumerate(((qR, 8), (kR[:, :, :, LAT], 16))):
                dve.wait_ge(rp_ev, units)
                x1, x2 = x[:, :, 0], x[:, :, 1]
                nc.vector.tensor_tensor(rope_t[:, 0], x2, sin, ALU.mult)
                link(nc.vector.tensor_tensor(rope_t[:, 1], x1, sin, ALU.mult))
                nc.vector.tensor_tensor(x1, x1, cos, ALU.mult)
                link(nc.vector.tensor_tensor(x2, x2, cos, ALU.mult))
                nc.vector.tensor_tensor(x1, x1, rope_t[:, 0], ALU.subtract)
                nc.vector.tensor_tensor(x2, x2, rope_t[:, 1], ALU.add).then_inc(rope_done, 1)
                dve.wait_ge(rope_done, n + 1)

            def decay_arg(h):
                lat = decayT[:, h % 2, 2:4].rearrange("p k t -> p (k t)")
                link(nc.vector.tensor_scalar(lat, cb[:, CB["lat_f"]], dec_t[:, 48 + h:49 + h], None, ALU.mult))
                nc.vector.scalar_tensor_tensor(lat, cb[:, CB["lat_b"]], dec_t[:, 52 + h:53 + h], lat, ALU.mult,
                                               ALU.add).then_inc(dk_arg, 1)

            decay_arg(0)
            for h in range(RET_H):
                if h + 1 < RET_H:
                    decay_arg(h + 1)
                dve.wait_ge(dk_exp, h + 1)
                ctxd = decayT[:, h % 2, 0:2].rearrange("p k t -> p (k t)")
                latd = decayT[:, h % 2, 2:4].rearrange("p k t -> p (k t)")
                nc.vector.tensor_tensor(ctxd, ctxd, rope_t[:, h % 2, 0:2].rearrange("p k t -> p (k t)"), ALU.add)
                link(nc.vector.tensor_tensor(latd, latd, cb[:, CB["twice"]], ALU.mult))
                dve.wait_ge(rs_mm, h + 1)
                if h >= 2:
                    dve.wait_ge(ro_mm, h - 1)
                for j in range(2):
                    nc.vector.scalar_tensor_tensor(
                        scoreT[:, h % 2, 2 * j:2 * j + 2].rearrange("p k t -> p (k t)"), ps[:, j, :], 0.0625,
                        (ctxd, latd)[j], ALU.mult, ALU.mult).then_inc(rs_rdy, 1)
                dve.wait_ge(rn_std, h + 1)
                link(nc.vector.reciprocal(irR, irR))
                g = gR[:, 4 * h:4 * h + 4]
                link(nc.vector.tensor_tensor(g, g, irR.unsqueeze(1).broadcast_to([P, 4, SEQ]), ALU.mult))
                nc.vector.tensor_tensor(g, g, oR, ALU.mult).then_inc(rn_rdy, 1)
            for m in range(8):
                dve.wait_ge(y_mm, m + 1)
                nc.vector.scalar_tensor_tensor(hT[:, m, LAT], ps[:, m % 4, 0:SEQ], modc[:, 1, 16 + m, 1:2], hT[:, m, LAT],
                                               ALU.mult, ALU.add).then_inc(y_ev if m < 7 else res_done, 1)
            norm(3)
            router(1)
            by_load(dve, 1, routed, dense)

            norm(4)
            dve.wait_ge(nm_tmp, 5 * KT)
            norm(5)
            a = sm[:, SM["lb"]].rearrange("p (d l h) -> p l d h", d=2, l=2)
            v16 = lambda at: lbt[:, at:at + 16].rearrange("p (d h) -> p d h", d=2)
            link(nc.vector.tensor_tensor(v16(0), a[:, 0], a[:, 1], ALU.max))
            nc.vector.tensor_tensor(v16(16), a[:, 0], v16(0), ALU.subtract)
            nc.vector.tensor_tensor(v16(32), a[:, 1], v16(0), ALU.subtract).then_inc(lb_s, 1)
            dve.wait_ge(lb_e, 1)
            link(nc.vector.tensor_tensor(v16(80), v16(48), v16(64), ALU.add))
            link(nc.vector.reciprocal(v16(96), v16(80)))
            link(nc.vector.tensor_tensor(v16(112), v16(48), v16(96), ALU.mult))
            link(nc.vector.tensor_scalar(tiny[:, 0:16], lbt[:, 112:128], -1.0, 1.0, ALU.mult, ALU.add))
            for d in range(2):
                dve.wait_ge(z1_ev, 6 + 4 * (d + 1))
                for h in range(HG):
                    at = 8 * d + h
                    last = nc.vector.tensor_scalar(zf[:, d, h], zf[:, d, h], tiny[:, at:at + 1], lbt[:, 112 + at:113 + at],
                                                   ALU.mult, ALU.add)
                last.then_inc(f_rdy, 1)
            dve.wait_ge(ld_cc, 16)
            link(nc.vector.memset(toep, 0.0))
            dve.wait_ge(tz_mm, 1)
            nc.vector.scalar_tensor_tensor(toep[0:24, 0:511], ps[0:24, 6, 0:511], 8.0, cc[0:24, CC["shut8"]],
                                           ALU.mult, ALU.add).then_inc(tz_rdy, 1)
            for d in range(2):
                dve.wait_ge(lf_rdy, d + 1)
                flat = zf[:, d].rearrange("p h t -> p (h t)")
                nc.vector.tensor_scalar(flat, flat, -1.0, 1.0, ALU.mult, ALU.add)
                step = 1 if d == 0 else -1
                for h in range(HG):
                    last = nc.vector.tensor_tensor_scan(bc[:, d, h, ::step], cc[:, CC["runs"]], lf[:, d, h, ::step], 0.0,
                                                        ALU.mult, ALU.add)
                last.then_inc(b_rdy, 1)
            for d in range(2):
                dve.wait_ge(e_rdy, d + 1)
                dve.wait_ge(z1_ev, 6 + 12)
                end = CH - 1 if d == 0 else 0
                link(nc.vector.tensor_copy(decs[:, d], lf[:, d].rearrange("p h (c t) -> p h c t", t=CH)[:, :, :, end]))
                nc.vector.tensor_tensor(lf[:, d], lf[:, d], q_b, ALU.mult)
                link(nc.vector.tensor_tensor(bc[:, d], bc[:, d], zf[:, d], ALU.mult))
                link(nc.vector.memset(zf[:, d], 0.0))

            def gla_keys(h):
                for d in range(2):
                    if h:
                        dve.wait_ge(K_used, 2 * (h - 1) + d + 1)
                    K = zf[:, d]
                    diag = bass.AP(tensor=arena, offset=d * 2048, ap=[[30400, P], [SEQ + CH, NCH], [1, CH]])
                    link(nc.vector.tensor_copy(diag, bc[:, d, h].rearrange("p (c t) -> p c t", t=CH)))
                    for c in range(1, NCH):
                        if d == 0:
                            to, of = K[:, c, 0:CH * c], K[:, c - 1, 0:CH * c]
                            dec = decs[:, d, h, c - 1:c]
                        else:
                            to, of = K[:, NCH - 1 - c, CH * (NCH - c):SEQ], K[:, NCH - c, CH * (NCH - c):SEQ]
                            dec = decs[:, d, h, NCH - c:NCH - c + 1]
                        ins = nc.vector.tensor_scalar(to, of, dec, None, ALU.mult)
                        if c < NCH - 1:
                            link(ins)
                        else:
                            ins.then_inc(K_rdy, 1)

            gla_keys(0)
            for h in range(HG):
                if h + 1 < HG:
                    gla_keys(h + 1)
                dve.wait_ge(K_used, 2 * h + 2)
                if h >= 2:
                    dve.wait_ge(ho_mm, h - 1)
                F, B = ps[:, 2 * (h % 2)], ps[:, 2 * (h % 2) + 1]
                pt = pt_b[:, h % 2]
                nc.vector.tensor_tensor(mrg[:, 0:P], F[:, 0:P], cc[:, CC["mask_f"]], ALU.mult)
                nc.vector.tensor_tensor(mrg[:, P:2 * P], F[:, SEQ:SEQ + P], cc[:, CC["mask_f"]], ALU.mult)
                nc.vector.tensor_tensor(pt[:, 0, 0:P], B[:, SEQ:SEQ + P], cc[:, CC["mask_b"]], ALU.mult)
                nc.vector.tensor_tensor(pt[:, 1, P:SEQ], B[:, P:SEQ], cc[:, CC["mask_b"]], ALU.mult)
                nc.vector.tensor_copy(pt[:, 0, P:SEQ], F[:, P:SEQ])
                link(nc.vector.tensor_copy(pt[:, 1, 0:P], B[:, 0:P]))
                nc.vector.tensor_tensor(pt[:, 0, 0:P], pt[:, 0, 0:P], mrg[:, 0:P], ALU.add)
                nc.vector.tensor_tensor(pt[:, 1, P:SEQ], pt[:, 1, P:SEQ], mrg[:, P:2 * P], ALU.add).then_inc(pt_rdy, 1)
                dve.wait_ge(hn_std, h + 1)
                r = ir_b[:, h % 2]
                link(nc.vector.reciprocal(r, r))
                link(nc.vector.scalar_tensor_tensor(o_b[:, h % 2], o_b[:, h % 2], sm[:, SM["hgw"]], r, ALU.mult, ALU.mult))
                nc.vector.tensor_tensor(g_b[:, h], g_b[:, h], o_b[:, h % 2], ALU.mult).then_inc(hg_done, 1)

            for u in range(12):
                dve.wait_ge(qn_std, u + 1)
                r = ir2[:, u % 2]
                link(nc.vector.reciprocal(r, r))
                w = sm[:, SM["qn" if u % 4 < 2 else "kn"]][:, u // 4:u // 4 + 1]
                z = z2[:, 4 + 2 * u:6 + 2 * u]
                nc.vector.scalar_tensor_tensor(z, z, w, r.rearrange("p (m t) -> p m t", m=2), ALU.mult, ALU.mult).then_inc(qn_done, 1)
            for i in range(len(AT_UNITS) + 2):
                if i < len(AT_UNITS):
                    h, q = AT_UNITS[i]
                    s = ps[:, 2 * (i % 2):2 * (i % 2) + 2, :].rearrange("p b k -> p (b k)")[:, 0:768]
                    dve.wait_ge(at_s, i + 1)
                    link(nc.vector.tensor_reduce(stat2[:, 4 * i:4 * i + 1], s, AX.X, ALU.max))
                    nc.vector.tensor_scalar(stat2[:, 4 * i + 1:4 * i + 2], stat2[:, 4 * i:4 * i + 1], -0.125, None,
                                            ALU.mult).then_inc(at_neg, 1)
                if 0 <= i - 1 < len(AT_UNITS):
                    u = i - 1
                    dve.wait_ge(at_e, u + 1)
                    link(nc.vector.reciprocal(stat2[:, 4 * u + 3:4 * u + 4], stat2[:, 4 * u + 2:4 * u + 3]))
                    nc.vector.tensor_scalar(probs2[:, u % 2], probs2[:, u % 2], stat2[:, 4 * u + 3:4 * u + 4], None,
                                            ALU.mult).then_inc(at_p, 1)
                if i >= 2:
                    u = i - 2
                    h, q = AT_UNITS[u]
                    dve.wait_ge(at_o, u + 1)
                    part = z2[half(h), h // 2, q * P:(q + 1) * P]
                    nc.vector.tensor_tensor(part, part, ps[half(h), 6 + u % 2, 0:P], ALU.mult).then_inc(at_ev, 1)
            for m in range(8):
                dve.wait_ge(ya_mm, m + 1)
                nc.vector.tensor_tensor(zgA[:, m], zgA[:, m], ps[:, m % 4, 0:SEQ], ALU.mult).then_inc(ya_ev, 1)
            dve.wait_ge(ya_ev, KT)
            for m in range(8):
                dve.wait_ge(yb_mm, m + 1)
                link(nc.vector.tensor_tensor(zgB[:, m], zgB[:, m], ps[:, 4 + m % 2, 0:SEQ], ALU.mult))
                nc.vector.tensor_tensor(zgA[:, m], zgA[:, m], zgB[:, m], ALU.add).then_inc(yb_ev, 1)
            for m in range(8):
                dve.wait_ge(yo_mm, m + 1)
                nc.vector.tensor_tensor(XT[:, m, LAT], hT[:, m, LAT], ps[:, m % 4, 0:SEQ], ALU.add).then_inc(yo_ev, 1)


def columns_of(v):
    return np.ascontiguousarray(v.reshape(-1, P).T)


def weight_blocks(w, rows, cols):
    k, m = w.shape
    b = w.reshape(k // rows, rows // P, P, m // cols, cols)
    return b.transpose(0, 3, 2, 1, 4).reshape(-1, P, rows // P * cols)


def kernel(**inputs):
    import concourse.bacc as bacc
    from concourse.bass_utils import run_bass_kernel_spmd as run

    a = {k: np.asarray(v) for k, v in inputs.items()}
    blocks = []
    for layer in range(2):
        blocks.append(weight_blocks(a["ada_w"][layer], D, 512))
    blocks.append(weight_blocks(a["mixab_w_in"][0], D, 512))
    blocks.append(weight_blocks(a["mixab_w_out"][0], D, 512))

    def expert_blocks(layer):
        w1 = a["moe_w1"][layer].reshape(EXPERTS, KT, P, 512).transpose(0, 2, 1, 3).reshape(EXPERTS, P, BLK)
        w3 = a["moe_w3"][layer].reshape(EXPERTS, KT, P, 2, 256).transpose(0, 2, 3, 1, 4).reshape(EXPERTS, P, BLK)
        w2 = a["moe_w2"][layer].reshape(EXPERTS, 4, P, D).transpose(0, 2, 1, 3).reshape(EXPERTS, P, BLK)
        return np.stack([w1, w3, w2], 1).reshape(3 * EXPERTS, P, BLK)

    blocks.append(expert_blocks(0))
    rw = a["ret_w_in"][0]
    qk = rw[:, :2048].reshape(D, 8, 2, 2, 64).transpose(0, 1, 3, 2, 4).reshape(D, 2048)
    blocks.append(weight_blocks(qk, D, 512))
    blocks.append(weight_blocks(rw[:, 2048:], D, 512))
    blocks.append(weight_blocks(a["ret_w_out"][0], 2048, 256))
    blocks.append(expert_blocks(1))
    w2 = weight_blocks(a["w_in_2"][0], D, 512)
    order = [12, 13, 14, 15, 10, 11, 18, 19, 20, 21, 22, 23, 16, 17, 9, 0, 1, 3, 4, 6, 7, 2, 5, 8]
    blocks.append(w2[order])
    blocks.append(weight_blocks(a["w_proj_a_2"][0], 512, D))
    blocks.append(weight_blocks(a["w_proj_b_2"][0], D, 512))
    blocks.append(weight_blocks(a["w_out_2"][0], D, 512))
    w_all = np.concatenate(blocks)

    h0 = np.concatenate([a["ctx"][0], a["x"][0]]).T.reshape(KT, P, T).transpose(1, 0, 2)
    rows = lambda v: np.broadcast_to(v.reshape(1, -1), (P, v.size))
    c2 = np.stack([columns_of(a["c_ctx"]), columns_of(a["c"][0])], -1).reshape(P, 2 * KT)
    rel = np.zeros((P, 24), a["rel_bias_2"].dtype)
    rel[:BUCKETS] = a["rel_bias_2"]
    lb = np.concatenate([columns_of(a[n][r]) for n in ("lb_fwd_2", "lb_bwd_2") for r in range(2)], 1)
    smalls = np.concatenate([
        c2, columns_of(a["ada_b"].reshape(-1)), columns_of(a["norm_g"].reshape(-1)), columns_of(a["final_norm_g"]),
        columns_of(a["norm_w_2"].reshape(-1)),
        a["router_w"].reshape(KT, P, 16).transpose(1, 0, 2).reshape(P, KT * 16), rows(a["router_b"]),
        rows(a["ret_decay"]), np.tile(a["q_norm_w_2"][0].T, (2, 1)), np.tile(a["k_norm_w_2"][0].T, (2, 1)), lb,
        a["hg_norm_w_2"].reshape(P, 1), rel], 1)
    assert w_all.shape[0] == N_BLK and smalls.shape[1] == SM_N

    arrays = {"w_all": w_all, "h0": h0, "smalls": smalls, "rpb": a["na_rpb"][0]}
    arrays.update({k + "_d": v for k, v in constants().items()})
    arrays = {k: np.ascontiguousarray(v) for k, v in arrays.items()}
    nc = bacc.Bacc("TRN2", target_bir_lowering=False, num_devices=1)
    args = {k: nc.dram_tensor(k, v.shape, F32, kind="ExternalInput").ap() for k, v in arrays.items()}
    args["toep_d"] = nc.dram_tensor("toep_d", (24, 512), F32, kind="Internal").ap()
    args["xtok_d"] = nc.dram_tensor("xtok_d", (T, D), F32, kind="Internal").ap()
    args["y_d"] = nc.dram_tensor("y_d", (EXPERTS * P, D), F32, kind="Internal").ap()
    args["out_d"] = nc.dram_tensor("out_d", (P, KT, SEQ), F32, kind="ExternalOutput").ap()
    build(nc, **args)
    r = run(nc, [arrays], core_ids=[0])
    return r.results[0]["out_d"].transpose(1, 0, 2).reshape(D, SEQ).T[None]
```
